# Optimizing a Trainium2 kernel written in Bass

```python
import jax, jax.numpy as jnp
from jax import lax
import numpy as np

D_MODEL = 2048
BATCH = 1
SEQ = 512
DEPTH = 1
DEC_BATCH = 8
DEC_SEQ = 1
PAST_LEN = 4096
PAGE_SIZE = 128

D_RWKV = D_MODEL // 2
D_NSA = D_MODEL - D_RWKV
HEAD_DIM_R = 64
H_R = D_RWKV // HEAD_DIM_R
LORA_W = 96
LORA_A = 96
LORA_G = 64
HEAD_DIM = 64
N_HEADS = D_NSA // HEAD_DIM
N_KV = 4
GQA = N_HEADS // N_KV
KV_W = N_KV * HEAD_DIM
L_CMP = 32
D_CMP = 16
L_SLC = 64
N_SELECT = 16
WINDOW = 512
PHI_HIDDEN = 64
Q_BLOCK = 128
SLC_Q_CHUNK = 64
D_FF = ((8 * D_MODEL + 3 * 256 - 1) // (3 * 256)) * 256
R_COLS = 3 * D_RWKV + LORA_W + LORA_A + LORA_G
D_IN = R_COLS + D_NSA + 6 * KV_W + 3 * N_HEADS
RMS_EPS = 1e-6
LNX_EPS = 64e-5
SCALE = HEAD_DIM ** -0.5

kernel_name = 'hymba_rwkv7_nsa_decode_step'

def rms_norm(x, g):
    xf = x.astype(jnp.float32)
    y = xf * lax.rsqrt(jnp.mean(xf * xf, axis=-1, keepdims=True) + RMS_EPS)
    return (y * g.astype(jnp.float32)).astype(x.dtype)

def masked_softmax(s, mask, axis=-1):
    s = jnp.where(mask, s.astype(jnp.float32), -jnp.inf)
    m = jnp.max(s, axis=axis, keepdims=True)
    m = jnp.where(jnp.isfinite(m), m, 0.0)
    e = jnp.where(mask, jnp.exp(s - m), 0.0)
    return e / jnp.maximum(jnp.sum(e, axis=axis, keepdims=True), 1e-30)

def token_shift(p, prev, mu):
    shifted = jnp.concatenate([prev[:, None, :].astype(p.dtype), p[:, :-1]], axis=1)
    return p + (shifted - p) * mu

def rwkv7_mix(xr, wkv0, lw):
    B, T, _ = xr.shape
    f32 = jnp.float32
    o1, o2, o3 = D_RWKV, 2 * D_RWKV, 3 * D_RWKV
    o4, o5 = o3 + LORA_W, o3 + LORA_W + LORA_A
    r, k, v = xr[..., :o1], xr[..., o1:o2], xr[..., o2:o3]
    wl, al, gl = xr[..., o3:o4], xr[..., o4:o5], xr[..., o5:]
    w_log = -jax.nn.softplus(-(lw['w0'] + jnp.tanh(wl) @ lw['w2']).astype(f32)) - 0.5
    decay = jnp.exp(-jnp.exp(w_log))
    a = jax.nn.sigmoid((lw['a0'] + al @ lw['a2']).astype(f32))
    g = jax.nn.sigmoid(gl) @ lw['g2']
    heads = lambda z: z.astype(f32).reshape(B, T, H_R, HEAD_DIM_R)
    kk = heads(k * lw['k_k'])
    kk = kk / jnp.maximum(jnp.sqrt(jnp.sum(kk * kk, axis=-1, keepdims=True)), 1e-12)
    kf = heads(k * (1.0 + (a - 1.0) * lw['k_a']))
    rf, vf, af, wf = heads(r), heads(v), heads(a), heads(decay)
    seq = lambda z: jnp.swapaxes(z, 0, 1)

    def step(S, inp):
        r_t, w_t, k_t, v_t, kk_t, a_t = inp
        sa = jnp.einsum('bhij,bhj->bhi', S, -kk_t)
        S = (S * w_t[:, :, None, :] + sa[..., None] * (kk_t * a_t)[:, :, None, :]
             + v_t[..., None] * k_t[:, :, None, :])
        return S, jnp.einsum('bhij,bhj->bhi', S, r_t)

    S_fin, ys = lax.scan(step, wkv0.astype(f32), tuple(seq(z) for z in (rf, wf, kf, vf, kk, af)))
    y = seq(ys)
    mean = jnp.mean(y, axis=-1, keepdims=True)
    var = jnp.mean(jnp.square(y - mean), axis=-1, keepdims=True)
    yn = ((y - mean) * lax.rsqrt(var + LNX_EPS)).reshape(B, T, D_RWKV) * lw['lnx_w'] + lw['lnx_b']
    bonus = jnp.sum(rf * kf * lw['r_k'].astype(f32).reshape(H_R, HEAD_DIM_R), axis=-1, keepdims=True) * vf
    out = (yn + bonus.reshape(B, T, D_RWKV)) * g
    return out.astype(xr.dtype), S_fin

def nsa_heads(rest):
    B, T = rest.shape[:2]
    q = rest[..., :D_NSA].reshape(B, T, N_KV, GQA, HEAD_DIM)
    kv = rest[..., D_NSA:D_NSA + 6 * KV_W].reshape(B, T, 3, 2, N_KV, HEAD_DIM)
    gates = jax.nn.sigmoid(rest[..., D_NSA + 6 * KV_W:].astype(jnp.float32)).reshape(B, T, 3, N_KV, GQA, 1)
    return q, kv[:, :, 0], kv[:, :, 1], kv[:, :, 2], gates

def pad_rows(z):
    pad = (-z.shape[1]) % L_SLC
    return jnp.pad(z, [(0, 0), (0, pad)] + [(0, 0)] * (z.ndim - 2))

def gather_full(pool, page_table, new_rows):
    B, S = new_rows.shape[:2]
    past = pool[page_table].reshape((B, -1) + pool.shape[2:])
    pad = (-(past.shape[1] + S)) % L_SLC
    zeros = jnp.zeros((B, pad) + new_rows.shape[2:], new_rows.dtype)
    return jnp.concatenate([past.astype(new_rows.dtype), new_rows, zeros], axis=1)

def compress(rows, lw):
    B, N = rows.shape[:2]
    R = L_CMP // D_CMP
    chunks = rows.reshape(B, N // D_CMP, D_CMP, 2, N_KV, HEAD_DIM)
    w1 = lw['phi_w1'].reshape(2, L_CMP, HEAD_DIM, PHI_HIDDEN)
    part = jnp.einsum('bcjehd,esjdf->bcsehf', chunks, w1.reshape(2, R, D_CMP, HEAD_DIM, PHI_HIDDEN))
    n_blk = N // D_CMP - R + 1
    pe_term = jnp.einsum('ejd,ejdf->ef', lw['phi_pe'], w1)[:, None, :]
    h = sum(part[:, s:s + n_blk, s] for s in range(R)) + pe_term
    return jnp.einsum('bcehf,efd->bcehd', jax.nn.silu(h), lw['phi_w2'])

def cmp_attend_select(q, kvc, q_pos, n_blocks):
    kc, vc = kvc[:, :, 0], kvc[:, :, 1]
    NC = kc.shape[1]
    s = jnp.einsum('bthgd,bchd->bthgc', q, kc).astype(jnp.float32) * SCALE
    c_end = jnp.arange(NC) * D_CMP + L_CMP - 1
    mask = (c_end[None, :] <= q_pos[:, None])[None, :, None, None, :]
    p = masked_softmax(s, mask)
    o_cmp = jnp.einsum('bthgc,bchd->bthgd', p.astype(vc.dtype), vc)
    imp = jnp.sum(p, axis=3)
    c_start = jnp.arange(NC) * D_CMP
    s_start = jnp.arange(n_blocks) * L_SLC
    overlap = ((c_start[:, None] < s_start[None, :] + L_SLC)
               & (c_start[:, None] + L_CMP > s_start[None, :])).astype(jnp.float32)
    imp_s = jnp.einsum('btkc,cs->btks', imp, overlap)
    q_blk = (q_pos // L_SLC)[:, None]
    blk = jnp.arange(n_blocks)[None, :]
    forced = ((blk == 0) | (blk == q_blk) | (blk == q_blk - 1))[None, :, None, :]
    causal = (blk <= q_blk)[None, :, None, :]
    score = jnp.where(forced, jnp.inf, jnp.where(causal, imp_s, -jnp.inf))
    top_val, top_idx = lax.top_k(score, min(N_SELECT, n_blocks))
    return o_cmp, top_idx, top_val > -jnp.inf

def slc_attend(q, q_pos, sel_idx, sel_ok, kv_blocks):
    B = q.shape[0]
    bi = jnp.arange(B)[:, None, None, None]
    hi = jnp.arange(N_KV)[None, None, :, None]
    g = kv_blocks[bi, sel_idx, :, :, hi, :]
    s = jnp.einsum('bthgd,bthnld->bthgnl', q, g[..., 0, :]).astype(jnp.float32) * SCALE
    key_pos = sel_idx[..., None] * L_SLC + jnp.arange(L_SLC)
    mask = sel_ok[..., None] & (key_pos <= q_pos[None, :, None, None, None])
    p = masked_softmax(s, mask[:, :, :, None], axis=(-2, -1))
    return jnp.einsum('bthgnl,bthnld->bthgd', p.astype(g.dtype), g[..., 1, :])

def window_prompt(q, win_kv):
    B, T = q.shape[:2]
    nb, nw = T // Q_BLOCK, WINDOW // Q_BLOCK
    padded = jnp.pad(win_kv, ((0, 0), (WINDOW, 0), (0, 0), (0, 0), (0, 0)))
    padded = padded.reshape(B, nb + nw, Q_BLOCK, 2, N_KV, HEAD_DIM)
    band = jnp.concatenate([padded[:, i:i + nb] for i in range(nw + 1)], axis=2)
    qb = q.reshape(B, nb, Q_BLOCK, N_KV, GQA, HEAD_DIM)
    qi = jnp.arange(Q_BLOCK)
    ki = jnp.arange(WINDOW + Q_BLOCK) - WINDOW
    diff = qi[:, None] - ki[None, :]

    def one_block(args):
        q_blk, kv_blk, n = args
        s = jnp.einsum('bqhgd,bkhd->bqhgk', q_blk, kv_blk[:, :, 0]).astype(jnp.float32) * SCALE
        mask = ((n * Q_BLOCK + ki)[None, :] >= 0) & (diff >= 0) & (diff < WINDOW)
        p = masked_softmax(s, mask[None, :, None, None, :])
        return jnp.einsum('bqhgk,bkhd->bqhgd', p.astype(kv_blk.dtype), kv_blk[:, :, 1])

    o = lax.map(one_block, (jnp.swapaxes(qb, 0, 1), jnp.swapaxes(band, 0, 1), jnp.arange(nb)))
    return jnp.swapaxes(o, 0, 1).reshape(q.shape)

def window_sample(q, q_pos, win_all, k_pos):
    s = jnp.einsum('bthgd,bkhd->bthgk', q, win_all[:, :, 0]).astype(jnp.float32) * SCALE
    diff = q_pos[:, None] - k_pos[None, :]
    mask = (diff >= 0) & (diff < WINDOW)
    p = masked_softmax(s, mask[None, :, None, None, :])
    return jnp.einsum('bthgk,bkhd->bthgd', p.astype(win_all.dtype), win_all[:, :, 1])

def nsa_combine(gates, o_cmp, o_slc, o_win):
    o = gates[:, :, 0] * o_cmp + gates[:, :, 1] * o_slc + gates[:, :, 2] * o_win
    B, T = o.shape[:2]
    return o.reshape(B, T, D_NSA).astype(o_cmp.dtype)

def token_mix_prompt(xn, lw):
    B, T, _ = xn.shape
    proj = xn @ lw['w_in']
    xr = token_shift(proj[..., :R_COLS], jnp.zeros((B, R_COLS), proj.dtype), lw['mu'])
    rwkv_out, wkv_fin = rwkv7_mix(xr, jnp.zeros((B, H_R, HEAD_DIM_R, HEAD_DIM_R), jnp.float32), lw)
    q, cmp_kv, slc_kv, win_kv, gates = nsa_heads(proj[..., R_COLS:])
    q_pos = jnp.arange(T)
    cmp_full, slc_full = pad_rows(cmp_kv), pad_rows(slc_kv)
    o_cmp, sel_idx, sel_ok = cmp_attend_select(q, compress(cmp_full, lw), q_pos, slc_full.shape[1] // L_SLC)
    slc_blocks = slc_full.reshape(B, -1, L_SLC, 2, N_KV, HEAD_DIM)
    c = min(SLC_Q_CHUNK, T)
    nc = T // c
    chunk = lambda z: jnp.swapaxes(z.reshape((B, nc, c) + z.shape[2:]), 0, 1)
    o_slc = lax.map(lambda a: slc_attend(a[0], a[1], a[2], a[3], slc_blocks),
                    (chunk(q), q_pos.reshape(nc, c), chunk(sel_idx), chunk(sel_ok)))
    o_slc = jnp.swapaxes(o_slc, 0, 1).reshape(q.shape)
    o_win = window_prompt(q, win_kv)
    nsa_out = nsa_combine(gates, o_cmp, o_slc, o_win)
    mix = jnp.concatenate([rwkv_out, nsa_out.astype(rwkv_out.dtype)], axis=-1) @ lw['w_o']
    new_state = (cmp_kv, slc_kv, win_kv[:, -min(WINDOW, T):], wkv_fin.astype(xn.dtype), xn[:, -1])
    return mix, new_state

def token_mix_sample(xn, cache_cmp, cache_slc, cache_win, wkv, shift, page_table, lw):
    B, S, _ = xn.shape
    proj = xn @ lw['w_in']
    prev = shift.astype(xn.dtype) @ lw['w_in'][:, :R_COLS]
    xr = token_shift(proj[..., :R_COLS], prev, lw['mu'])
    rwkv_out, wkv_fin = rwkv7_mix(xr, wkv, lw)
    q, cmp_kv, slc_kv, win_kv, gates = nsa_heads(proj[..., R_COLS:])
    past_len = page_table.shape[1] * cache_cmp.shape[1]
    q_pos = past_len + jnp.arange(S)
    cmp_full = gather_full(cache_cmp, page_table, cmp_kv)
    slc_full = gather_full(cache_slc, page_table, slc_kv)
    o_cmp, sel_idx, sel_ok = cmp_attend_select(q, compress(cmp_full, lw), q_pos, slc_full.shape[1] // L_SLC)
    o_slc = slc_attend(q, q_pos, sel_idx, sel_ok, slc_full.reshape(B, -1, L_SLC, 2, N_KV, HEAD_DIM))
    win_all = jnp.concatenate([cache_win.astype(win_kv.dtype), win_kv], axis=1)
    n_buf = cache_win.shape[1]
    k_pos = past_len - n_buf + jnp.arange(n_buf + S)
    o_win = window_sample(q, q_pos, win_all, k_pos)
    nsa_out = nsa_combine(gates, o_cmp, o_slc, o_win)
    mix = jnp.concatenate([rwkv_out, nsa_out.astype(rwkv_out.dtype)], axis=-1) @ lw['w_o']
    new_state = (cmp_kv, slc_kv, win_all[:, -min(WINDOW, n_buf + S):], wkv_fin.astype(xn.dtype), xn[:, -1])
    return mix, new_state

def channel_mix(x, lw):
    h = rms_norm(x, lw['g_ffn'])
    return x + (jax.nn.silu(h @ lw['w_gate']) * (h @ lw['w_up'])) @ lw['w_down']

def setup_inputs(seed: int = 0) -> dict:
    key = jax.random.key(seed)
    keys = jax.random.split(key, 32)
    f32 = jnp.float32
    nrm = lambda i, shape, scale: jax.random.normal(keys[i], shape, f32) * scale
    n_pages = PAST_LEN // PAGE_SIZE
    n_pool = (5 * DEC_BATCH * n_pages + 3) // 4
    n_buf = min(WINDOW, PAST_LEN)
    page_table = jax.random.permutation(keys[8], n_pool)[:DEC_BATCH * n_pages]
    page_table = page_table.reshape(DEC_BATCH, n_pages).astype(jnp.int32)
    return {
        'x_prompt': nrm(0, (BATCH, SEQ, D_MODEL), 1.0),
        'x_sample': nrm(1, (DEC_BATCH, DEC_SEQ, D_MODEL), 1.0),
        'cache_cmp_kv': nrm(2, (DEPTH, n_pool, PAGE_SIZE, 2, N_KV, HEAD_DIM), 1.0),
        'cache_slc_kv': nrm(3, (DEPTH, n_pool, PAGE_SIZE, 2, N_KV, HEAD_DIM), 1.0),
        'cache_win_kv': nrm(4, (DEPTH, DEC_BATCH, n_buf, 2, N_KV, HEAD_DIM), 1.0),
        'state_wkv': nrm(5, (DEPTH, DEC_BATCH, H_R, HEAD_DIM_R, HEAD_DIM_R), 0.5),
        'state_shift': nrm(6, (DEPTH, DEC_BATCH, D_MODEL), 1.0),
        'page_table': page_table,
        'g_mix': 1.0 + nrm(9, (DEPTH, D_MODEL), 0.05),
        'w_in': nrm(10, (DEPTH, D_MODEL, D_IN), D_MODEL ** -0.5),
        'mu': jax.random.uniform(keys[11], (DEPTH, R_COLS), f32),
        'w0': nrm(12, (DEPTH, D_RWKV), 0.5),
        'w2': nrm(13, (DEPTH, LORA_W, D_RWKV), LORA_W ** -0.5),
        'a0': nrm(14, (DEPTH, D_RWKV), 0.5),
        'a2': nrm(15, (DEPTH, LORA_A, D_RWKV), LORA_A ** -0.5),
        'g2': nrm(16, (DEPTH, LORA_G, D_RWKV), LORA_G ** -0.5),
        'k_k': 0.85 + nrm(17, (DEPTH, D_RWKV), 0.05),
        'k_a': 1.0 + nrm(18, (DEPTH, D_RWKV), 0.05),
        'r_k': nrm(19, (DEPTH, D_RWKV), 0.1),
        'lnx_w': 1.0 + nrm(20, (DEPTH, D_RWKV), 0.05),
        'lnx_b': nrm(21, (DEPTH, D_RWKV), 0.02),
        'phi_pe': nrm(22, (DEPTH, 2, L_CMP, HEAD_DIM), 0.1),
        'phi_w1': nrm(23, (DEPTH, 2, L_CMP * HEAD_DIM, PHI_HIDDEN), (L_CMP * HEAD_DIM) ** -0.5),
        'phi_w2': nrm(24, (DEPTH, 2, PHI_HIDDEN, HEAD_DIM), PHI_HIDDEN ** -0.5),
        'w_o': nrm(25, (DEPTH, D_MODEL, D_MODEL), D_MODEL ** -0.5),
        'g_ffn': 1.0 + nrm(26, (DEPTH, D_MODEL), 0.05),
        'w_gate': nrm(27, (DEPTH, D_MODEL, D_FF), D_MODEL ** -0.5),
        'w_up': nrm(28, (DEPTH, D_MODEL, D_FF), D_MODEL ** -0.5),
        'w_down': nrm(29, (DEPTH, D_FF, D_MODEL), D_FF ** -0.5),
        'g_final': 1.0 + nrm(30, (D_MODEL,), 0.05),
    }

def reference(x_prompt, x_sample, cache_cmp_kv, cache_slc_kv, cache_win_kv, state_wkv, state_shift, page_table,
              g_mix, w_in, mu, w0, w2, a0, a2, g2, k_k, k_a, r_k, lnx_w, lnx_b, phi_pe, phi_w1, phi_w2,
              w_o, g_ffn, w_gate, w_up, w_down, g_final):
    names = ('g_mix', 'w_in', 'mu', 'w0', 'w2', 'a0', 'a2', 'g2', 'k_k', 'k_a', 'r_k', 'lnx_w', 'lnx_b',
             'phi_pe', 'phi_w1', 'phi_w2', 'w_o', 'g_ffn', 'w_gate', 'w_up', 'w_down')
    params = (g_mix, w_in, mu, w0, w2, a0, a2, g2, k_k, k_a, r_k, lnx_w, lnx_b,
              phi_pe, phi_w1, phi_w2, w_o, g_ffn, w_gate, w_up, w_down)
    xp, xs = x_prompt, x_sample
    st_p, st_s = [], []
    for layer in range(DEPTH):
        lw = {n: p[layer] for n, p in zip(names, params)}
        mix_p, sp = token_mix_prompt(rms_norm(xp, lw['g_mix']), lw)
        xp = channel_mix(xp + mix_p, lw)
        mix_s, ss = token_mix_sample(rms_norm(xs, lw['g_mix']), cache_cmp_kv[layer], cache_slc_kv[layer],
                                     cache_win_kv[layer], state_wkv[layer], state_shift[layer], page_table, lw)
        xs = channel_mix(xs + mix_s, lw)
        st_p.append(sp)
        st_s.append(ss)
    stk = lambda grp, i: jnp.stack([s[i] for s in grp], axis=0)
    y_prompt = rms_norm(xp, g_final)
    y_sample = rms_norm(xs, g_final)
    return (y_prompt, y_sample,
            stk(st_p, 0), stk(st_p, 1), stk(st_p, 2), stk(st_p, 3), stk(st_p, 4),
            stk(st_s, 0), stk(st_s, 1), stk(st_s, 2), stk(st_s, 3), stk(st_s, 4))


_drawn_inputs = setup_inputs


def setup_inputs(seed=0):
    import zlib

    import numpy as np

    out = dict(_drawn_inputs(seed))
    spreads = {}
    factors = {'k_k': 29.054,
     'lnx_w': 2.943,
     'lnx_b': 7.255,
     'cache_cmp_kv': 3.552,
     'cache_slc_kv': 3.897,
     'phi_pe': 3.432}
    for name, (base, spread) in spreads.items():
        noise = np.random.default_rng([zlib.crc32(name.encode()), seed]).standard_normal(out[name].shape)
        drawn = base * np.exp(spread * noise) if base else spread * noise
        out[name] = __import__('jax').numpy.asarray(drawn.astype(out[name].dtype))
    for name, factor in factors.items():
        out[name] = (out[name] * factor).astype(out[name].dtype)
    return out
```

```python
from contextlib import ExitStack

import concourse.bass as bass
from concourse import mybir

F32 = mybir.dt.float32
I32 = mybir.dt.int32
U32 = mybir.dt.uint32
ALU = mybir.AluOpType
ACT = mybir.ActivationFunctionType
AX_X = mybir.AxisListType.X

P = 128
D = 2048
KT = D // P
SEQ = 512
NB = 8
TC = SEQ + NB
TA = TC + NB
HALF = TA // 2
D_R = 1024
NPAIR = D_R // P
R_COLS = 3328
KV0 = R_COLS + 1024
KVG = 1584
C = 64
D_IN = KV0 + KVG
LW, LA, LG = 96, 96, 64
D_FF = 5632
EPS = 1e-6
NEG = -1e30
ROW_TILES = [(0, 128), (128, 128), (256, 128), (384, 128), (SEQ, NB)]


POOL_DMA = ("stored", "loaded", "rows_out", "state_out", "gain_in", "mix_in")


def new_sem(nc, g, name):
    sem = nc.alloc_semaphore(name)
    if not any(n in name for n in POOL_DMA):
        g.sems.append(sem)
    return sem


def take_wait(g, eng):
    eng.sem_inc(g.waited, 1)


def retire_sems(nc, g):
    with nc.Block() as block:
        @block.gpsimd
        def _(pool):
            for sem in g.sems:
                pool.sem_clear(sem)
    for sem in g.sems:
        nc.release_semaphore(sem)
    g.sems = []


def stage_norm(nc, g):
    with ExitStack() as ctx:
        rows = ctx.enter_context(nc.sbuf_tensor("n_rows", [P, 2, D], F32))
        junk = ctx.enter_context(nc.sbuf_tensor("n_junk", [P, D], F32))
        gain = ctx.enter_context(nc.sbuf_tensor("n_gain", [P, D], F32))
        xnr = ctx.enter_context(nc.sbuf_tensor("n_xnr", [P, 2, D], F32))
        stat = ctx.enter_context(nc.sbuf_tensor("n_stat", [P, 6, 4], F32))
        ps = ctx.enter_context(nc.psum_tensor("n_ps", [P, 4, 512], F32))
        loaded = [new_sem(nc, g, f"n_loaded{i}") for i in range(2)]
        gain_in = new_sem(nc, g, "n_gain_in")
        ms_ready = new_sem(nc, g, "n_ms_ready")
        root_ready = new_sem(nc, g, "n_root_ready")
        xn_ready = new_sem(nc, g, "n_xn_ready")
        turned = new_sem(nc, g, "n_turned")
        copied = new_sem(nc, g, "n_copied")
        stored_prompt = new_sem(nc, g, "n_stored_prompt")
        stored_sample = new_sem(nc, g, "n_stored_sample")
        chain = new_sem(nc, g, "n_chain")
        tiles = [(g.x_prompt[r:r + n, :], r, n) for r, n in ROW_TILES[:4]]
        tiles += [(g.x_sample, SEQ, NB), (g.shift, TC, NB)]
        with nc.Block() as block:
            @block.sync
            def _(sp):
                sp.dma_start(gain[:], g.g_mix[None, :].to_broadcast([P, D])).then_inc(gain_in, 16)
                for i, (src, _c, n) in enumerate(tiles):
                    if i >= 2:
                        sp.wait_ge(xn_ready, i - 1)
                    sp.dma_start(rows[0:n, i % 2, :], src).then_inc(loaded[i % 2], 16)

            @block.vector
            def _(dve):
                c = 0
                dve.memset(junk[:], 0.0).then_inc(chain, 1)
                c += 1
                dve.wait_ge(chain, c)
                for i, (_s, _c, n) in enumerate(tiles):
                    x = rows[0:n, i % 2, :]
                    dve.wait_ge(loaded[i % 2], 16 * (i // 2 + 1))
                    if i < 5:
                        dve.tensor_tensor_reduce(out=junk[0:n, :], in0=x, in1=x, scale=1.0, scalar=0.0, op0=ALU.mult,
                                                 op1=ALU.add, accum_out=stat[0:n, i, 0:1]).then_inc(chain, 1)
                        c += 1
                        dve.wait_ge(chain, c)
                        dve.tensor_scalar(stat[0:n, i, 1:2], stat[0:n, i, 0:1], 1.0 / D, EPS, ALU.mult,
                                          ALU.add).then_inc(ms_ready, 1)
                        dve.wait_ge(root_ready, i + 1)
                        dve.reciprocal(stat[0:n, i, 3:4], stat[0:n, i, 2:3]).then_inc(chain, 1)
                        c += 1
                        dve.wait_ge(chain, c)
                    if i == 0:
                        dve.wait_ge(gain_in, 16)
                    if i >= 2:
                        dve.wait_ge(turned, 4 * (i - 1))
                    if i == 5:
                        dve.wait_ge(stored_prompt, 16)
                    if i < 5:
                        dve.scalar_tensor_tensor(out=xnr[0:n, i % 2, :], in0=x, scalar=stat[0:n, i, 3:4],
                                                 in1=gain[0:n, :], op0=ALU.mult, op1=ALU.mult).then_inc(xn_ready, 1)
                    else:
                        dve.tensor_copy(xnr[0:n, i % 2, :], x).then_inc(xn_ready, 1)
                    for q in range(4):
                        dve.wait_ge(turned, 4 * i + q + 1)
                        dve.tensor_copy(g.xn[:, 4 * q:4 * q + 4, _c:_c + n],
                                        ps[:, q, :].rearrange("p (k t) -> p k t", k=4)[:, :, 0:n]).then_inc(copied, 1)

            @block.scalar
            def _(act):
                for i in range(5):
                    n = tiles[i][2]
                    act.wait_ge(ms_ready, i + 1)
                    act.activation(stat[0:n, i, 2:3], stat[0:n, i, 1:2], ACT.Sqrt).then_inc(root_ready, 1)

            @block.tensor
            def _(pe):
                for i, (_s, _c, n) in enumerate(tiles):
                    pe.wait_ge(xn_ready, i + 1)
                    for q in range(4):
                        if i >= 1:
                            pe.wait_ge(copied, 4 * (i - 1) + q + 1)
                        for k in range(4):
                            last = pe.transpose(ps[:, q, k * P:k * P + n],
                                                xnr[0:n, i % 2, (4 * q + k) * P:(4 * q + k + 1) * P],
                                                g.ident[0:n, 0:n])
                        last.then_inc(turned, 1)

            @block.gpsimd
            def _(pool):
                pool.wait_ge(xn_ready, 4)
                pool.dma_start(g.new_shift_prompt, xnr[P - 1:P, 1, :]).then_inc(stored_prompt, 16)
                pool.wait_ge(xn_ready, 5)
                pool.dma_start(g.new_shift_sample, xnr[0:NB, 0, :]).then_inc(stored_sample, 16)
                pool.wait_ge(stored_prompt, 16)
                pool.wait_ge(stored_sample, 16)



def stage_in_proj(nc, g):
    with ExitStack() as ctx:
        wbuf = ctx.enter_context(nc.sbuf_tensor("p_w", [P, 2, KT, 256], F32))
        ob = ctx.enter_context(nc.sbuf_tensor("p_ob", [P, 4, TA], F32))
        orow = ctx.enter_context(nc.sbuf_tensor("p_orow", [P, 2, 5, 256], F32))
        ps = ctx.enter_context(nc.psum_tensor("p_ps", [P, 8, 512], F32))
        loaded = [new_sem(nc, g, f"p_loaded{i}") for i in range(2)]
        summed = [new_sem(nc, g, f"p_summed{i}") for i in range(4)]
        copied = [new_sem(nc, g, f"p_copied{i}") for i in range(4)]
        stored = [new_sem(nc, g, f"p_stored{i}") for i in range(4)]
        row_summed = [new_sem(nc, g, f"p_row_summed{i}") for i in range(5)]
        row_copied = [new_sem(nc, g, f"p_row_copied{i}") for i in range(5)]
        row_stored = [new_sem(nc, g, f"p_row_stored{i}") for i in range(2)]
        w_view = g.w_in.rearrange("(k p) n -> p k n", p=P)
        pairs = KV0 // 512
        kpairs = 3
        assert KV0 == pairs * 512 + 256

        with nc.Block() as block:
            @block.sync
            def _(sp):
                def load(b, col, n):
                    sp.dma_start(wbuf[:, b, :, 0:n], w_view[:, :, bass.ds(col, n)]).then_inc(loaded[b], 16)
                with sp.Fori(0, pairs) as i:
                    for b in range(2):
                        sp.wait_ge(summed[2 * b + 1], i)
                        load(b, i * 512 + b * 256, 256)
                sp.wait_ge(summed[1], pairs)
                load(0, pairs * 512, 256)
                for b in (1, 0):
                    sp.wait_ge(summed[2 * b + 1], pairs + 1 - b)
                load(1, KV0, 256)
                with sp.Fori(0, kpairs - 1) as i:
                    sp.wait_ge(row_summed[4], i * 2)
                    load(0, i * 512 + KV0 + 256, 256)
                    sp.wait_ge(row_summed[4], i * 2 + 1)
                    load(1, i * 512 + KV0 + 512, 256)
                sp.wait_ge(row_summed[4], 2 * kpairs - 2)
                load(0, KV0 + 1280, 256)
                sp.wait_ge(row_summed[4], 2 * kpairs - 1)
                load(1, KV0 + 1536, 48)

            @block.tensor
            def _(pe):
                def columns(i, b):
                    pe.wait_ge(loaded[b], (i + 1) * 16)
                    for m in range(2):
                        s = 2 * b + m
                        pe.wait_ge(copied[s], i * 2)
                        for k in range(KT):
                            for h in range(2):
                                last = pe.matmul(ps[:, 2 * s + h, 0:HALF], wbuf[:, b, k, m * P:(m + 1) * P],
                                                 g.xn[:, k, h * HALF:(h + 1) * HALF], start=(k == 0),
                                                 stop=(k == KT - 1))
                        last.then_inc(summed[s], 1)

                def rows(chunk, b, uses, n):
                    pe.wait_ge(loaded[b], (uses + 1) * 16)
                    for t, (r, m) in enumerate(ROW_TILES):
                        pe.wait_ge(row_copied[t], chunk)
                        for k in range(KT):
                            last = pe.matmul(ps[0:m, t, 0:n], g.xn[:, k, r:r + m],
                                             wbuf[:, b, k, 0:n], start=(k == 0), stop=(k == KT - 1))
                        last.then_inc(row_summed[t], 1)

                with pe.Fori(0, pairs) as i:
                    for b in range(2):
                        columns(i, b)
                columns(pairs, 0)
                for s in range(4):
                    pe.wait_ge(copied[s], 2 * (pairs + (s < 2)))
                with pe.Fori(0, kpairs) as i:
                    for b in (1, 0):
                        rows(2 * i + 1 - b, b, i + pairs + 1 - b, 256)
                rows(2 * kpairs, 1, pairs + kpairs, 48)

            def copy_columns(eng, i, b, m, copy):
                s = 2 * b + m
                eng.wait_ge(summed[s], i + 1)
                eng.wait_ge(stored[s], i * 16)
                for h in range(2):
                    copy(ob[:, s, h * HALF:(h + 1) * HALF], ps[:, 2 * s + h, 0:HALF]).then_inc(copied[s], 1)

            @block.vector
            def _(dve):
                with dve.Fori(0, pairs) as i:
                    for b in range(2):
                        copy_columns(dve, i, b, 0, dve.tensor_copy)
                copy_columns(dve, pairs, 0, 0, dve.tensor_copy)
                with dve.Fori(0, kpairs) as i:
                    for b in (1, 0):
                        dve.wait_ge(row_stored[b], i * 32)
                        for t, (_r, m) in enumerate(ROW_TILES):
                            dve.wait_ge(row_summed[t], 2 * i + 2 - b)
                            dve.tensor_copy(orow[0:m, b, t, :], ps[0:m, t, 0:256]).then_inc(row_copied[t], 1)

            @block.scalar
            def _(act):
                with act.Fori(0, pairs) as i:
                    for b in range(2):
                        copy_columns(act, i, b, 1, act.copy)
                copy_columns(act, pairs, 0, 1, act.copy)
                act.wait_ge(row_stored[1], kpairs * 32)
                for t, (_r, m) in enumerate(ROW_TILES):
                    act.wait_ge(row_summed[t], 2 * kpairs + 1)
                    act.activation(orow[0:m, 1, t, 0:48], ps[0:m, t, 0:48], ACT.Sigmoid).then_inc(row_copied[t], 1)

            @block.gpsimd
            def _(pool):
                def store_columns(i, b):
                    for m in range(2):
                        s = 2 * b + m
                        pool.wait_ge(copied[s], i * 2 + 2)
                        pool.dma_start(g.proj_t[bass.ds(i * 512 + s * P, P), :], ob[:, s, :]).then_inc(stored[s], 16)

                def store_rows(chunk, b, dst, n):
                    for t in range(5):
                        pool.wait_ge(row_copied[t], chunk + 1)
                    pool.dma_start(dst[0:SEQ].rearrange("(t p) n -> p t n", p=P),
                                   orow[:, b, 0:4, 0:n]).then_inc(row_stored[b], 16)
                    pool.dma_start(dst[SEQ:TC], orow[0:NB, b, 4, 0:n]).then_inc(row_stored[b], 16)

                with pool.Fori(0, pairs) as i:
                    for b in range(2):
                        store_columns(i, b)
                store_columns(pairs, 0)
                with pool.Fori(0, kpairs) as i:
                    for b in (1, 0):
                        store_rows(2 * i + 1 - b, b, g.kv_rows[:, bass.ds(i * 512 + (1 - b) * 256, 256)], 256)
                store_rows(2 * kpairs, 1, g.gates, 48)
                for s in range(4):
                    pool.wait_ge(stored[s], 16 * (pairs + (s < 2)))
                for b in range(2):
                    pool.wait_ge(row_stored[b], 32 * (kpairs + b))


class Arrays:
    pass


class Chain:

    def __init__(self, eng, sem, base=0):
        self.eng, self.sem, self.base, self.n = eng, sem, base, 0

    def __call__(self, ins):
        ins.then_inc(self.sem, 1)
        self.n += 1
        self.eng.wait_ge(self.sem, self.base + self.n)


def stage_rwkv_prep(nc, g):
    CH = SEQ // C
    HC = TC // 2
    DECAY = -0.6065306597126334
    with ExitStack() as ctx:
        def sb(name, shape):
            return ctx.enter_context(nc.sbuf_tensor("r_" + name, shape, F32))

        def sem(name):
            return new_sem(nc, g, "r_" + name)

        raw = sb("raw", [P, 3, TA + 1])
        diff = sb("diff", [P, 3, TC])
        xr = sb("xr", [P, 3, TC])
        lraw = sb("lraw", [P, 3, TA + 1])
        lora = sb("lora", [P, 3, TC])
        lmu = sb("lmu", [P, 3])
        lw = sb("lw", [P, 3, P])
        vec = sb("vec", [P, 8, NPAIR])
        cv = sb("cv", [P, 8])
        reset = sb("reset", [P, CH, C])
        sw = sb("sw", [P, TC])
        a = sb("a", [P, TC])
        dec = sb("dec", [P, TC])
        kk = sb("kk", [P, TC])
        sq = sb("sq", [P, TC])
        nrm = sb("nrm", [P, TC])
        kf = sb("kf", [P, TC])
        bvec = sb("bvec", [P, TC])
        rkk = sb("rkk", [P, TC])
        cum = sb("cum", [P, 2, SEQ])
        ex = sb("ex", [P, 3, SEQ])
        samp = sb("samp", [P, NPAIR, 6, NB])
        srow = sb("srow", [6 * NB, D_R])
        outb = sb("outb", [P, CH, 5, C])
        ps = ctx.enter_context(nc.psum_tensor("r_ps", [P, 8, 512], F32))
        vec_in, lraw_in, raw_in, lw_in = sem("vec_in"), sem("lraw_in"), sem("raw_in"), sem("lw_in")
        chain, lora_ready, lora_act = sem("chain"), sem("lora_ready"), sem("lora_act")
        z_done, cv_ready, sig_done, g_done = sem("z_done"), sem("cv_ready"), sem("sig_done"), sem("g_done")
        x_ready, sq_ready, ss_done, norm_done = sem("x_ready"), sem("sq_ready"), sem("ss_done"), sem("norm_done")
        rkk_ready, bonus_done, cum_ready, exp_done = sem("rkk_ready"), sem("bonus_done"), sem("cum_ready"), sem("exp_done")
        out_ready, stored, rows_turned, rows_copied, rows_out = (sem("out_ready"), sem("stored"), sem("rows_turned"),
                                                                 sem("rows_copied"), sem("rows_out"))
        zero_ready, bonus_used = sem("zero_ready"), sem("bonus_used")
        lora_rows = [(3 * D_R, LW), (3 * D_R + LW, LA), (3 * D_R + LW + LA, LG)]
        vecs = [g.mu[0:D_R], g.mu[D_R:2 * D_R], g.mu[2 * D_R:3 * D_R], g.w0, g.a0, g.k_k, g.k_a, g.r_k]
        STEPS = 18

        with nc.Block() as block:
            @block.sync
            def _(sp):
                with nc.allow_non_contiguous_dma(reason="one value to a partition"):
                    for j, v in enumerate(vecs):
                        sp.dma_start(vec[:, j, :], v.rearrange("(q p) -> p q", p=P)).then_inc(vec_in, 16)
                    for j, (r, n) in enumerate(lora_rows):
                        sp.dma_start(lmu[0:n, j:j + 1], g.mu[r:r + n].rearrange("(p o) -> p o", o=1)).then_inc(vec_in, 16)
                for j, (r, n) in enumerate(lora_rows):
                    sp.dma_start(lraw[0:n, j, 1:], g.proj_t[r:r + n, :]).then_inc(lraw_in, 16)
                with sp.Fori(0, NPAIR) as i:
                    sp.wait_ge(z_done, i * 3)
                    sp.wait_ge(x_ready, i)
                    for j in range(3):
                        sp.dma_start(raw[:, j, 1:], g.proj_t[bass.ds(i * P + j * D_R, P), :]).then_inc(raw_in, 16)
                    for j, w in enumerate((g.w2, g.a2, g.g2)):
                        n = lora_rows[j][1]
                        sp.dma_start(lw[0:n, j, :], w[:, bass.ds(i * P, P)]).then_inc(lw_in, 16)

            @block.gpsimd
            def _(pool):
                with pool.Fori(0, NPAIR) as i:
                    pool.wait_ge(out_ready, i + 1)
                    pool.dma_start(g.rk_chunks[:, :, bass.ds(i, 1), :].rearrange("c p q n -> p c (q n)"),
                                   outb[:].rearrange("p c f t -> p c (f t)")).then_inc(stored, 16)
                pool.wait_ge(rows_copied, 2)
                pool.dma_start(g.samp_rows, srow[:]).then_inc(rows_out, 16)
                pool.wait_ge(stored, 16 * NPAIR)
                pool.wait_ge(rows_out, 16)

            @block.tensor
            def _(pe):
                pe.wait_ge(lora_act, 3)
                with pe.Fori(0, NPAIR) as i:
                    pe.wait_ge(lw_in, i * 48 + 48)
                    pe.wait_ge(bonus_used, i)
                    pe.wait_ge(sig_done, i * 2)
                    pe.wait_ge(g_done, i)
                    for j in range(3):
                        n = lora_rows[j][1]
                        for h in range(2):
                            last = pe.matmul(ps[:, 2 * j + h, 0:HC], lw[0:n, j, :], lora[0:n, j, h * HC:(h + 1) * HC],
                                             start=True, stop=True)
                        last.then_inc(z_done, 1)
                    pe.wait_ge(sq_ready, i + 1)
                    pe.wait_ge(norm_done, i)
                    for h in range(2):
                        last = pe.matmul(ps[:, 6 + h, 0:HC], g.blk64[:], sq[:, h * HC:(h + 1) * HC], start=True, stop=True)
                    last.then_inc(ss_done, 1)
                    pe.wait_ge(rkk_ready, i + 1)
                    pe.wait_ge(sig_done, i * 2 + 2)
                    for h in range(2):
                        last = pe.matmul(ps[:, h, 0:HC], g.blk64[:], rkk[:, h * HC:(h + 1) * HC], start=True, stop=True)
                    last.then_inc(bonus_done, 1)
                pe.wait_ge(out_ready, NPAIR)
                pe.wait_ge(g_done, NPAIR)
                for q in range(NPAIR):
                    last = pe.transpose(ps[0:6 * NB, 4 + q // 4, (q % 4) * P:(q % 4 + 1) * P],
                                        samp[:, q, :, :].rearrange("p f b -> p (f b)"), g.ident[:])
                last.then_inc(rows_turned, 1)

            @block.scalar
            def _(act):
                act.wait_ge(lora_ready, 3)
                act.activation(lora[0:LW, 0, :], lora[0:LW, 0, :], ACT.Tanh).then_inc(lora_act, 1)
                act.copy(lora[0:LA, 1, :], lora[0:LA, 1, :]).then_inc(lora_act, 1)
                act.activation(lora[0:LG, 2, :], lora[0:LG, 2, :], ACT.Sigmoid).then_inc(lora_act, 1)
                with act.Fori(0, NPAIR) as i:
                    act.wait_ge(cv_ready, i + 1)
                    for j, (dst, sem_) in enumerate(((sw, sig_done), (a, sig_done))):
                        act.wait_ge(z_done, i * 3 + j + 1)
                        act.activation(dst[:, 0:HC], ps[:, 2 * j, 0:HC], ACT.Sigmoid, bias=cv[:, 3 + j:4 + j])
                        act.activation(dst[:, HC:TC], ps[:, 2 * j + 1, 0:HC], ACT.Sigmoid,
                                       bias=cv[:, 3 + j:4 + j]).then_inc(sem_, 1)
                    act.wait_ge(z_done, i * 3 + 3)
                    gt = g.gate_t[:, bass.ds(i, 1), :].rearrange("p a t -> p (a t)")
                    act.copy(gt[:, 0:HC], ps[:, 4, 0:HC])
                    act.copy(gt[:, HC:TC], ps[:, 5, 0:HC]).then_inc(g_done, 1)
                    act.wait_ge(ss_done, i + 1)
                    act.activation(nrm[:, 0:HC], ps[:, 6, 0:HC], ACT.Sqrt)
                    act.activation(nrm[:, HC:TC], ps[:, 7, 0:HC], ACT.Sqrt).then_inc(norm_done, 1)
                    act.wait_ge(cum_ready, i + 1)
                    act.activation(ex[:, 0, :], cum[:, 0, :], ACT.Exp)
                    act.activation(ex[:, 1, :], cum[:, 0, :], ACT.Exp, scale=-1.0)
                    act.activation(ex[:, 2, :], cum[:, 1, :], ACT.Exp)
                    act.activation(samp[:, bass.ds(i, 1), 0, :].rearrange("p a b -> p (a b)"), dec[:, SEQ:TC],
                                   ACT.Exp).then_inc(exp_done, 1)

            @block.vector
            def _(dve):
                step = Chain(dve, chain)
                step(dve.memset(raw[:, :, 0:1], 0.0))
                step(dve.memset(lraw[:, :, 0:1], 0.0))
                step(dve.memset(reset[:], 1.0))
                step(dve.memset(reset[:, :, 0:1], 0.0))
                dve.wait_ge(vec_in, 16 * 11)
                dve.wait_ge(lraw_in, 48)
                for j, (_r, n) in enumerate(lora_rows):
                    x, d, o = lraw[0:n, j, :], diff[0:n, j, :], lora[0:n, j, :]
                    step(dve.tensor_tensor(d[:, 0:SEQ], x[:, 0:SEQ], x[:, 1:SEQ + 1], ALU.subtract))
                    step(dve.tensor_tensor(d[:, SEQ:TC], x[:, TC + 1:TA + 1], x[:, SEQ + 1:TC + 1], ALU.subtract))
                    dve.scalar_tensor_tensor(out=o, in0=d, scalar=lmu[0:n, j:j + 1], in1=x[:, 1:TC + 1], op0=ALU.mult,
                                             op1=ALU.add).then_inc(lora_ready, 1)
                dve.wait_ge(lora_ready, 3)
                before = step.n
                with dve.Fori(0, NPAIR) as i:
                    step = Chain(dve, chain, i * STEPS + before)
                    dve.wait_ge(sig_done, i * 2)
                    dve.tensor_copy(cv[:], vec[:, :, bass.ds(i, 1)].rearrange("p v a -> p (v a)")).then_inc(cv_ready, 1)
                    dve.wait_ge(cv_ready, i + 1)
                    dve.wait_ge(raw_in, i * 48 + 48)
                    step(dve.tensor_tensor(diff[:, :, 0:SEQ], raw[:, :, 0:SEQ], raw[:, :, 1:SEQ + 1], ALU.subtract))
                    step(dve.tensor_tensor(diff[:, :, SEQ:TC], raw[:, :, TC + 1:TA + 1], raw[:, :, SEQ + 1:TC + 1],
                                           ALU.subtract))
                    for j in range(3):
                        ins = dve.scalar_tensor_tensor(out=xr[:, j, :], in0=diff[:, j, :], scalar=cv[:, j:j + 1],
                                                       in1=raw[:, j, 1:TC + 1], op0=ALU.mult, op1=ALU.add)
                    ins.then_inc(x_ready, 1)
                    dve.wait_ge(x_ready, i + 1)
                    r, k, v = xr[:, 0, :], xr[:, 1, :], xr[:, 2, :]
                    step(dve.tensor_scalar(kk[:], k, cv[:, 5:6], None, ALU.mult))
                    dve.tensor_tensor(sq[:], kk[:], kk[:], ALU.mult).then_inc(sq_ready, 1)
                    dve.wait_ge(sig_done, i * 2 + 2)
                    step(dve.tensor_scalar(kf[:], a[:], -1.0, cv[:, 6:7], ALU.add, ALU.mult))
                    step(dve.scalar_tensor_tensor(out=kf[:], in0=kf[:], scalar=1.0, in1=k, op0=ALU.add, op1=ALU.mult))
                    dve.scalar_tensor_tensor(out=rkk[:], in0=r, scalar=cv[:, 7:8], in1=kf[:], op0=ALU.mult,
                                             op1=ALU.mult).then_inc(rkk_ready, 1)
                    step(dve.tensor_scalar(dec[:], sw[:], DECAY, None, ALU.mult))
                    step(dve.tensor_tensor_scan(cum[:, 0, :], reset[:].rearrange("p c t -> p (c t)"), dec[:, 0:SEQ], 0.0,
                                                ALU.mult, ALU.add))
                    dve.tensor_tensor(cum[:, 1, :], cum[:, 0, :], dec[:, 0:SEQ], ALU.subtract).then_inc(cum_ready, 1)
                    dve.wait_ge(norm_done, i + 1)
                    step(dve.tensor_scalar(nrm[:], nrm[:], 1e-12, None, ALU.max))
                    step(dve.reciprocal(nrm[:], nrm[:]))
                    step(dve.tensor_tensor(kk[:], kk[:], nrm[:], ALU.mult))
                    step(dve.tensor_tensor(bvec[:], kk[:], a[:], ALU.mult))
                    dve.wait_ge(bonus_done, i + 1)
                    bt = g.bonus_t[:, bass.ds(i, 1), :].rearrange("p a t -> p (a t)")
                    step(dve.tensor_tensor(bt[:, 0:HC], v[:, 0:HC], ps[:, 0, 0:HC], ALU.mult))
                    dve.tensor_tensor(bt[:, HC:TC], v[:, HC:TC], ps[:, 1, 0:HC], ALU.mult).then_inc(bonus_used, 1)
                    dve.wait_ge(exp_done, i + 1)
                    dve.wait_ge(stored, i * 16)

                    def chunks(x):
                        return x.rearrange("p (c t) -> p c t", t=C)

                    dve.scalar_tensor_tensor(out=outb[:, :, 0, :], in0=chunks(kk[:, 0:SEQ]), scalar=-1.0,
                                             in1=chunks(ex[:, 2, :]), op0=ALU.mult, op1=ALU.mult)
                    dve.tensor_tensor(outb[:, :, 1, :], chunks(r[:, 0:SEQ]), chunks(ex[:, 0, :]), ALU.mult)
                    dve.tensor_copy(outb[:, :, 2, :], chunks(v[:, 0:SEQ]))
                    dve.tensor_tensor(outb[:, :, 3, :], chunks(bvec[:, 0:SEQ]), chunks(ex[:, 1, :]), ALU.mult)
                    dve.tensor_tensor(outb[:, :, 4, :], chunks(kf[:, 0:SEQ]), chunks(ex[:, 1, :]), ALU.mult)
                    step(dve.tensor_copy(g.chunk_decay[:, bass.ds(i, 1), :].rearrange("p a c -> p (a c)"),
                                         chunks(ex[:, 0, :])[:, :, C - 1]))
                    sm = samp[:, bass.ds(i, 1), :, :].rearrange("p a f b -> p (a f) b")
                    step(dve.tensor_scalar(sm[:, 1, :], kk[:, SEQ:TC], -1.0, None, ALU.mult))
                    step(dve.tensor_copy(sm[:, 2, :], bvec[:, SEQ:TC]))
                    step(dve.tensor_copy(sm[:, 3, :], kf[:, SEQ:TC]))
                    step(dve.tensor_copy(sm[:, 4, :], r[:, SEQ:TC]))
                    step(dve.tensor_copy(sm[:, 5, :], v[:, SEQ:TC]))
                    dve.tensor_copy(g.v_samp[:, bass.ds(i, 1), :].rearrange("p a b -> p (a b)"),
                                    v[:, SEQ:TC]).then_inc(out_ready, 1)
                    dve.wait_ge(out_ready, i + 1)
                    assert step.n == STEPS, step.n
                dve.wait_ge(rows_turned, 1)
                for h in range(2):
                    dve.tensor_copy(srow[:, h * 512:(h + 1) * 512], ps[0:6 * NB, 4 + h, :]).then_inc(rows_copied, 1)


def stage_rwkv_chunks(nc, g):
    CH = SEQ // C
    NH = 8
    with ExitStack() as ctx:
        def sb(name, shape):
            return ctx.enter_context(nc.sbuf_tensor("s_" + name, shape, F32))

        def sem(name):
            return new_sem(nc, g, "s_" + name)

        cur = sb("cur", [P, 2, NPAIR, 5, C])
        G = sb("G", [P, 2, NH, P])
        L1, Lo32, Lo64 = sb("L1", [C, 2, NH, C]), sb("Lo32", [C, 2, NH, C]), sb("Lo64", [C, 2, NH, C])
        N1, X = sb("N1", [C, 2, NH, C]), sb("X", [C, 2, NH, C])
        N2, L2, N4, L4, L8 = (sb(n, [C, 2, NH, C]) for n in ("N2", "L2", "N4", "L4", "L8"))
        W, XT, Up = sb("W", [C, 2, NH, C]), sb("XT", [C, 2, NH, C]), sb("Up", [C, 2, NH, C])
        UV = sb("UV", [P, NPAIR, P])
        BK = sb("BK", [P, NPAIR, P])
        S = sb("S", [P, NPAIR, C])
        tmp = sb("tmp", [P, NPAIR, C])
        srow = sb("srow", [C, NPAIR, P])
        ps = ctx.enter_context(nc.psum_tensor("s_ps", [P, 8, 512], F32))
        loaded = [sem("loaded0"), sem("loaded1")]
        pe_done = [sem("pe_done0"), sem("pe_done1")]
        dve_done = [sem("dve_done0"), sem("dve_done1")]
        act_done = [sem("act_done0"), sem("act_done1")]
        zeroed, state_turned, state_copied, state_out = sem("zeroed"), sem("state_turned"), sem("state_copied"), sem("state_out")
        PN, DN, AN = 22, 14, 14

        def bank(gr, n, rows=P):
            return ps[0:rows, 4 * gr + n, :]

        def heads(ap, w=C):
            return ap.rearrange("p (h t) -> p h t", t=w)

        with nc.Block() as block:
            @block.sync
            def _(sp):
                def load(c, b):
                    sp.dma_start(cur[:, b, :, :, :].rearrange("p q f t -> p (q f t)"),
                                 g.rk_chunks[bass.ds(c, 1), :, :, :].rearrange("c p q n -> p (c q n)")
                                 ).then_inc(loaded[b], 16)
                for b in range(2):
                    load(b, b)
                with sp.Fori(0, CH // 2 - 1) as i:
                    for b in range(2):
                        for gr in range(2):
                            sp.wait_ge(pe_done[gr], i * 2 * PN + (b + 1) * PN)
                        load(i * 2 + 2 + b, b)

            @block.tensor
            def _(pe):
                pe.wait_ge(zeroed, 2)
                with pe.Fori(0, CH // 2) as i:
                    for b in range(2):
                        c = i * 2 + b
                        pe.wait_ge(loaded[b], i * 16 + 16)

                        def feat(q, gr, f):
                            return cur[gr * C:(gr + 1) * C, b, q, f, :]

                        def square(out, lhs, rhs, gr):
                            for h in range(NH):
                                last = pe.matmul(out[:, h * C:(h + 1) * C], lhs[:, gr, h, :], rhs[:, gr, h, :],
                                                 start=True, stop=True)
                            return last

                        def need(gr, d, a):
                            pe.wait_ge(dve_done[gr], c * DN + d) if d is not None else None
                            pe.wait_ge(act_done[gr], c * AN + a) if a is not None else None
                            take_wait(g, pe)

                        for gr in range(2):
                            need(gr, 0, 0)
                            for h in range(NH):
                                lo = gr * C
                                last = pe.matmul(bank(gr, h // 4)[:, (h % 4) * P:(h % 4 + 1) * P],
                                                 cur[lo:lo + C, b, h, 3:5, :].rearrange("p f t -> p (f t)"),
                                                 cur[lo:lo + C, b, h, 0:2, :].rearrange("p f t -> p (f t)"),
                                                 start=True, stop=True)
                            last.then_inc(pe_done[gr], 1)
                        for gr in range(2):
                            for h in range(NH):
                                last = pe.matmul(bank(gr, 2, C)[:, h * C:(h + 1) * C], feat(h, gr, 0), feat(h, gr, 3),
                                                 start=True, stop=True)
                            last.then_inc(pe_done[gr], 1)
                        for gr in range(2):
                            for q in range(4):
                                last = pe.transpose(bank(gr, 3)[:, q * P:(q + 1) * P],
                                                    cur[:, b, gr * 4 + q, 1:3, :].rearrange("p f t -> p (f t)"), g.ident[:])
                            last.then_inc(pe_done[gr], 1)
                        for gr in range(2):
                            need(gr, 4, None)
                            for q in range(4):
                                last = pe.transpose(bank(gr, 2)[:, q * P:(q + 1) * P],
                                                    cur[:, b, gr * 4 + q, 3:5, :].rearrange("p f t -> p (f t)"), g.ident[:])
                            last.then_inc(pe_done[gr], 1)
                        for n, lhs, rhs, d, a in ((0, L1, N1, 5, 1), (1, N1, L1, 5, 1),
                                                  (3, L2, N2, 5, 4), (0, N2, L2, 5, 4),
                                                  (2, L2, X, 6, 4),
                                                  (1, N4, L4, 6, 6), (3, L4, X, 7, 6),
                                                  (0, L8, X, 8, 7), (1, Lo32, X, 9, 7)):
                            for gr in range(2):
                                need(gr, d, a)
                                square(bank(gr, n, C), lhs, rhs, gr).then_inc(pe_done[gr], 1)
                        for n, d, a in ((2, 9, 8),):
                            for gr in range(2):
                                need(gr, d, a)
                                for h in range(NH):
                                    last = pe.transpose(bank(gr, n, C)[:, h * C:(h + 1) * C], X[:, gr, h, :],
                                                        g.ident[0:C, 0:C])
                                last.then_inc(pe_done[gr], 1)
                        for n, lhs, rhs, d, a in ((3, XT, W, 9, 9), (0, Lo64, X, 10, 9)):
                            for gr in range(2):
                                need(gr, d, a)
                                square(bank(gr, n, C), lhs, rhs, gr).then_inc(pe_done[gr], 1)
                        for gr in range(2):
                            need(gr, 10, 9)
                            for h in range(NH):
                                last = pe.transpose(bank(gr, 1, C)[:, h * C:(h + 1) * C], X[:, gr, h, :],
                                                    g.ident[0:C, 0:C])
                            last.then_inc(pe_done[gr], 1)
                        for gr in range(2):
                            need(gr, 10, 11)
                            square(bank(gr, 2, C), XT, W, gr).then_inc(pe_done[gr], 1)
                        for gr in range(2):
                            lo = gr * C
                            for q in range(NPAIR):
                                out = bank(gr, 3, C)[:, q * C:(q + 1) * C]
                                pe.matmul(out, feat(q, gr, 0), S[lo:lo + C, q, :], start=True, stop=False)
                                last = pe.matmul(out, G[:, gr, q, 0:C], UV[:, q, lo:lo + C], start=False, stop=True)
                            last.then_inc(pe_done[gr], 1)
                        for gr in range(2):
                            need(gr, 11, 12)
                            square(bank(gr, 0, C), X, Up, gr).then_inc(pe_done[gr], 1)
                        for gr in range(2):
                            need(gr, 11, 13)
                            lo = gr * C
                            for q in range(NPAIR):
                                out = ps[lo:lo + C, 4 * gr + 1, q * C:(q + 1) * C]
                                pe.matmul(out, S[lo:lo + C, q, :], feat(q, gr, 1), start=True, stop=False)
                                last = pe.matmul(out, UV[:, q, lo:lo + C], G[:, gr, q, C:P], start=False, stop=True)
                            last.then_inc(pe_done[gr], 1)
                        for gr in range(2):
                            for q in range(4):
                                last = pe.matmul(bank(gr, 2)[:, q * P:(q + 1) * P], BK[:, 4 * gr + q, :],
                                                 UV[:, 4 * gr + q, :], start=True, stop=True)
                            last.then_inc(pe_done[gr], 1)
                for gr in range(2):
                    pe.wait_ge(dve_done[gr], CH * DN)
                    pe.wait_ge(act_done[gr], CH * AN)
                for q in range(NPAIR):
                    last = pe.transpose(ps[0:C, q // 4, (q % 4) * P:(q % 4 + 1) * P], S[:, q, :], g.ident[:])
                last.then_inc(state_turned, 1)

            @block.scalar
            def _(act):
                with act.Fori(0, CH // 2) as i:
                    for b in range(2):
                        c = i * 2 + b

                        def copy(gr, p, out, in_):
                            act.wait_ge(pe_done[gr], c * PN + p)
                            act.copy(out, in_).then_inc(act_done[gr], 1)

                        for gr in range(2):
                            copy(gr, 3, UV[C:P, 4 * gr:4 * gr + 4, :], heads(ps[C:P, 4 * gr + 3, :], P))
                        for gr in range(2):
                            copy(gr, 4, BK[:, 4 * gr:4 * gr + 4, :], heads(bank(gr, 2), P))
                        for p, n, dst in ((5, 0, N2), (6, 1, L2), (7, 3, N4), (8, 0, L4), (10, 1, L8),
                                          (13, 1, W), (14, 2, XT), (16, 0, W), (17, 1, XT),
                                          (19, 3, Up)):
                            for gr in range(2):
                                copy(gr, p, dst[:, gr, :, :], heads(bank(gr, n, C)))
                        for gr in range(2):
                            copy(gr, 20, UV[0:C, :, gr * C:(gr + 1) * C], heads(bank(gr, 0, C)))
                        for gr in range(2):
                            copy(gr, 21, g.y_t[gr * C:(gr + 1) * C, :, bass.ds(c * C, C)],
                                 heads(ps[gr * C:(gr + 1) * C, 4 * gr + 1, :]))

            @block.vector
            def _(dve):
                dve.memset(UV[0:C, :, :], 0.0).then_inc(zeroed, 1)
                dve.memset(S[:], 0.0).then_inc(zeroed, 1)
                dve.wait_ge(zeroed, 2)
                with dve.Fori(0, CH // 2) as i:
                    for b in range(2):
                        c = i * 2 + b

                        def done(gr, ins):
                            ins.then_inc(dve_done[gr], 1)

                        def mask(m, rows=C, w=C):
                            return m.unsqueeze(1).to_broadcast([rows, NH, w])

                        for gr in range(2):
                            dve.wait_ge(pe_done[gr], c * PN + 1)
                            done(gr, dve.tensor_tensor(
                                G[:, gr, :, :], heads(ps[:, 4 * gr:4 * gr + 2, :].rearrange("p a n -> p (a n)"), P),
                                mask(g.mask_g[:], P, P), ALU.mult))
                        for gr in range(2):
                            dve.wait_ge(pe_done[gr], c * PN + 2)
                            for dst, m in ((L1, g.low16), (Lo32, g.low32), (Lo64, g.low64)):
                                done(gr, dve.tensor_tensor(dst[:, gr, :, :], heads(bank(gr, 2, C)), mask(m[:]), ALU.mult))
                        for gr in range(2):
                            dve.wait_ge(dve_done[gr], c * DN + 1)
                            done(gr, dve.tensor_tensor(N1[:, gr, :, :], G[0:C, gr, :, 0:C], mask(g.up16[:]), ALU.mult))
                        for gr in range(2):
                            dve.wait_ge(dve_done[gr], c * DN + 5)
                            done(gr, dve.tensor_tensor(X[:, gr, :, :], N1[:, gr, :, :], mask(g.ident[0:C, 0:C]), ALU.add))
                        for d, p, n in ((6, 9, 2), (7, 11, 3), (8, 12, 0), (9, 15, 3), (10, 18, 2)):
                            for gr in range(2):
                                dve.wait_ge(pe_done[gr], c * PN + p)
                                dve.wait_ge(dve_done[gr], c * DN + d)
                                done(gr, dve.tensor_tensor(X[:, gr, :, :], X[:, gr, :, :], heads(bank(gr, n, C)), ALU.add))
                        for gr in range(2):
                            dve.wait_ge(pe_done[gr], c * PN + 22)
                            qs = slice(gr * 4, gr * 4 + 4)
                            d = heads(bank(gr, 2), P)
                            dve.tensor_tensor(tmp[0:C, qs, :], S[0:C, qs, :], d[0:C, :, 0:C], ALU.add)
                            done(gr, dve.tensor_tensor(tmp[C:P, qs, :], S[C:P, qs, :], d[C:P, :, C:P], ALU.add))
                        for gr in range(2):
                            qs = slice(gr * 4, gr * 4 + 4)
                            dve.wait_ge(dve_done[gr], c * DN + 12)
                            done(gr, dve.tensor_tensor(
                                S[:, qs, :], tmp[:, qs, :],
                                g.chunk_decay[:, qs, bass.ds(c, 1)].to_broadcast([P, 4, C]), ALU.mult))
                        for gr in range(2):
                            dve.wait_ge(pe_done[1 - gr], c * PN + 22)
                            done(gr, dve.memset(UV[0:C, gr * 4:gr * 4 + 4, :], 0.0))
                dve.wait_ge(state_turned, 1)
                dve.tensor_copy(srow[:].rearrange("p (a q) n -> p a (q n)", a=2), ps[0:C, 0:2, :]).then_inc(state_copied, 1)

            @block.gpsimd
            def _(pool):
                pool.wait_ge(state_copied, 1)
                pool.dma_start(g.new_wkv_prompt.rearrange("h i j -> i h j"),
                               srow[:].rearrange("p q (a j) -> p (q a) j", a=2)).then_inc(state_out, 16)
                pool.wait_ge(state_out, 16)


def stage_rwkv_sample(nc, g):
    with ExitStack() as ctx:
        S = ctx.enter_context(nc.sbuf_tensor("d_S", [P, 2, NPAIR, C], F32))
        vecs = ctx.enter_context(nc.sbuf_tensor("d_vecs", [P, 2, 5, NPAIR, C], F32))
        t = ctx.enter_context(nc.sbuf_tensor("d_t", [P, 2, NPAIR, C], F32))
        sa = ctx.enter_context(nc.sbuf_tensor("d_sa", [P, NPAIR], F32))
        state_in = [new_sem(nc, g, f"d_state_in{i}") for i in range(2)]
        vecs_in = [new_sem(nc, g, f"d_vecs_in{i}") for i in range(2)]
        chain = new_sem(nc, g, "d_chain")
        state_ready = new_sem(nc, g, "d_state_ready")
        y_ready = new_sem(nc, g, "d_y_ready")
        stored = [new_sem(nc, g, f"d_stored{i}") for i in range(2)]
        STEPS = 7
        rows = g.samp_rows.rearrange("(f b) (q a j) -> f b a q j", b=NB, a=2, j=C)
        wkv_in = g.state_wkv.rearrange("b (q a) i j -> b a i q j", a=2)
        wkv_out = g.new_wkv_sample.rearrange("b (q a) i j -> b a i q j", a=2)
        with nc.Block() as block:
            @block.sync
            def _(sp):
                for b in range(NB):
                    s = b % 2
                    if b >= 2:
                        sp.wait_ge(y_ready, b - 1)
                        sp.wait_ge(stored[s], 32 * (b // 2))
                    for a in range(2):
                        sp.dma_start(S[a * C:(a + 1) * C, s, :, :], wkv_in[b, a]).then_inc(state_in[s], 16)

            @block.scalar
            def _(act):
                for b in range(NB):
                    s = b % 2
                    if b >= 2:
                        act.wait_ge(y_ready, b - 1)
                    for a in range(2):
                        for f in range(5):
                            act.dma_start(vecs[a * C:(a + 1) * C, s, f, :, :],
                                          rows[f, b, a].unsqueeze(0).to_broadcast([C, NPAIR, C])).then_inc(vecs_in[s], 16)

            @block.gpsimd
            def _(pool):
                for b in range(NB):
                    s = b % 2
                    pool.wait_ge(state_ready, b + 1)
                    for a in range(2):
                        pool.dma_start(wkv_out[b, a], S[a * C:(a + 1) * C, s, :, :]).then_inc(stored[s], 16)
                for s in range(2):
                    pool.wait_ge(stored[s], 16 * NB)

            @block.vector
            def _(dve):
                step = Chain(dve, chain)
                for b in range(NB):
                    s = b % 2
                    dve.wait_ge(state_in[s], 32 * (b // 2 + 1))
                    dve.wait_ge(vecs_in[s], 160 * (b // 2 + 1))
                    st = S[:, s, :, :]
                    w, nkk, kka, kf, r = (vecs[:, s, f, :, :] for f in range(5))
                    t0, t1 = t[:, 0, :, :], t[:, 1, :, :]
                    step(dve.tensor_tensor(t0, st, nkk, ALU.mult))
                    step(dve.tensor_reduce(sa[:], t0, AX_X, ALU.add))
                    dve.tensor_tensor(st, st, w, ALU.mult)
                    dve.tensor_tensor(t0, kka, sa[:].unsqueeze(2).to_broadcast([P, NPAIR, C]), ALU.mult)
                    step(dve.tensor_tensor(t1, kf, g.v_samp[:, :, b:b + 1].to_broadcast([P, NPAIR, C]), ALU.mult))
                    step(dve.tensor_tensor(t0, t0, t1, ALU.add))
                    dve.tensor_tensor(st, st, t0, ALU.add).then_inc(state_ready, 1)
                    dve.wait_ge(state_ready, b + 1)
                    step(dve.tensor_tensor(t1, st, r, ALU.mult))
                    dve.tensor_reduce(g.y_t[:, :, SEQ + b:SEQ + b + 1].rearrange("p q a -> p (q a)"), t1, AX_X,
                                      ALU.add).then_inc(y_ready, 1)
                    dve.wait_ge(y_ready, b + 1)


def stage_rwkv_post(nc, g):
    HC = TC // 2
    with ExitStack() as ctx:
        yc = ctx.enter_context(nc.sbuf_tensor("e_yc", [P, TC], F32))
        sq = ctx.enter_context(nc.sbuf_tensor("e_sq", [P, TC], F32))
        rs = ctx.enter_context(nc.sbuf_tensor("e_rs", [P, TC], F32))
        ob = ctx.enter_context(nc.sbuf_tensor("e_ob", [P, 2, TC], F32))
        vec = ctx.enter_context(nc.sbuf_tensor("e_vec", [P, 2, NPAIR], F32))
        ps = ctx.enter_context(nc.psum_tensor("e_ps", [P, 4, 512], F32))
        vec_in, mean_done, yc_ready = (new_sem(nc, g, "e_" + n) for n in ("vec_in", "mean_done", "yc_ready"))
        sq_ready, var_done, ve_ready, root_ready = (new_sem(nc, g, "e_" + n) for n in
                                                    ("sq_ready", "var_done", "ve_ready", "root_ready"))
        chain, out_ready = new_sem(nc, g, "e_chain"), new_sem(nc, g, "e_out_ready")
        stored = [new_sem(nc, g, f"e_stored{i}") for i in range(2)]
        with nc.Block() as block:
            @block.sync
            def _(sp):
                with nc.allow_non_contiguous_dma(reason="one value to a partition"):
                    for j, v in enumerate((g.lnx_w, g.lnx_b)):
                        sp.dma_start(vec[:, j, :], v.rearrange("(q p) -> p q", p=P)).then_inc(vec_in, 16)
                for q in range(NPAIR):
                    sp.wait_ge(out_ready, q + 1)
                    sp.dma_start(g.mix_t[q * P:(q + 1) * P, :], ob[:, q % 2, :]).then_inc(stored[q % 2], 16)
                for s in range(2):
                    sp.wait_ge(stored[s], 16 * NPAIR // 2)

            @block.tensor
            def _(pe):
                for q in range(NPAIR):
                    if q:
                        pe.wait_ge(yc_ready, 2 * q)
                    for h in range(2):
                        last = pe.matmul(ps[:, h, 0:HC], g.blk64[:], g.y_t[:, q, h * HC:(h + 1) * HC], start=True, stop=True)
                    last.then_inc(mean_done, 1)
                    pe.wait_ge(sq_ready, q + 1)
                    if q:
                        pe.wait_ge(ve_ready, 2 * q)
                    for h in range(2):
                        last = pe.matmul(ps[:, 2 + h, 0:HC], g.blk64[:], sq[:, h * HC:(h + 1) * HC], start=True, stop=True)
                    last.then_inc(var_done, 1)

            @block.scalar
            def _(act):
                for q in range(NPAIR):
                    act.wait_ge(yc_ready, 2 * q + 2)
                    act.activation(sq[:], yc[:], ACT.Square).then_inc(sq_ready, 1)
                    act.wait_ge(ve_ready, 2 * q + 2)
                    act.activation(rs[:], rs[:], ACT.Sqrt).then_inc(root_ready, 1)

            @block.vector
            def _(dve):
                step = Chain(dve, chain)
                dve.wait_ge(vec_in, 32)
                for q in range(NPAIR):
                    dve.wait_ge(mean_done, q + 1)
                    for h in range(2):
                        w = slice(h * HC, (h + 1) * HC)
                        dve.scalar_tensor_tensor(out=yc[:, w], in0=ps[:, h, 0:HC], scalar=-1.0 / C, in1=g.y_t[:, q, w],
                                                 op0=ALU.mult, op1=ALU.add).then_inc(yc_ready, 1)
                    dve.wait_ge(var_done, q + 1)
                    for h in range(2):
                        dve.tensor_scalar(rs[:, h * HC:(h + 1) * HC], ps[:, 2 + h, 0:HC], 1.0 / C, 64e-5, ALU.mult,
                                          ALU.add).then_inc(ve_ready, 1)
                    dve.wait_ge(root_ready, q + 1)
                    step(dve.reciprocal(rs[:], rs[:]))
                    step(dve.tensor_tensor(yc[:], yc[:], rs[:], ALU.mult))
                    step(dve.tensor_scalar(yc[:], yc[:], vec[:, 0, q:q + 1], vec[:, 1, q:q + 1], ALU.mult, ALU.add))
                    step(dve.tensor_tensor(yc[:], yc[:], g.bonus_t[:, q, :], ALU.add))
                    if q >= 2:
                        dve.wait_ge(stored[q % 2], 16 * (q // 2))
                    dve.tensor_tensor(ob[:, q % 2, :], yc[:], g.gate_t[:, q, :], ALU.mult).then_inc(out_ready, 1)
                    dve.wait_ge(out_ready, q + 1)


def stage_compress(nc, g):
    JP = 8
    with ExitStack() as ctx:
        def sb(name, shape, dt=F32):
            return ctx.enter_context(nc.sbuf_tensor("m_" + name, shape, dt))

        def sem(name):
            return new_sem(nc, g, "m_" + name)

        w1 = sb("w1", [P, 2, JP, P])
        pe_in = sb("pe_in", [P, 2, JP, 2])
        w2 = sb("w2", [C, 2, C])
        pt = sb("pt", [P, NB * 2], I32)
        ptf = sb("ptf", [P, NB * 2])
        row = sb("row", [P, 1], I32)
        rowf = sb("rowf", [P, 1])
        grp = sb("grp", [P, 1], I32)
        grpf = sb("grpf", [P, 1])
        idx = sb("idx", [P, NB * 2], I32)
        idc = sb("idc", [P, 2], I32)
        kv = sb("kv", [P, 2, 16, 512])
        kvr = sb("kvr", [P, 2, 4, 16, C])
        tb = sb("tb", [P, 4, 512])
        part = sb("part", [P, 2, 4, 256])
        pes = sb("pes", [P, 2, 2])
        bias = sb("bias", [C, 2])
        hs = sb("hs", [C, 2, 4, 256])
        ko = sb("ko", [P, 2, 31])
        vo = sb("vo", [31, 256])
        ps = ctx.enter_context(nc.psum_tensor("m_ps", [P, 8, 512], F32))
        w_in, pt_in, chain, idx_ready, idc_ready = (sem(n) for n in ("w_in", "pt_in", "chain", "idx_ready", "idc_ready"))
        loaded = [sem("loaded0"), sem("loaded1")]
        arranged = [sem("arranged_k"), sem("arranged_v")]
        turned, dve_ev, act_ev, mm_done, part_ev = (sem(n) for n in ("turned", "dve_ev", "act_ev", "mm_done", "part_ev"))
        shifted, hid_ready, fin_done, fin_ev = (sem(n) for n in ("shifted", "hid_ready", "fin_done", "fin_ev"))
        pe_summed, pe_copied, bias_summed, bias_ready = (sem(n) for n in ("pe_summed", "pe_copied", "bias_summed", "bias_ready"))
        prompt_in, prompt_ready, prompt_out, iota_ready = (sem(n) for n in ("prompt_in", "prompt_ready", "prompt_out", "iota_ready"))
        cache = g.cache_cmp.rearrange("n (c r) w -> (n c) (r w)", r=16)
        T, EV, PA, F2 = 32, 16, 4, 2

        with nc.Block() as block:
            @block.sync
            def _(sp):
                for e in range(2):
                    for s in range(2):
                        sp.dma_start(w1[:, e, :, s * C:(s + 1) * C],
                                     g.phi_w1[e, s * 1024:(s + 1) * 1024].rearrange("(q p) f -> p q f", p=P)).then_inc(w_in, 16)
                    sp.dma_start(w2[:, e, :], g.phi_w2[e]).then_inc(w_in, 16)
                with nc.allow_non_contiguous_dma(reason="small tables"):
                    for e in range(2):
                        for s in range(2):
                            sp.dma_start(pe_in[:, e, :, s],
                                         g.phi_pe[e, s * 16:(s + 1) * 16].rearrange("(q a) d -> (a d) q", a=2)).then_inc(w_in, 16)
                    by_page = g.page_table.rearrange("b (h n) -> n (b h)", h=2)
                    for n in range(16):
                        sp.dma_start(pt[8 * n:8 * n + 8, :], by_page[n:n + 1, :].to_broadcast([8, 16])).then_inc(pt_in, 16)
                for e in range(2):
                    sp.wait_ge(arranged[e], 2 * NB - 1)
                sp.dma_start(kv[0:32, 0, :, :], g.kv_rows[0:SEQ, 0:512].rearrange("(c j) w -> c j w", j=16)).then_inc(prompt_in, 16)
                sp.wait_ge(prompt_ready, 2)
                sp.dma_start(g.kc_prompt.rearrange("(q p) c -> p q c", p=P), ko[:]).then_inc(prompt_out, 16)
                sp.dma_start(g.vc_prompt, vo[:]).then_inc(prompt_out, 16)
                sp.wait_ge(prompt_out, 32)

            def arrange(eng, i, half, e, w):
                if w == P:
                    eng.wait_ge(loaded[half], i * 16 + 16)
                else:
                    eng.wait_ge(prompt_in, 16)
                eng.wait_ge(turned, i * T + max(0, 8 * (2 * half + e - 1)))
                take_wait(g, eng)
                eng.tensor_copy(kvr[0:w, e], kv[0:w, half, :, e * 256:e * 256 + 256].rearrange(
                    "p j (h d) -> p h j d", h=4)).then_inc(arranged[e], 1)

            def evac_even(dve, i, n, w):
                dve.wait_ge(turned, i * T + n + 1)
                dve.wait_ge(mm_done, i * T + max(0, n - 3))
                dve.tensor_copy(tb[:, n % 4, 0:4 * w], ps[:, n % 4, 0:4 * w]).then_inc(dve_ev, 1)

            @block.gpsimd
            def _(pool):
                pool.iota(row[:], pattern=[[0, 1]], base=0, channel_multiplier=1).then_inc(iota_ready, 1)
                pool.wait_ge(idx_ready, 1)

                def load(col, h, n):
                    pool.tensor_copy(idc[:, h:h + 1], idx[:, bass.ds(col, 1)]).then_inc(idc_ready, 1)
                    pool.wait_ge(idc_ready, n)
                    take_wait(g, pool)
                    pool.indirect_dma_start(
                        out=kv[:, h, :, :].rearrange("p j w -> p (j w)"), out_offset=None, in_=cache,
                        in_offset=bass.IndirectOffsetOnAxis(ap=idc[:, h:h + 1], axis=0)).then_inc(loaded[h], 16)
                for h in range(2):
                    load(h, h, h + 1)
                with pool.Fori(0, NB - 1) as i:
                    for h in range(2):
                        arrange(pool, i, h, 1, P)
                        for e in range(2):
                            pool.wait_ge(arranged[e], i * 2 + h + 1)
                        load(i * 2 + 2 + h, h, i * 2 + 3 + h)
                for h in range(2):
                    arrange(pool, NB - 1, h, 1, P)
                arrange(pool, NB, 0, 1, 32)

            @block.tensor
            def _(pe):
                pe.wait_ge(w_in, 16 * 10)
                for e in range(2):
                    for q in range(JP):
                        last = pe.matmul(ps[:, 4 + e, 0:2], w1[:, e, q, :], pe_in[:, e, q, :], start=(q == 0), stop=(q == JP - 1))
                    last.then_inc(pe_summed, 1)
                pe.wait_ge(pe_copied, 2)
                for e in range(2):
                    for s in range(2):
                        last = pe.matmul(ps[0:C, 6 + e, 0:1], g.ident[:, s * C:(s + 1) * C], pes[:, e, s:s + 1],
                                         start=(s == 0), stop=(s == 1))
                    last.then_inc(bias_summed, 1)
                pe.wait_ge(bias_ready, 2)

                def batch(i, halves, w):
                    units = 2 * halves

                    def turn(n):
                        u, q = n // JP, n % JP
                        half, e = u // 2, u % 2
                        if q == 0:
                            pe.wait_ge(arranged[e], i * 2 + half + 1)
                        if n < 2:
                            pe.wait_ge(fin_ev, i * F2)
                        if n % 2 == 0:
                            pe.wait_ge(dve_ev, i * EV + max(0, n // 2 - 1))
                        else:
                            pe.wait_ge(act_ev, i * EV + max(0, n // 2 - 1))
                        for h in range(4):
                            last = pe.transpose(ps[:, n % 4, h * w:(h + 1) * w],
                                                kvr[0:w, e, h, 2 * q:2 * q + 2, :].rearrange("p j d -> p (j d)"),
                                                g.ident[0:w, 0:w])
                        last.then_inc(turned, 1)

                    def mult(n):
                        u, q = n // JP, n % JP
                        e = u % 2
                        pe.wait_ge(dve_ev if n % 2 == 0 else act_ev, i * EV + n // 2 + 1)
                        if q == 0:
                            pe.wait_ge(part_ev, i * PA + max(0, u - 1))
                        pe.matmul(ps[:, 4 + u % 2, 0:4 * w], w1[:, e, q, :], tb[:, n % 4, 0:4 * w], start=(q == 0),
                                  stop=(q == JP - 1)).then_inc(mm_done, 1)

                    turn(0)
                    for n in range(1, JP * units):
                        turn(n)
                        mult(n - 1)
                    mult(JP * units - 1)
                    pe.wait_ge(part_ev, i * PA + units)
                    nc_ = w * halves - 1
                    for e in range(2):
                        pe.wait_ge(hid_ready, i * F2 + e)
                        take_wait(g, pe)
                        for hh in range(2):
                            for s in range(2):
                                last = pe.matmul(ps[0:C, 6 + hh, 0:2 * nc_], g.ident[:, s * C:(s + 1) * C],
                                                 part[:, e, 2 * hh:2 * hh + 2, s:s + nc_], start=(s == 0), stop=(s == 1))
                        last.then_inc(shifted, 1)
                    pe.wait_ge(hid_ready, i * F2 + 2)
                    take_wait(g, pe)
                    for h in range(4):
                        lo = (h % 2) * C
                        last = pe.matmul(ps[lo:lo + C, 0, (h // 2) * nc_:(h // 2 + 1) * nc_], w2[:, 0, :], hs[:, 0, h, 0:nc_],
                                         start=True, stop=True)
                    last.then_inc(fin_done, 1)
                    for t in range(halves):
                        m = min(w, nc_ - t * w)
                        for h in range(4):
                            last = pe.matmul(ps[0:m, 1, t * 256 + h * C:t * 256 + (h + 1) * C], hs[:, 1, h, t * w:t * w + m],
                                             w2[:, 1, :], start=True, stop=True)
                    last.then_inc(fin_done, 1)

                with pe.Fori(0, NB) as i:
                    batch(i, 2, P)
                batch(NB, 1, 32)

            @block.scalar
            def _(act):
                def batch(i, halves, w):
                    for n in range(1, JP * 2 * halves, 2):
                        act.wait_ge(turned, i * T + n + 1)
                        act.wait_ge(mm_done, i * T + max(0, n - 3))
                        act.copy(tb[:, n % 4, 0:4 * w], ps[:, n % 4, 0:4 * w]).then_inc(act_ev, 1)
                    nc_ = w * halves - 1
                    act.wait_ge(fin_done, i * F2)
                    for e in range(2):
                        act.wait_ge(shifted, i * F2 + e + 1)
                        for hh in range(2):
                            last = act.activation(hs[:, e, 2 * hh:2 * hh + 2, 0:nc_],
                                                  ps[0:C, 6 + hh, 0:2 * nc_].rearrange("p (h c) -> p h c", h=2),
                                                  ACT.Silu, bias=bias[:, e:e + 1])
                        last.then_inc(hid_ready, 1)
                act.wait_ge(bias_ready, 2)
                with act.Fori(0, NB) as i:
                    batch(i, 2, P)
                batch(NB, 1, 32)

            @block.vector
            def _(dve):
                step = Chain(dve, chain)
                dve.wait_ge(pt_in, 16 * 16)
                dve.wait_ge(iota_ready, 1)
                step(dve.tensor_scalar(grp[:], row[:], 7, None, ALU.bitwise_and))
                step(dve.tensor_copy(grpf[:], grp[:]))
                step(dve.tensor_copy(ptf[:], pt[:]))
                step(dve.tensor_scalar(ptf[:], ptf[:], 8.0, grpf[:, 0:1], ALU.mult, ALU.add))
                dve.tensor_copy(idx[:], ptf[:]).then_inc(idx_ready, 1)
                for e in range(2):
                    dve.wait_ge(pe_summed, e + 1)
                    dve.tensor_copy(pes[:, e, :], ps[:, 4 + e, 0:2]).then_inc(pe_copied, 1)
                for e in range(2):
                    dve.wait_ge(bias_summed, e + 1)
                    dve.tensor_copy(bias[:, e:e + 1], ps[0:C, 6 + e, 0:1]).then_inc(bias_ready, 1)

                def batch(i, halves, w, last):
                    dve.wait_ge(shifted, i * F2)
                    for u in range(2 * halves):
                        half, e = u // 2, u % 2
                        if u == 0:
                            arrange(dve, i, 0, 0, w)
                        for n in range(u * JP, (u + 1) * JP, 2):
                            evac_even(dve, i, n, w)
                        dve.wait_ge(mm_done, i * T + (u + 1) * JP)
                        dve.tensor_copy(part[:, e, :, half * P:half * P + w],
                                        ps[:, 4 + u % 2, 0:4 * w].rearrange("p (h c) -> p h c", h=4)).then_inc(part_ev, 1)
                        if u == 0 and halves == 2:
                            arrange(dve, i, 1, 0, w)
                    nc_ = w * halves - 1
                    dve.wait_ge(fin_done, i * F2 + 1)
                    keys = ps[:, 0, 0:2 * nc_].rearrange("p (h c) -> p h c", h=2)
                    if last:
                        dve.tensor_copy(ko[:], keys).then_inc(prompt_ready, 1)
                        dve.wait_ge(fin_done, i * F2 + 2)
                        dve.tensor_copy(vo[:], ps[0:31, 1, 0:256]).then_inc(prompt_ready, 1)
                    else:
                        dve.tensor_copy(g.kc[:, bass.ds(i * 2, 2), :], keys).then_inc(fin_ev, 1)
                        dve.wait_ge(fin_done, i * F2 + 2)
                        v = g.vc[:, bass.ds(i, 1), :].rearrange("p a n -> p (a n)")
                        dve.tensor_copy(v[:, 0:256], ps[:, 1, 0:256])
                        dve.tensor_copy(v[0:P - 1, 256:512], ps[0:P - 1, 1, 256:512]).then_inc(fin_ev, 1)

                with dve.Fori(0, NB) as i:
                    batch(i, 2, P, False)
                batch(NB, 1, 32, True)


def stage_nsa_sample(nc, g):
    PG = 32
    NQD = PG // 4
    NC = 255
    with ExitStack() as ctx:
        def sb(name, shape, dt=F32):
            return ctx.enter_context(nc.sbuf_tensor("b_" + name, shape, dt))

        def sem(name):
            return new_sem(nc, g, "b_" + name)

        qs = sb("qs", [P, 2, 4, NB])
        qz = sb("qz", [P, NB * 272])
        kvn = sb("kvn", [NB, 1536])
        knT = sb("knT", [P, 2, NB])
        gts = sb("gts", [P, 3])
        pages = sb("pages", [P, NB * PG], I32)
        pagef = sb("pagef", [P, NB * PG])
        prow = sb("prow", [P, 1], I32)
        prowf = sb("prowf", [P, 1])
        idx = [sb("idx_k", [P, NB * PG], I32), sb("idx_v", [P, NB * PG], I32)]
        idc = sb("idc", [P, 4, 4], I32)
        bsel = sb("bsel", [P, NB])
        zero = sb("zero", [P, P])
        pc = sb("pc", [P, 256])
        imp = sb("imp", [P, 260])
        score = sb("score", [P, 65])
        best = sb("best", [P, 8])
        off = sb("off", [P, 65])
        kbuf = sb("kbuf", [P, 4, 4, 256])
        kT = sb("kT", [P, 2, 2, 512])
        sl = sb("sl", [P, PG * P + 1])
        sw = sb("sw", [P, 512])
        pTs = sb("pTs", [P, PG, P])
        pTw = sb("pTw", [P, 4, P])
        pTc = sb("pTc", [P, 2, P])
        st = sb("st", [P, 3, 4])
        diag = sb("diag", [P, P])
        pn = sb("pn", [NB, P])
        os_ = sb("os", [P, 2, 4, NB])
        ps = ctx.enter_context(nc.psum_tensor("b_ps", [P, 8, 512], F32))
        in_done, made, chain, idx_ready, idc_ready, qz_ready = (sem(n) for n in (
            "in_done", "made", "chain", "idx_ready", "idc_ready", "qz_ready"))
        cmp_done, nmax_ready, exp_done, pc_ready, imp_done, off_ready = (sem(n) for n in (
            "cmp_done", "nmax_ready", "exp_done", "pc_ready", "imp_done", "off_ready"))
        kloaded = [sem(f"kloaded{s}") for s in range(4)]
        vloaded = [sem(f"vloaded{s}") for s in range(4)]
        kwin = [sem(f"kwin{s}") for s in range(4)]
        vwin = [sem(f"vwin{s}") for s in range(4)]
        kturned, kev_d, kev_a, kmm, score_ev, vmm = (sem(n) for n in ("kturned", "kev_d", "kev_a", "kmm", "score_ev", "vmm"))
        kn_turned, kn_copied, sn_done = sem("kn_turned"), sem("kn_copied"), sem("sn_done")
        p_ready, pt_turned, pt_copied, diag_ready, pn_done, pn_copied = (sem(n) for n in (
            "p_ready", "pt_turned", "pt_copied", "diag_ready", "pn_done", "pn_copied"))
        o_done, os_ready, out_done = sem("o_done"), sem("os_ready"), sem("out_done")
        cache = g.cache_slc.rearrange("n r (k w) -> (n r k) w", k=2)
        heads = g.proj_t[R_COLS:KV0, SEQ:TC].rearrange("(h a g d) b -> a d h g b", h=2, a=2, g=4)
        mix_heads = g.mix_t[D_R:D, SEQ:TC].rearrange("(h a g d) b -> a d h g b", h=2, a=2, g=4)
        NW = NQD * NB

        def window(eng, b, slot, loaded, kv):
            w = slice(kv * 256, kv * 256 + 256)
            eng.dma_start(kbuf[:, slot, 0:3, :], g.cache_win[b, 1:385, w].rearrange("(t p) n -> p t n", p=P)).then_inc(loaded, 16)
            eng.dma_start(kbuf[0:P - 1, slot, 3, :], g.cache_win[b, 385:512, w]).then_inc(loaded, 16)
            eng.dma_start(kbuf[P - 1:P, slot, 3, :], g.kv_rows[SEQ + b:SEQ + b + 1, 1024 + kv * 256:1280 + kv * 256]).then_inc(loaded, 16)

        with nc.Block() as block:
            @block.sync
            def _(sp):
                with nc.allow_non_contiguous_dma(reason="small tables"):
                    for a in range(2):
                        for h in range(2):
                            sp.dma_start(qs[a * C:(a + 1) * C, h, :, :], heads[a, :, h]).then_inc(in_done, 16)
                    for b in range(NB):
                        sp.dma_start(gts[16 * b:16 * b + 16, :], g.gates[SEQ + b].rearrange("(r m) -> m r", r=3)).then_inc(in_done, 16)
                    sp.dma_start(pages[:], g.page_table.rearrange("(o b) n -> o (b n)", o=1).to_broadcast([P, NB * PG])).then_inc(in_done, 16)
                    sp.dma_start(kvn[:], g.kv_rows[SEQ:TC, :]).then_inc(in_done, 16)
                for b in range(NB):
                    sp.wait_ge(kturned, 2 * (NW + b - 3))
                    window(sp, b, b % 4, kwin[b % 4], 0)
                for b in range(NB):
                    sp.wait_ge(vmm, NW + b - 3)
                    window(sp, b, b % 4, vwin[b % 4], 1)
                sp.wait_ge(os_ready, 2)
                for a in range(2):
                    for h in range(2):
                        sp.dma_start(mix_heads[a, :, h], os_[a * C:(a + 1) * C, h, :, :]).then_inc(out_done, 16)
                sp.wait_ge(out_done, 64)

            @block.gpsimd
            def _(pool):
                step = Chain(pool, made)
                step(pool.iota(prow[:], pattern=[[0, 1]], base=0, channel_multiplier=1))
                step(pool.memset(zero[:], 0.0))
                step(pool.memset(qz[:], 0.0))
                step(pool.memset(bsel[:], 1.0))
                step(pool.affine_select(out=bsel[:], in_=bsel[:], compare_op=ALU.is_ge, fill=0.0, base=0,
                                        pattern=[[-16, NB]], channel_multiplier=1))
                step(pool.affine_select(out=bsel[:], in_=bsel[:], compare_op=ALU.is_ge, fill=0.0, base=15,
                                        pattern=[[16, NB]], channel_multiplier=-1))
                step(pool.memset(imp[:], 0.0))
                pool.wait_ge(idx_ready, 2)

                def load(quad, b, kv, loaded):
                    s = b % 4
                    pool.tensor_copy(idc[:, s, :], idx[kv][:, bass.ds(quad * 4 + b * PG, 4)]).then_inc(idc_ready, 1)
                    pool.wait_ge(idc_ready, quad * NB + (kv * NW + b + 1))
                    take_wait(g, pool)
                    for n in range(4):
                        pool.indirect_dma_start(
                            out=kbuf[:, s, n, :], out_offset=None, in_=cache,
                            in_offset=bass.IndirectOffsetOnAxis(ap=idc[:, s, n:n + 1], axis=0)).then_inc(loaded[s], 16)

                def stream(kv, loaded, free, per, base):
                    for b in range(4):
                        load(0, b, kv, loaded)
                    with pool.Fori(0, NQD - 1) as i:
                        for b in range(NB):
                            pool.wait_ge(free, i * (NB * per) + (b + 1) * per)
                            load(i if b < 4 else i + 1, (b + 4) % NB, kv, loaded)
                    for b in range(4, NB):
                        pool.wait_ge(free, ((NQD - 1) * NB + b - 3) * per)
                        load(NQD - 1, b, kv, loaded)
                stream(0, kloaded, kturned, 2, 0)
                pool.wait_ge(kturned, 2 * (NW + NB))
                stream(1, vloaded, vmm, 1, 0)

            @block.tensor
            def _(pe):
                pe.wait_ge(qz_ready, 2)
                for b in range(NB):
                    for h in range(2):
                        last = pe.matmul(ps[:, 5, 0:NC], qz[:, b * 256 + h * P:b * 256 + (h + 1) * P], g.kc[:, 2 * b + h, :],
                                         start=(b + h == 0), stop=(b + h == NB))
                last.then_inc(cmp_done, 1)
                for h in range(2):
                    last = pe.transpose(ps[:, 7, h * NB:(h + 1) * NB], kvn[:, 512 + h * P:512 + (h + 1) * P], g.ident[0:NB, 0:NB])
                last.then_inc(kn_turned, 1)
                pe.wait_ge(kn_copied, 1)
                for b in range(NB):
                    for h in range(2):
                        last = pe.matmul(ps[:, 7, 0:1], qz[:, b * 256 + h * P:b * 256 + (h + 1) * P], knT[:, h, b:b + 1],
                                         start=(b + h == 0), stop=(b + h == NB))
                last.then_inc(sn_done, 1)
                pe.wait_ge(pc_ready, 1)
                pe.matmul(ps[:, 5, 0:NC], g.blk4[:], pc[:, 0:NC], start=True, stop=True).then_inc(imp_done, 1)

                def quad(i, loaded, uses):
                    def turn(b):
                        pe.wait_ge(loaded[b % 4], uses(b))
                        pe.wait_ge(kev_d, i * NB + max(0, b - 1))
                        pe.wait_ge(kev_a, i * NB + max(0, b - 1))
                        for h in range(2):
                            for n in range(4):
                                last = pe.transpose(ps[:, 2 * (b % 2) + h, n * P:(n + 1) * P],
                                                    kbuf[:, b % 4, n, h * P:(h + 1) * P], g.ident[:])
                            last.then_inc(kturned, 1)

                    def mult(b):
                        pe.wait_ge(kev_d, i * NB + b + 1)
                        pe.wait_ge(kev_a, i * NB + b + 1)
                        if b == 0:
                            pe.wait_ge(score_ev, i)
                        for h in range(2):
                            last = pe.matmul(ps[:, 4, :], qz[:, b * 256 + h * P:b * 256 + (h + 1) * P], kT[:, b % 2, h, :],
                                             start=(b + h == 0), stop=(b + h == NB))
                        last.then_inc(kmm, 1)
                    turn(0)
                    for b in range(1, NB):
                        turn(b)
                        mult(b - 1)
                    mult(NB - 1)

                with pe.Fori(0, NQD) as i:
                    quad(i, kloaded, lambda b: i * 128 + 64 * (b // 4 + 1))
                quad(NQD, kwin, lambda b: 48 * (b // 4 + 1))
                pe.wait_ge(score_ev, NQD + 1)
                pe.wait_ge(p_ready, 1)
                pe.transpose(ps[:, 0, 0:P], pc[:, 0:P], g.ident[:])
                pe.transpose(ps[0:P - 1, 0, P:2 * P], pc[:, P:NC], g.ident[:]).then_inc(pt_turned, 1)
                pe.wait_ge(p_ready, 2)
                for n in range(4):
                    last = pe.transpose(ps[:, 1, n * P:(n + 1) * P], sw[:, n * P:(n + 1) * P], g.ident[:])
                last.then_inc(pt_turned, 1)
                pe.wait_ge(p_ready, 3)
                for q in range(NQD):
                    if q >= 2:
                        pe.wait_ge(pt_copied, q + 1)
                    for n in range(4):
                        last = pe.transpose(ps[:, 2 + q % 2, n * P:(n + 1) * P], sl[:, (4 * q + n) * P:(4 * q + n + 1) * P], g.ident[:])
                    last.then_inc(pt_turned, 1)
                pe.wait_ge(diag_ready, 1)
                pe.matmul(ps[0:NB, 5, 0:P], bsel[:], diag[:], start=True, stop=True).then_inc(pn_done, 1)
                out = ps[:, 6, 0:P]
                pe.matmul(out, zero[:], g.ident[:], start=True, stop=False, skip_group_check=True)
                pe.wait_ge(pn_copied, 1)
                for h in range(2):
                    pe.matmul(out.rearrange("p (b h m) -> p b h m", b=NB, h=2)[:, :, h, :], kvn[:, 768 + h * P:768 + (h + 1) * P],
                              pn[:].rearrange("p (b h m) -> p b h m", b=NB, h=2)[:, :, h, :], start=False, stop=False,
                              skip_group_check=True)
                pe.wait_ge(pt_copied, NQD + 2)
                for b in range(NB):
                    for t in range(2):
                        m = P - t
                        for h in range(2):
                            cols = slice(b * 16 + h * 8, b * 16 + h * 8 + 8)
                            pe.matmul(out[:, cols], g.vc[0:m, b, t * 256 + h * P:t * 256 + (h + 1) * P], pTc[0:m, t, cols],
                                      start=False, stop=False, skip_group_check=True)

                def values(loaded, uses, probs):
                    for b in range(NB):
                        pe.wait_ge(loaded[b % 4], uses(b))
                        for n in range(4):
                            for h in range(2):
                                cols = slice(b * 16 + h * 8, b * 16 + h * 8 + 8)
                                last = pe.matmul(out[:, cols], kbuf[:, b % 4, n, h * P:(h + 1) * P], probs(n)[:, cols],
                                                 start=False, stop=False, skip_group_check=True)
                        last.then_inc(vmm, 1)
                    return last

                with pe.Fori(0, NQD) as i:
                    values(vloaded, lambda b: i * 128 + 64 * (b // 4 + 1),
                           lambda n: pTs[:, bass.ds(i * 4 + n, 1), :].rearrange("p a m -> p (a m)"))
                values(vwin, lambda b: 48 * (b // 4 + 1), lambda n: pTw[:, n, :])

            @block.scalar
            def _(act):
                act.wait_ge(nmax_ready, 1)
                act.activation(pc[:, 0:NC], ps[:, 5, 0:NC], ACT.Exp, bias=st[:, 0, 1:2], accum_out=st[:, 0, 2:3]).then_inc(exp_done, 1)
                with act.Fori(0, NQD + 1) as i:
                    for b in range(NB):
                        act.wait_ge(kturned, i * 16 + 2 * b + 2)
                        act.wait_ge(kmm, i * NB + max(0, b - 1))
                        act.copy(kT[:, b % 2, 1, :], ps[:, 2 * (b % 2) + 1, :]).then_inc(kev_a, 1)
                act.wait_ge(nmax_ready, 2)
                act.activation(sw[:], sw[:], ACT.Exp, bias=st[:, 2, 1:2], accum_out=st[:, 2, 2:3]).then_inc(exp_done, 1)
                act.wait_ge(nmax_ready, 3)
                act.activation(sl[:], sl[:], ACT.Exp, bias=st[:, 1, 1:2], accum_out=st[:, 1, 2:3]).then_inc(exp_done, 1)

            @block.vector
            def _(dve):
                step = Chain(dve, chain)
                dve.wait_ge(in_done, 16 * 14)
                dve.wait_ge(made, 7)
                step(dve.tensor_copy(prowf[:], prow[:]))
                step(dve.tensor_scalar(prowf[:], prowf[:], 2.0, None, ALU.mult))
                step(dve.tensor_copy(pagef[:], pages[:]))
                step(dve.tensor_scalar(pagef[:], pagef[:], 256.0, prowf[:, 0:1], ALU.mult, ALU.add))
                dve.tensor_copy(idx[0][:], pagef[:]).then_inc(idx_ready, 1)
                dve.tensor_scalar(idx[1][:], pagef[:], 1.0, None, ALU.add).then_inc(idx_ready, 1)
                for a in range(2):
                    dst = qz[a * C:(a + 1) * C, :].rearrange("p (b h y) -> p b h y", b=NB, h=2)[:, :, :, 4 * a:4 * a + 4]
                    dve.tensor_scalar(dst, qs[a * C:(a + 1) * C].rearrange("p h g b -> p b h g"), 0.125, None,
                                      ALU.mult).then_inc(qz_ready, 1)

                def negmax(br, scores):
                    step(dve.reduce_max(st[:, br, 0:1], scores, AX_X))
                    dve.tensor_scalar(st[:, br, 1:2], st[:, br, 0:1], -1.0, None, ALU.mult).then_inc(nmax_ready, 1)

                def factor(br):
                    step(dve.tensor_scalar(st[:, br, 3:4], st[:, br, 2:3], 1e-30, None, ALU.max))
                    step(dve.reciprocal(st[:, br, 3:4], st[:, br, 3:4]))

                dve.wait_ge(cmp_done, 1)
                negmax(0, ps[:, 5, 0:NC])
                dve.wait_ge(kn_turned, 1)
                dve.tensor_copy(knT[:].rearrange("p h b -> p (h b)"), ps[:, 7, 0:2 * NB]).then_inc(kn_copied, 1)
                dve.wait_ge(exp_done, 1)
                factor(0)
                dve.tensor_scalar(pc[:, 0:NC], pc[:, 0:NC], st[:, 0, 3:4], None, ALU.mult).then_inc(pc_ready, 1)
                dve.wait_ge(imp_done, 1)
                step(dve.tensor_copy(imp[:, 1:NC + 1], ps[:, 5, 0:NC]))
                taps = [imp[:, n:n + 256].rearrange("p (s f) -> p s f", f=4)[:, :, 0] for n in range(5)]
                step(dve.tensor_tensor(score[:, 0:64], taps[0], taps[1], ALU.add))
                for n in range(2, 5):
                    step(dve.tensor_tensor(score[:, 0:64], score[:, 0:64], taps[n], ALU.add))
                step(dve.memset(score[:, 0:1], -NEG))
                step(dve.memset(score[:, 63:65], -NEG))
                for n in range(2):
                    step(dve.max(best[:], score[:]))
                    step(dve.match_replace(score[:], best[:], score[:], -1.0))
                dve.tensor_scalar(off[:], score[:], 0.0, NEG, ALU.is_ge, ALU.mult).then_inc(off_ready, 1)
                dve.tensor_scalar(pc[:, 0:NC], pc[:, 0:NC], gts[:, 0:1], None, ALU.mult).then_inc(p_ready, 1)
                dve.wait_ge(off_ready, 1)
                dve.wait_ge(sn_done, 1)
                step(dve.tensor_copy(sl[:, PG * P:PG * P + 1], ps[:, 7, 0:1]))

                def evac(i):
                    for b in range(NB):
                        dve.wait_ge(kturned, i * 16 + 2 * b + 1)
                        dve.wait_ge(kmm, i * NB + max(0, b - 1))
                        dve.tensor_copy(kT[:, b % 2, 0, :], ps[:, 2 * (b % 2), :]).then_inc(kev_d, 1)
                    dve.wait_ge(kmm, i * NB + NB)
                with dve.Fori(0, NQD) as i:
                    evac(i)
                    dve.tensor_tensor(sl[:, bass.ds(i * 512, 512)].rearrange("p (s r) -> p s r", r=64),
                                      ps[:, 4, :].rearrange("p (s r) -> p s r", r=64),
                                      off[:, bass.ds(i * 8, 8)].unsqueeze(2).to_broadcast([P, 8, 64]),
                                      ALU.add).then_inc(score_ev, 1)
                evac(NQD)
                dve.tensor_copy(sw[:], ps[:, 4, :]).then_inc(score_ev, 1)
                dve.wait_ge(score_ev, NQD + 1)
                negmax(2, sw[:])
                negmax(1, sl[:])
                for n, (br, t) in enumerate(((2, sw), (1, sl))):
                    dve.wait_ge(exp_done, n + 2)
                    factor(br)
                    step(dve.tensor_tensor(st[:, br, 3:4], st[:, br, 3:4], gts[:, br:br + 1], ALU.mult))
                    dve.tensor_scalar(t[:], t[:], st[:, br, 3:4], None, ALU.mult).then_inc(p_ready, 1)
                dve.wait_ge(p_ready, 3)
                dve.tensor_scalar(diag[:], g.ident[:], sl[:, PG * P:PG * P + 1], None, ALU.mult).then_inc(diag_ready, 1)
                dve.wait_ge(pt_turned, 1)
                dve.tensor_copy(pTc[:, 0, :], ps[:, 0, 0:P])
                dve.tensor_copy(pTc[0:P - 1, 1, :], ps[0:P - 1, 0, P:2 * P]).then_inc(pt_copied, 1)
                dve.wait_ge(pt_turned, 2)
                dve.tensor_copy(pTw[:].rearrange("p n m -> p (n m)"), ps[:, 1, :]).then_inc(pt_copied, 1)
                for q in range(NQD):
                    dve.wait_ge(pt_turned, q + 3)
                    dve.tensor_copy(pTs[:, 4 * q:4 * q + 4, :].rearrange("p n m -> p (n m)"), ps[:, 2 + q % 2, :]).then_inc(pt_copied, 1)
                dve.wait_ge(pn_done, 1)
                dve.tensor_copy(pn[:], ps[0:NB, 5, 0:P]).then_inc(pn_copied, 1)
                dve.wait_ge(vmm, NW + NB)
                for a in range(2):
                    src = ps[a * C:(a + 1) * C, 6, 0:P].rearrange("p (b h a g) -> p a h g b", b=NB, h=2, a=2)[:, a]
                    dve.tensor_copy(os_[a * C:(a + 1) * C], src).then_inc(os_ready, 1)


def stage_nsa_prompt(nc, g):
    NQ = SEQ // P
    NC = SEQ // 16 - 1
    units = [(t, br, q) for t in range(NQ) for br in range(3) for q in range(4)]
    NU = len(units)
    SCALE = 0.125
    with ExitStack() as ctx:
        def sb(name, shape):
            return ctx.enter_context(nc.sbuf_tensor("a_" + name, shape, F32))

        def sem(name):
            return new_sem(nc, g, "a_" + name)

        qT = sb("qT", [C, 4, SEQ])
        rows = sb("rows", [P, NQ, 4, C])
        kT = sb("kT", [C, 2, SEQ])
        kcT = sb("kcT", [C, NC])
        vc = sb("vc", [NC, C])
        gates = sb("gates", [P, NQ, 48])
        causal = sb("causal", [P, P])
        cmask = sb("cmask", [P, NQ, NC])
        pr = sb("pr", [P, 3, SEQ])
        pT = sb("pT", [P, 3, SEQ])
        mx = sb("mx", [P, NU])
        nm = sb("nm", [P, NU])
        sums = sb("sums", [P, NU])
        fac = sb("fac", [P, NU])
        acc = sb("acc", [P, NQ, 4, C])
        tmp = sb("tmp", [P, 4, C])
        mo = sb("mo", [P, 2, SEQ])
        ps = ctx.enter_context(nc.psum_tensor("a_ps", [P, 8, 512], F32))
        gates_in, masks_ready, mask_step, head_in, k_turned, k_copied = (sem(n) for n in (
            "gates_in", "masks_ready", "mask_step", "head_in", "k_turned", "k_copied"))
        s_done, max_done, nm_done, e_done, t_done, ptd, pta, o_done = (sem(n) for n in (
            "s_done", "max_done", "nm_done", "e_done", "t_done", "pt_dve", "pt_act", "o_done"))
        chain, comb_done, mix_turned, mix_copied, stored = (sem(n) for n in (
            "chain", "comb_done", "mix_turned", "mix_copied", "stored"))
        fac_done, tmp_done = sem("fac_done"), sem("tmp_done")
        GR = NU // 4
        CH = 2 * GR

        def width(t, br):
            return NC if br == 0 else (t + 1) * P

        def blocks(t, br):
            return [(0, NC)] if br == 0 else [(j * P, P) for j in range(t + 1)]

        with nc.Block() as block:
            @block.sync
            def _(sp):
                sp.dma_start(gates[:], g.gates[0:SEQ].rearrange("(t p) n -> p t n", p=P)).then_inc(gates_in, 16)
                with sp.Fori(0, 4) as i:
                    sp.wait_ge(o_done, i * NU)
                    for q in range(4):
                        sp.dma_start(qT[:, q, :], g.proj_t[bass.ds(i * 256 + R_COLS + q * C, C), 0:SEQ]).then_inc(head_in, 16)
                    for j in range(4):
                        sp.dma_start(rows[:, :, j, :], g.kv_rows[0:SEQ, bass.ds(i * C + 512 + j * 256, C)].rearrange(
                            "(t p) d -> p t d", p=P)).then_inc(head_in, 16)
                    sp.dma_start(kcT[:], g.kc_prompt[bass.ds(i * C, C), :]).then_inc(head_in, 16)
                    sp.dma_start(vc[:], g.vc_prompt[:, bass.ds(i * C, C)]).then_inc(head_in, 16)

            @block.gpsimd
            def _(pool):
                step = Chain(pool, mask_step)
                step(pool.memset(causal[:], 0.0))
                step(pool.memset(cmask[:], 0.0))
                step(pool.affine_select(out=causal[:], in_=causal[:], compare_op=ALU.is_ge, fill=NEG, base=0,
                                        pattern=[[-1, P]], channel_multiplier=1))
                pool.affine_select(out=cmask[:], in_=cmask[:], compare_op=ALU.is_ge, fill=NEG, base=-31,
                                   pattern=[[P, NQ], [-16, NC]], channel_multiplier=1).then_inc(masks_ready, 1)
                with pool.Fori(0, 4) as i:
                    pool.wait_ge(mix_copied, i * 2 + 2)
                    pool.dma_start(g.mix_t[bass.ds(i * 256 + D_R, 256), 0:SEQ].rearrange("(a p) t -> p a t", p=P),
                                   mo[:]).then_inc(stored, 16)
                for c, dst in enumerate((g.new_cmp_prompt, g.new_slc_prompt, g.new_win_prompt)):
                    pool.dma_start(dst, g.kv_rows[0:SEQ, c * 512:(c + 1) * 512]).then_inc(stored, 16)
                for c, dst in enumerate((g.new_cmp_sample, g.new_slc_sample)):
                    pool.dma_start(dst, g.kv_rows[SEQ:TC, c * 512:(c + 1) * 512]).then_inc(stored, 16)
                pool.dma_start(g.new_win_sample[:, SEQ - 1, :], g.kv_rows[SEQ:TC, 1024:1536]).then_inc(stored, 16)
                pool.dma_start(g.new_win_sample[:, 0:SEQ - 1, :], g.cache_win[:, 1:SEQ, :]).then_inc(stored, 16)
                pool.wait_ge(stored, 16 * 11)

            @block.tensor
            def _(pe):
                pe.wait_ge(masks_ready, 1)
                with pe.Fori(0, 4) as i:
                    pe.wait_ge(head_in, i * 160 + 160)
                    pe.wait_ge(mix_copied, i * 2)
                    for j in range(2):
                        pe.wait_ge(k_copied, i * 2 + j)
                        take_wait(g, pe)
                        for t in range(NQ):
                            last = pe.transpose(ps[0:C, 7, t * P:(t + 1) * P], rows[:, t, 2 * j, :], g.ident[:])
                        last.then_inc(k_turned, 1)

                    def scores(u):
                        t, br, q = units[u]
                        if u == 0:
                            pe.wait_ge(k_copied, i * 2 + 2)
                        pe.wait_ge(e_done, i * NU + max(0, u - 2))
                        out = ps[:, u % 3, 0:width(t, br)]
                        query = qT[:, q, t * P:(t + 1) * P]
                        if br == 0:
                            pe.matmul(out, query, kcT[:], start=True, stop=False)
                            last = pe.matmul(out, g.ident[:], cmask[:, t, :], start=False, stop=True)
                        else:
                            own = slice(t * P, (t + 1) * P)
                            if t:
                                pe.matmul(out[:, 0:t * P], query, kT[:, br - 1, 0:t * P], start=True, stop=True)
                            pe.matmul(out[:, own], query, kT[:, br - 1, own], start=True, stop=False)
                            last = pe.matmul(out[:, own], g.ident[:], causal[:], start=False, stop=True)
                        last.then_inc(s_done, 1)

                    def turn(u):
                        t, br, q = units[u]
                        pe.wait_ge(e_done, i * NU + u + 1)
                        pe.wait_ge(ptd if u % 2 == 0 else pta, i * (NU // 2) + max(0, u // 2))
                        for a, w in blocks(t, br):
                            last = pe.transpose(ps[0:w, 3 + u % 2, a:a + P], pr[:, u % 3, a:a + w], g.ident[:])
                        last.then_inc(t_done, 1)

                    def out(u):
                        t, br, q = units[u]
                        gr = u // 4
                        pe.wait_ge(ptd if u % 2 == 0 else pta, i * (NU // 2) + u // 2 + 1)
                        if q == 0:
                            pe.wait_ge(comb_done, i * GR + max(0, gr - 1))
                        bl = blocks(t, br)
                        for n, (a, w) in enumerate(bl):
                            v = vc[:] if br == 0 else rows[:, a // P, 2 * br - 1, :]
                            last = pe.matmul(ps[:, 5 + gr % 2, q * C:(q + 1) * C], pT[0:w, u % 3, a:a + P], v,
                                             start=(n == 0), stop=(n == len(bl) - 1))
                        last.then_inc(o_done, 1)

                    for n in range(NU + 3):
                        if n < NU:
                            scores(n)
                        if 0 <= n - 2 < NU:
                            turn(n - 2)
                        if 0 <= n - 3 < NU:
                            out(n - 3)
                    pe.wait_ge(comb_done, i * GR + GR)
                    for a in range(2):
                        pe.wait_ge(mix_copied, i * 2 + a)
                        for t in range(NQ):
                            last = pe.transpose(ps[:, 7, t * P:(t + 1) * P],
                                                acc[:, t, 2 * a:2 * a + 2, :].rearrange("p q d -> p (q d)"), g.ident[:])
                        last.then_inc(mix_turned, 1)

            @block.scalar
            def _(act):
                with act.Fori(0, 4) as i:
                    for n in range(NU + 2):
                        if n < NU:
                            t, br, q = units[n]
                            w = width(t, br)
                            act.wait_ge(nm_done, i * NU + n + 1)
                            act.wait_ge(t_done, i * NU + max(0, n - 2))
                            if n == 0:
                                act.wait_ge(comb_done, i * GR)
                            act.activation(pr[:, n % 3, 0:w], ps[:, n % 3, 0:w], ACT.Exp, bias=nm[:, n:n + 1], scale=SCALE,
                                           accum_out=sums[:, n:n + 1]).then_inc(e_done, 1)
                        u = n - 2
                        if u >= 0 and u % 2 == 1:
                            t, br, q = units[u]
                            act.wait_ge(t_done, i * NU + u + 1)
                            act.wait_ge(o_done, i * NU + max(0, u - 2))
                            w = NC if br == 0 else P
                            act.copy(pT[0:w, u % 3, 0:(P if br == 0 else width(t, br))],
                                     ps[0:w, 3 + u % 2, 0:(P if br == 0 else width(t, br))]).then_inc(pta, 1)

            @block.vector
            def _(dve):
                dve.wait_ge(gates_in, 16)
                with dve.Fori(0, 4) as i:
                    step = Chain(dve, chain, i * CH)
                    for j in range(2):
                        dve.wait_ge(k_turned, i * 2 + j + 1)
                        dve.tensor_copy(kT[:, j, :], ps[0:C, 7, :]).then_inc(k_copied, 1)
                    for n in range(NU + 4):
                        if n < NU:
                            t, br, q = units[n]
                            dve.wait_ge(s_done, i * NU + n + 1)
                            dve.reduce_max(mx[:, n:n + 1], ps[:, n % 3, 0:width(t, br)], AX_X).then_inc(max_done, 1)
                            dve.wait_ge(max_done, i * NU + n + 1)
                            dve.tensor_scalar(nm[:, n:n + 1], mx[:, n:n + 1], 0.1 * NEG, -SCALE, ALU.max,
                                              ALU.mult).then_inc(nm_done, 1)
                        u = n - 2
                        if 0 <= u < NU and u % 2 == 0:
                            t, br, q = units[u]
                            dve.wait_ge(t_done, i * NU + u + 1)
                            dve.wait_ge(o_done, i * NU + max(0, u - 2))
                            w = NC if br == 0 else P
                            dve.tensor_copy(pT[0:w, u % 3, 0:(P if br == 0 else width(t, br))],
                                            ps[0:w, 3 + u % 2, 0:(P if br == 0 else width(t, br))]).then_inc(ptd, 1)
                        u = n - 4
                        if u >= 0 and u % 4 == 3:
                            t, br, q = units[u]
                            us = slice(u - 3, u + 1)
                            dve.wait_ge(e_done, i * NU + u + 1)
                            step(dve.tensor_scalar(fac[:, us], sums[:, us], 1e-30, None, ALU.max))
                            step(dve.reciprocal(fac[:, us], fac[:, us]))
                            dve.tensor_tensor(fac[:, us], fac[:, us], gates[:, t, bass.ds(i * 4 + br * 16, 4)],
                                              ALU.mult).then_inc(fac_done, 1)
                            dve.wait_ge(fac_done, i * GR + u // 4 + 1)
                            dve.wait_ge(o_done, i * NU + u + 1)
                            if u == 3:
                                dve.wait_ge(mix_turned, i * 2)
                            ob = ps[:, 5 + (u // 4) % 2, 0:4 * C].rearrange("p (q d) -> p q d", q=4)
                            fb = fac[:, us].unsqueeze(2).to_broadcast([P, 4, C])
                            if br == 0:
                                dve.tensor_tensor(acc[:, t, :, :], ob, fb, ALU.mult).then_inc(comb_done, 1)
                            else:
                                dve.tensor_tensor(tmp[:], ob, fb, ALU.mult).then_inc(tmp_done, 1)
                                dve.wait_ge(tmp_done, i * (GR - NQ) + 2 * t + br)
                                dve.tensor_tensor(acc[:, t, :, :], acc[:, t, :, :], tmp[:], ALU.add).then_inc(comb_done, 1)
                            dve.wait_ge(comb_done, i * GR + u // 4 + 1)
                    assert step.n == CH
                    for a in range(2):
                        dve.wait_ge(mix_turned, i * 2 + a + 1)
                        dve.wait_ge(stored, i * 16)
                        dve.tensor_copy(mo[:, a, :], ps[:, 7, :]).then_inc(mix_copied, 1)


def stage_turn_x(nc, g):
    with ExitStack() as ctx:
        rows = ctx.enter_context(nc.sbuf_tensor("t_rows", [P, 2, D], F32))
        ps = ctx.enter_context(nc.psum_tensor("t_ps", [P, 4, 512], F32))
        loaded = [new_sem(nc, g, f"t_loaded{i}") for i in range(2)]
        turned = new_sem(nc, g, "t_turned")
        copied = new_sem(nc, g, "t_copied")
        srcs = [g.x_prompt[r:r + n, :] for r, n in ROW_TILES[:4]] + [g.x_sample]
        with nc.Block() as block:
            @block.sync
            def _(sp):
                for i, (r, n) in enumerate(ROW_TILES):
                    if i >= 2:
                        sp.wait_ge(turned, 4 * (i - 1))
                    sp.dma_start(rows[0:n, i % 2, :], srcs[i]).then_inc(loaded[i % 2], 16)

            @block.tensor
            def _(pe):
                for i, (r, n) in enumerate(ROW_TILES):
                    pe.wait_ge(loaded[i % 2], 16 * (i // 2 + 1))
                    for q in range(4):
                        if i >= 1:
                            pe.wait_ge(copied, 4 * (i - 1) + q + 1)
                        for k in range(4):
                            last = pe.transpose(ps[:, q, k * P:k * P + n],
                                                rows[0:n, i % 2, (4 * q + k) * P:(4 * q + k + 1) * P],
                                                g.ident[0:n, 0:n])
                        last.then_inc(turned, 1)

            @block.vector
            def _(dve):
                for i, (r, n) in enumerate(ROW_TILES):
                    for q in range(4):
                        dve.wait_ge(turned, 4 * i + q + 1)
                        dve.tensor_copy(g.xt[:, 4 * q:4 * q + 4, r:r + n],
                                        ps[:, q, :].rearrange("p (k t) -> p k t", k=4)[:, :, 0:n]).then_inc(copied, 1)


def stage_out_proj(nc, g):
    HC = TC // 2
    with ExitStack() as ctx:
        wbuf = ctx.enter_context(nc.sbuf_tensor("o_w", [P, 2, KT, 256], F32))
        mx = ctx.enter_context(nc.sbuf_tensor("o_mix", [P, KT, TC], F32))
        sq = ctx.enter_context(nc.sbuf_tensor("o_sq", [P, 2, TC], F32))
        rstd = ctx.enter_context(nc.sbuf_tensor("o_rstd", [P, 3, TC], F32))
        gain = ctx.enter_context(nc.sbuf_tensor("o_gain", [P, KT], F32))
        ps = ctx.enter_context(nc.psum_tensor("o_ps", [P, 8, 512], F32))
        loaded = [new_sem(nc, g, f"o_loaded{i}") for i in range(2)]
        mix_in = new_sem(nc, g, "o_mix_in")
        gain_in = new_sem(nc, g, "o_gain_in")
        summed = [new_sem(nc, g, f"o_summed{i}") for i in range(4)]
        added = [new_sem(nc, g, f"o_added{i}") for i in range(4)]
        squared = new_sem(nc, g, "o_squared")
        sums_ready = new_sem(nc, g, "o_sums_ready")
        sum_step = new_sem(nc, g, "o_sum_step")
        ms_ready = new_sem(nc, g, "o_ms_ready")
        root_ready = new_sem(nc, g, "o_root_ready")
        rstd_ready = new_sem(nc, g, "o_rstd_ready")
        w_view = g.w_o.rearrange("(k p) n -> p k n", p=P)
        pairs = D // 512
        with nc.Block() as block:
            @block.sync
            def _(sp):
                with sp.Fori(0, pairs) as i:
                    for b in range(2):
                        sp.wait_ge(summed[2 * b + 1], i)
                        sp.dma_start(wbuf[:, b, :, :], w_view[:, :, bass.ds(i * 512 + b * 256, 256)]).then_inc(loaded[b], 16)

            @block.gpsimd
            def _(pool):
                pool.dma_start(mx[:], g.mix_t.rearrange("(k p) t -> p k t", p=P)).then_inc(mix_in, 16)
                with nc.allow_non_contiguous_dma(reason="one value to a partition"):
                    pool.dma_start(gain[:], g.g_ffn.rearrange("(k p) -> p k", p=P)).then_inc(gain_in, 16)

            @block.tensor
            def _(pe):
                pe.wait_ge(mix_in, 16)
                with pe.Fori(0, pairs) as i:
                    for b in range(2):
                        pe.wait_ge(loaded[b], i * 16 + 16)
                        for m in range(2):
                            s = 2 * b + m
                            pe.wait_ge(added[s], i * 2)
                            for k in range(KT):
                                for h in range(2):
                                    last = pe.matmul(ps[:, 2 * s + h, 0:HC], wbuf[:, b, k, m * P:(m + 1) * P],
                                                     mx[:, k, h * HC:(h + 1) * HC], start=(k == 0), stop=(k == KT - 1))
                            last.then_inc(summed[s], 1)
                for s in range(4):
                    pe.wait_ge(added[s], 2 * pairs)
                for k in range(KT):
                    pe.wait_ge(squared, k + 1)
                    for h in range(2):
                        last = pe.matmul(ps[:, h, 0:HC], g.ones[:], sq[:, k % 2, h * HC:(h + 1) * HC],
                                         start=(k == 0), stop=(k == KT - 1))
                    last.then_inc(sum_step, 1)

            @block.vector
            def _(dve):
                with dve.Fori(0, pairs) as i:
                    for s in range(4):
                        dve.wait_ge(summed[s], i + 1)
                        for h in range(2):
                            x = g.xt[:, bass.ds(i * 4 + s, 1), h * HC:(h + 1) * HC].rearrange("p a t -> p (a t)")
                            dve.tensor_tensor(x, x, ps[:, 2 * s + h, 0:HC], ALU.add).then_inc(added[s], 1)
                dve.wait_ge(sum_step, KT)
                dve.tensor_scalar(rstd[:, 0, 0:HC], ps[:, 0, 0:HC], 1.0 / D, EPS, ALU.mult, ALU.add).then_inc(ms_ready, 1)
                dve.tensor_scalar(rstd[:, 0, HC:TC], ps[:, 1, 0:HC], 1.0 / D, EPS, ALU.mult, ALU.add).then_inc(ms_ready, 1)
                dve.wait_ge(root_ready, 1)
                dve.reciprocal(rstd[:, 2, :], rstd[:, 1, :]).then_inc(rstd_ready, 1)
                dve.wait_ge(rstd_ready, 1)
                dve.wait_ge(gain_in, 16)
                for k in range(KT):
                    dve.scalar_tensor_tensor(out=g.ht[:, k, :], in0=g.xt[:, k, :], scalar=gain[:, k:k + 1],
                                             in1=rstd[:, 2, :], op0=ALU.mult, op1=ALU.mult)

            @block.scalar
            def _(act):
                for s in range(4):
                    act.wait_ge(added[s], 2 * pairs)
                for k in range(KT):
                    if k >= 2:
                        act.wait_ge(sum_step, k - 1)
                    act.activation(sq[:, k % 2, :], g.xt[:, k, :], ACT.Square).then_inc(squared, 1)
                act.wait_ge(ms_ready, 2)
                act.activation(rstd[:, 1, :], rstd[:, 0, :], ACT.Sqrt).then_inc(root_ready, 1)


def stage_ffn(nc, g):
    HC = TC // 2
    KH = D_FF // P // 2
    U = KH // 2
    B = D // 512
    with ExitStack() as ctx:
        wbuf = ctx.enter_context(nc.sbuf_tensor("f_w", [P, 2, KH * 256], F32))
        hid = ctx.enter_context(nc.sbuf_tensor("f_hid", [P, KH, TC], F32))
        sg = ctx.enter_context(nc.sbuf_tensor("f_sg", [P, 4, HC], F32))
        ps = ctx.enter_context(nc.psum_tensor("f_ps", [P, 8, 512], F32))
        loaded = [new_sem(nc, g, f"f_loaded{i}") for i in range(2)]
        gu_summed = [new_sem(nc, g, f"f_gu_summed{i}") for i in range(2)]
        silu_ready = [new_sem(nc, g, f"f_silu_ready{i}") for i in range(2)]
        hid_ready = [new_sem(nc, g, f"f_hid_ready{i}") for i in range(2)]
        down_summed = [new_sem(nc, g, f"f_down_summed{i}") for i in range(2)]
        added = [new_sem(nc, g, f"f_added{i}") for i in range(2)]
        gate_v = g.w_gate.rearrange("(k p) n -> p k n", p=P)
        up_v = g.w_up.rearrange("(k p) n -> p k n", p=P)
        down_v = g.w_down.rearrange("(k p) n -> p k n", p=P)
        wg = wbuf[:, :, 0:KT * 256].rearrange("p b (k n) -> p b k n", k=KT)
        wd = wbuf[:].rearrange("p b (k n) -> p b k n", k=KH)
        KQ = KH // 2
        with nc.Block() as block:
            @block.sync
            def _(sp):
                for f in range(2):
                    if f:
                        for b in range(2):
                            sp.wait_ge(down_summed[b], 2 * B * f)
                    with sp.Fori(0, U) as i:
                        for b in range(2):
                            sp.wait_ge(gu_summed[b], i * 2 + 2 * U * f)
                            col = i * 256 + (f * KH + b) * P
                            sp.dma_start(wg[:, b, :, 0:P], gate_v[:, :, bass.ds(col, P)]).then_inc(loaded[b], 16)
                            sp.dma_start(wg[:, b, :, P:256], up_v[:, :, bass.ds(col, P)]).then_inc(loaded[b], 16)
                    for b in range(2):
                        sp.wait_ge(gu_summed[b], 2 * U * (f + 1))
                    with sp.Fori(0, B) as i:
                        for b in range(2):
                            sp.wait_ge(down_summed[b], i * 2 + 2 * B * f)
                            for q in range(2):
                                sp.dma_start(wd[:, b, q * KQ:(q + 1) * KQ, :],
                                             down_v[:, f * KH + q * KQ:f * KH + (q + 1) * KQ,
                                                    bass.ds(i * 512 + b * 256, 256)]).then_inc(loaded[b], 16)

            @block.tensor
            def _(pe):
                for f in range(2):
                    for b in range(2):
                        if f:
                            pe.wait_ge(added[b], 4 * B * f)
                    with pe.Fori(0, U) as i:
                        for b in range(2):
                            pe.wait_ge(loaded[b], i * 32 + 32 * ((U + B) * f + 1))
                            pe.wait_ge(hid_ready[b], i * 2 + 2 * U * f)
                            for h in range(2):
                                for m in range(2):
                                    for k in range(KT):
                                        last = pe.matmul(ps[:, 4 * b + 2 * h + m, 0:HC], wg[:, b, k, m * P:(m + 1) * P],
                                                         g.ht[:, k, h * HC:(h + 1) * HC], start=(k == 0),
                                                         stop=(k == KT - 1))
                                last.then_inc(gu_summed[b], 1)
                    for b in range(2):
                        pe.wait_ge(hid_ready[b], 2 * U * (f + 1))
                    with pe.Fori(0, B) as i:
                        for b in range(2):
                            pe.wait_ge(loaded[b], i * 32 + 32 * ((U + B) * f + U + 1))
                            pe.wait_ge(added[b], i * 4 + 4 * B * f)
                            for m in range(2):
                                for k in range(KH):
                                    for h in range(2):
                                        last = pe.matmul(ps[:, 4 * b + 2 * m + h, 0:HC], wd[:, b, k, m * P:(m + 1) * P],
                                                         hid[:, k, h * HC:(h + 1) * HC], start=(k == 0),
                                                         stop=(k == KH - 1))
                                last.then_inc(down_summed[b], 1)

            @block.scalar
            def _(act):
                for f in range(2):
                    with act.Fori(0, U) as i:
                        for b in range(2):
                            act.wait_ge(hid_ready[b], i * 2 + 2 * U * f)
                            for h in range(2):
                                act.wait_ge(gu_summed[b], i * 2 + 2 * U * f + h + 1)
                                act.activation(sg[:, 2 * b + h, :], ps[:, 4 * b + 2 * h, 0:HC],
                                               ACT.Silu).then_inc(silu_ready[b], 1)

            @block.vector
            def _(dve):
                for f in range(2):
                    with dve.Fori(0, U) as i:
                        for b in range(2):
                            for h in range(2):
                                dve.wait_ge(silu_ready[b], i * 2 + 2 * U * f + h + 1)
                                out = hid[:, bass.ds(i * 2 + b, 1), h * HC:(h + 1) * HC].rearrange("p a t -> p (a t)")
                                dve.tensor_tensor(out, sg[:, 2 * b + h, :], ps[:, 4 * b + 2 * h + 1, 0:HC],
                                                  ALU.mult).then_inc(hid_ready[b], 1)
                    for b in range(2):
                        if f:
                            dve.wait_ge(added[b], 4 * B * f)
                    with dve.Fori(0, B) as i:
                        for b in range(2):
                            for m in range(2):
                                dve.wait_ge(down_summed[b], i * 2 + 2 * B * f + m + 1)
                                for h in range(2):
                                    x = g.xt[:, bass.ds(i * 4 + 2 * b + m, 1), h * HC:(h + 1) * HC].rearrange("p a t -> p (a t)")
                                    dve.tensor_tensor(x, x, ps[:, 4 * b + 2 * m + h, 0:HC], ALU.add).then_inc(added[b], 1)


def stage_final(nc, g):
    with ExitStack() as ctx:
        rows = ctx.enter_context(nc.sbuf_tensor("z_rows", [P, 2, D], F32))
        yrow = ctx.enter_context(nc.sbuf_tensor("z_yrow", [P, 2, D], F32))
        gain = ctx.enter_context(nc.sbuf_tensor("z_gain", [P, D], F32))
        junk = ctx.enter_context(nc.sbuf_tensor("z_junk", [P, D], F32))
        stat = ctx.enter_context(nc.sbuf_tensor("z_stat", [P, 5, 4], F32))
        ps = ctx.enter_context(nc.psum_tensor("z_ps", [P, 4, 512], F32))
        gain_in = new_sem(nc, g, "z_gain_in")
        turned = new_sem(nc, g, "z_turned")
        copied = new_sem(nc, g, "z_copied")
        squares = new_sem(nc, g, "z_squares")
        chain = new_sem(nc, g, "z_chain")
        ms_ready = new_sem(nc, g, "z_ms_ready")
        root_ready = new_sem(nc, g, "z_root_ready")
        y_ready = new_sem(nc, g, "z_y_ready")
        stored = [new_sem(nc, g, f"z_stored{i}") for i in range(2)]
        dsts = [g.y_prompt[r:r + n, :] for r, n in ROW_TILES[:4]] + [g.y_sample]
        with nc.Block() as block:
            @block.sync
            def _(sp):
                sp.dma_start(gain[:], g.g_final[None, :].to_broadcast([P, D])).then_inc(gain_in, 16)
                for i, (r, n) in enumerate(ROW_TILES):
                    sp.wait_ge(y_ready, i + 1)
                    sp.dma_start(dsts[i], yrow[0:n, i % 2, :]).then_inc(stored[i % 2], 16)
                sp.wait_ge(stored[0], 48)
                sp.wait_ge(stored[1], 32)

            @block.tensor
            def _(pe):
                for i, (r, n) in enumerate(ROW_TILES):
                    for q in range(4):
                        if i >= 1:
                            pe.wait_ge(copied, 4 * (i - 1) + q + 1)
                        for k in range(4):
                            last = pe.transpose(ps[0:n, q, k * P:(k + 1) * P], g.xt[:, 4 * q + k, r:r + n], g.ident[:])
                        last.then_inc(turned, 1)

            @block.scalar
            def _(act):
                for i, (r, n) in enumerate(ROW_TILES):
                    act.wait_ge(ms_ready, i + 1)
                    act.activation(stat[0:n, i, 2:3], stat[0:n, i, 1:2], ACT.Sqrt).then_inc(root_ready, 1)

            @block.vector
            def _(dve):
                c = 0
                for i, (r, n) in enumerate(ROW_TILES):
                    for q in range(4):
                        dve.wait_ge(turned, 4 * i + q + 1)
                        dve.tensor_copy(rows[0:n, i % 2, q * 512:(q + 1) * 512], ps[0:n, q, :]).then_inc(copied, 1)
                    dve.wait_ge(copied, 4 * i + 4)
                    x = rows[0:n, i % 2, :]
                    dve.tensor_tensor_reduce(out=junk[0:n, :], in0=x, in1=x, scale=1.0, scalar=0.0, op0=ALU.mult,
                                             op1=ALU.add, accum_out=stat[0:n, i, 0:1]).then_inc(chain, 1)
                    c += 1
                    dve.wait_ge(chain, c)
                    dve.tensor_scalar(stat[0:n, i, 1:2], stat[0:n, i, 0:1], 1.0 / D, EPS, ALU.mult, ALU.add).then_inc(ms_ready, 1)
                    dve.wait_ge(root_ready, i + 1)
                    dve.reciprocal(stat[0:n, i, 3:4], stat[0:n, i, 2:3]).then_inc(chain, 1)
                    c += 1
                    dve.wait_ge(chain, c)
                    if i == 0:
                        dve.wait_ge(gain_in, 16)
                    if i >= 2:
                        dve.wait_ge(stored[i % 2], 16 * (i // 2))
                    dve.scalar_tensor_tensor(out=yrow[0:n, i % 2, :], in0=x, scalar=stat[0:n, i, 3:4],
                                             in1=gain[0:n, :], op0=ALU.mult, op1=ALU.mult).then_inc(y_ready, 1)


def stage_constants(nc, g):
    made = new_sem(nc, g, "c_made")

    with nc.Block() as block:
        @block.gpsimd
        def _(pool):
            step = Chain(pool, made)

            def band(t, rows, cols, pattern, mult, base, op, fill=0.0):
                step(pool.affine_select(out=t, in_=t, compare_op=op, fill=fill, base=base, pattern=pattern,
                                        channel_multiplier=mult))

            step(pool.memset(g.ident[:], 0.0))
            band(g.ident[:], P, P, [[-1, P]], 1, 0, ALU.not_equal, 1.0)
            step(pool.memset(g.ones[:], 1.0))

            def blocks(t, rows, cols, w):
                step(pool.memset(t, 1.0))
                v = t.rearrange("p (n w) -> p n w", w=w)
                band(v, rows, cols, [[-w, cols // w], [0, w]], 1, 0, ALU.is_ge)
                band(v, rows, cols, [[w, cols // w], [0, w]], -1, w - 1, ALU.is_ge)

            blocks(g.blk64[:], P, P, 64)
            blocks(g.blk4[:], P, P, 4)
            step(pool.memset(g.mask_g[:], 1.0))
            for lo in (0, C):
                rows = g.mask_g[lo:lo + C, :]
                band(rows[:, 0:C], C, C, [[1, C]], -1, -1, ALU.is_ge)
                band(rows[:, C:P], C, C, [[1, C]], -1, 0, ALU.is_ge)
            blocks(g.up16[:], C, C, 16)
            band(g.up16[:], C, C, [[1, C]], -1, -1, ALU.is_ge)
            blocks(g.low16[:], C, C, 16)
            band(g.low16[:], C, C, [[-1, C]], 1, -1, ALU.is_ge)
            step(pool.memset(g.low32[:], 0.0))
            step(pool.memset(g.low64[:], 0.0))
            for j in range(2):
                t = g.low32[:, 32 * j:32 * j + 16]
                step(pool.memset(t, 1.0))
                band(t, C, 16, [[0, 16]], 1, -(32 * j + 16), ALU.is_ge)
                band(t, C, 16, [[0, 16]], -1, 32 * j + 31, ALU.is_ge)
            t = g.low64[:, 0:32]
            step(pool.memset(t, 1.0))
            band(t, C, 32, [[0, 32]], 1, -32, ALU.is_ge)


def constants(nc, g, ctx):
    def sb(name, rows, cols):
        return ctx.enter_context(nc.sbuf_tensor(name, [rows, cols], F32))
    g.ident, g.ones, g.blk64, g.blk4, g.mask_g = (sb(n, P, P) for n in ("ident", "ones", "blk64", "blk4", "mask_g"))
    g.up16, g.low16, g.low32, g.low64 = (sb(n, C, C) for n in ("up16", "low16", "low32", "low64"))


def rwkv(nc, g):
    with ExitStack() as ctx:
        def sb(name, shape):
            return ctx.enter_context(nc.sbuf_tensor(name, shape, F32))
        g.gate_t = sb("gate_t", [P, NPAIR, TC])
        g.bonus_t = sb("bonus_t", [P, NPAIR, TC])
        g.y_t = sb("y_t", [P, NPAIR, TC])
        g.chunk_decay = sb("chunk_decay", [P, NPAIR, SEQ // C])
        g.v_samp = sb("v_samp", [P, NPAIR, NB])
        stage_rwkv_prep(nc, g)
        stage_rwkv_chunks(nc, g)
        stage_rwkv_sample(nc, g)
        stage_rwkv_post(nc, g)


def nsa(nc, g):
    with ExitStack() as ctx:
        g.kc = ctx.enter_context(nc.sbuf_tensor("kc", [P, 2 * NB, 255], F32))
        g.vc = ctx.enter_context(nc.sbuf_tensor("vc", [P, NB, 512], F32))
        stage_compress(nc, g)
        stage_nsa_sample(nc, g)
    stage_nsa_prompt(nc, g)


def build(nc, g):
    g.sems, g.waited = [], nc.alloc_semaphore("waited")
    g.proj_t = nc.dram_tensor("proj_t", [KV0, TA], F32, kind="Internal").ap()
    g.kv_rows = nc.dram_tensor("kv_rows", [TC, 1536], F32, kind="Internal").ap()
    g.gates = nc.dram_tensor("gates", [TC, 48], F32, kind="Internal").ap()
    g.rk_chunks = nc.dram_tensor("rk_chunks", [SEQ // C, P, NPAIR, 5 * C], F32, kind="Internal").ap()
    g.samp_rows = nc.dram_tensor("samp_rows", [6 * NB, D_R], F32, kind="Internal").ap()
    g.kc_prompt = nc.dram_tensor("kc_prompt", [256, 31], F32, kind="Internal").ap()
    g.vc_prompt = nc.dram_tensor("vc_prompt", [31, 256], F32, kind="Internal").ap()
    g.mix_t = nc.dram_tensor("mix_t", [D, TC], F32, kind="Internal").ap()
    with ExitStack() as ctx:
        constants(nc, g, ctx)
        stage_constants(nc, g)
        with ExitStack() as c2:
            g.xn = c2.enter_context(nc.sbuf_tensor("xn", [P, KT, TA], F32))
            stage_norm(nc, g)
            stage_in_proj(nc, g)
        rwkv(nc, g)
        retire_sems(nc, g)
        nsa(nc, g)
        retire_sems(nc, g)
        with ExitStack() as c2:
            g.xt = c2.enter_context(nc.sbuf_tensor("xt", [P, KT, TC], F32))
            stage_turn_x(nc, g)
            with ExitStack() as c3:
                g.ht = c3.enter_context(nc.sbuf_tensor("ht", [P, KT, TC], F32))
                stage_out_proj(nc, g)
                stage_ffn(nc, g)
            stage_final(nc, g)


def views(ins, outs):
    i = ins
    g = Arrays()
    g.x_prompt = i["x_prompt"][0]
    g.x_sample = i["x_sample"][:, 0, :]
    g.shift = i["state_shift"][0]
    g.g_mix = i["g_mix"][0]
    g.w_in = i["w_in"][0]
    g.mu = i["mu"][0]
    g.w0 = i["w0"][0]
    g.w2 = i["w2"][0]
    g.a0 = i["a0"][0]
    g.a2 = i["a2"][0]
    g.g2 = i["g2"][0]
    g.k_k = i["k_k"][0]
    g.k_a = i["k_a"][0]
    g.r_k = i["r_k"][0]
    g.lnx_w = i["lnx_w"][0]
    g.lnx_b = i["lnx_b"][0]
    g.state_wkv = i["state_wkv"][0]
    g.phi_pe = i["phi_pe"][0]
    g.phi_w1 = i["phi_w1"][0]
    g.phi_w2 = i["phi_w2"][0]
    g.page_table = i["page_table"]
    g.cache_cmp = i["cache_cmp_kv"][0].rearrange("n r k h d -> n r (k h d)")
    g.cache_slc = i["cache_slc_kv"][0].rearrange("n r k h d -> n r (k h d)")
    g.cache_win = i["cache_win_kv"][0].rearrange("b r k h d -> b r (k h d)")
    g.new_cmp_prompt = outs[2][0, 0].rearrange("r k h d -> r (k h d)")
    g.new_slc_prompt = outs[3][0, 0].rearrange("r k h d -> r (k h d)")
    g.new_win_prompt = outs[4][0, 0].rearrange("r k h d -> r (k h d)")
    g.new_cmp_sample = outs[7][0, :, 0].rearrange("b k h d -> b (k h d)")
    g.new_slc_sample = outs[8][0, :, 0].rearrange("b k h d -> b (k h d)")
    g.new_win_sample = outs[9][0].rearrange("b r k h d -> b r (k h d)")
    g.new_wkv_prompt = outs[5][0, 0]
    g.new_wkv_sample = outs[10][0]
    g.w_o = i["w_o"][0]
    g.g_ffn = i["g_ffn"][0]
    g.w_gate = i["w_gate"][0]
    g.w_up = i["w_up"][0]
    g.w_down = i["w_down"][0]
    g.g_final = i["g_final"]
    g.y_prompt = outs[0][0]
    g.y_sample = outs[1][:, 0, :]
    g.new_shift_prompt = outs[6][0]
    g.new_shift_sample = outs[11][0]
    g.ins = ins
    g.outs = outs
    return g


_OUTS = [(1, 512, 2048), (8, 1, 2048), (1, 1, 512, 2, 4, 64), (1, 1, 512, 2, 4, 64), (1, 1, 512, 2, 4, 64),
         (1, 1, 16, 64, 64), (1, 1, 2048), (1, 8, 1, 2, 4, 64), (1, 8, 1, 2, 4, 64), (1, 8, 512, 2, 4, 64),
         (1, 8, 16, 64, 64), (1, 8, 2048)]


def kernel(**inputs):
    import numpy as _np
    import concourse.bacc as _bacc
    from concourse import mybir as _mybir
    from concourse.bass_utils import run_bass_kernel_spmd as _run

    nc = _bacc.Bacc("TRN2", target_bir_lowering=False, num_devices=1)
    arrays, ins = {}, {}
    for name, a in inputs.items():
        a = _np.ascontiguousarray(a)
        arrays[f"in_{name}"] = a
        ins[name] = nc.dram_tensor(f"in_{name}", a.shape, _mybir.dt.from_np(a.dtype), kind="ExternalInput").ap()
    outs = [nc.dram_tensor(f"out_{n}", shape, F32, kind="ExternalOutput").ap() for n, shape in enumerate(_OUTS)]
    build(nc, views(ins, outs))
    r = _run(nc, [arrays], core_ids=[0])
    return tuple(r.results[0][f"out_{n}"] for n in range(len(_OUTS)))
```

```python
from contextlib import ExitStack

import concourse.bass as bass
from concourse import mybir

F32 = mybir.dt.float32
F32R = mybir.dt.float32r
I32 = mybir.dt.int32
U32 = mybir.dt.uint32
ALU = mybir.AluOpType
ACT = mybir.ActivationFunctionType
AX_X = mybir.AxisListType.X

P = 128
D = 2048
KT = D // P
SEQ = 512
NB = 8
TC = SEQ + NB
TA = TC + NB
HALF = TA // 2
D_R = 1024
NPAIR = D_R // P
R_COLS = 3328
KV0 = R_COLS + 1024
KVG = 1584
C = 64
D_IN = KV0 + KVG
LW, LA, LG = 96, 96, 64
D_FF = 5632
EPS = 1e-6
NEG = -1e30
ROW_TILES = [(0, 128), (128, 128), (256, 128), (384, 128), (SEQ, NB)]


POOL_DMA = ("stored", "loaded", "rows_out", "state_out", "gain_in", "mix_in")


def three_products(pe, out, w_hi, w_lo, x_hi, x_lo, start, stop):
    n = len(out)
    for j in range(n):
        pe.matmul(out[j], w_hi, x_hi[j], start=start, stop=False)
    for j in range(n):
        pe.matmul(out[j], w_hi, x_lo[j], start=False, stop=False)
    for j in range(n):
        last = pe.matmul(out[j], w_lo, x_hi[j], start=False, stop=stop)
    return last


def new_sem(nc, g, name):
    sem = nc.alloc_semaphore(name)
    if not any(n in name for n in POOL_DMA):
        g.sems.append(sem)
    return sem


def take_wait(g, eng):
    eng.sem_inc(g.waited, 1)


def retire_sems(nc, g):
    with nc.Block() as block:
        @block.gpsimd
        def _(pool):
            for sem in g.sems:
                pool.sem_clear(sem)
    for sem in g.sems:
        nc.release_semaphore(sem)
    g.sems = []


def stage_norm(nc, g):
    with ExitStack() as ctx:
        rows = ctx.enter_context(nc.sbuf_tensor("n_rows", [P, 2, D], F32))
        junk = ctx.enter_context(nc.sbuf_tensor("n_junk", [P, D], F32))
        gain = ctx.enter_context(nc.sbuf_tensor("n_gain", [P, D], F32))
        xnr = ctx.enter_context(nc.sbuf_tensor("n_xnr", [P, 2, D], F32))
        stat = ctx.enter_context(nc.sbuf_tensor("n_stat", [P, 6, 4], F32))
        ps = ctx.enter_context(nc.psum_tensor("n_ps", [P, 4, 512], F32))
        loaded = [new_sem(nc, g, f"n_loaded{i}") for i in range(2)]
        gain_in = new_sem(nc, g, "n_gain_in")
        ms_ready = new_sem(nc, g, "n_ms_ready")
        root_ready = new_sem(nc, g, "n_root_ready")
        xn_ready = new_sem(nc, g, "n_xn_ready")
        turned = new_sem(nc, g, "n_turned")
        hi_ready = new_sem(nc, g, "n_hi_ready")
        copied = new_sem(nc, g, "n_copied")
        stored_prompt = new_sem(nc, g, "n_stored_prompt")
        stored_sample = new_sem(nc, g, "n_stored_sample")
        chain = new_sem(nc, g, "n_chain")
        tiles = [(g.x_prompt[r:r + n, :], r, n) for r, n in ROW_TILES[:4]]
        tiles += [(g.x_sample, SEQ, NB), (g.shift, TC, NB)]
        with nc.Block() as block:
            @block.sync
            def _(sp):
                sp.dma_start(gain[:], g.g_mix[None, :].to_broadcast([P, D])).then_inc(gain_in, 16)
                for i, (src, _c, n) in enumerate(tiles):
                    if i >= 2:
                        sp.wait_ge(xn_ready, i - 1)
                    sp.dma_start(rows[0:n, i % 2, :], src).then_inc(loaded[i % 2], 16)

            @block.vector
            def _(dve):
                c = 0
                dve.memset(junk[:], 0.0).then_inc(chain, 1)
                c += 1
                dve.wait_ge(chain, c)
                for i, (_s, _c, n) in enumerate(tiles):
                    x = rows[0:n, i % 2, :]
                    dve.wait_ge(loaded[i % 2], 16 * (i // 2 + 1))
                    if i < 5:
                        dve.tensor_tensor_reduce(out=junk[0:n, :], in0=x, in1=x, scale=1.0, scalar=0.0, op0=ALU.mult,
                                                 op1=ALU.add, accum_out=stat[0:n, i, 0:1]).then_inc(chain, 1)
                        c += 1
                        dve.wait_ge(chain, c)
                        dve.tensor_scalar(stat[0:n, i, 1:2], stat[0:n, i, 0:1], 1.0 / D, EPS, ALU.mult,
                                          ALU.add).then_inc(ms_ready, 1)
                        dve.wait_ge(root_ready, i + 1)
                        dve.reciprocal(stat[0:n, i, 3:4], stat[0:n, i, 2:3]).then_inc(chain, 1)
                        c += 1
                        dve.wait_ge(chain, c)
                    if i == 0:
                        dve.wait_ge(gain_in, 16)
                    if i >= 2:
                        dve.wait_ge(turned, 4 * (i - 1))
                    if i == 5:
                        dve.wait_ge(stored_prompt, 16)
                    if i < 5:
                        dve.scalar_tensor_tensor(out=xnr[0:n, i % 2, :], in0=x, scalar=stat[0:n, i, 3:4],
                                                 in1=gain[0:n, :], op0=ALU.mult, op1=ALU.mult).then_inc(xn_ready, 1)
                    else:
                        dve.tensor_copy(xnr[0:n, i % 2, :], x).then_inc(xn_ready, 1)
                    for q in range(4):
                        dve.wait_ge(hi_ready, 4 * i + q + 1)
                        dve.tensor_tensor(g.xl[:, 4 * q:4 * q + 4, _c:_c + n],
                                          ps[:, q, :].rearrange("p (k t) -> p k t", k=4)[:, :, 0:n],
                                          g.xh[:, 4 * q:4 * q + 4, _c:_c + n].bitcast(F32), ALU.subtract).then_inc(copied, 1)

            @block.scalar
            def _(act):
                for i, (_s, c, n) in enumerate(tiles):
                    if i < 5:
                        act.wait_ge(ms_ready, i + 1)
                        act.activation(stat[0:n, i, 2:3], stat[0:n, i, 1:2], ACT.Sqrt).then_inc(root_ready, 1)
                    for q in range(4):
                        act.wait_ge(turned, 4 * i + q + 1)
                        act.copy(g.xh[:, 4 * q:4 * q + 4, c:c + n],
                                 ps[:, q, :].rearrange("p (k t) -> p k t", k=4)[:, :, 0:n]).then_inc(hi_ready, 1)

            @block.tensor
            def _(pe):
                for i, (_s, _c, n) in enumerate(tiles):
                    pe.wait_ge(xn_ready, i + 1)
                    for q in range(4):
                        if i >= 1:
                            pe.wait_ge(copied, 4 * (i - 1) + q + 1)
                        for k in range(4):
                            last = pe.transpose(ps[:, q, k * P:k * P + n],
                                                xnr[0:n, i % 2, (4 * q + k) * P:(4 * q + k + 1) * P],
                                                g.ident[0:n, 0:n])
                        last.then_inc(turned, 1)

            @block.gpsimd
            def _(pool):
                pool.wait_ge(xn_ready, 4)
                pool.dma_start(g.new_shift_prompt, xnr[P - 1:P, 1, :]).then_inc(stored_prompt, 16)
                pool.wait_ge(xn_ready, 5)
                pool.dma_start(g.new_shift_sample, xnr[0:NB, 0, :]).then_inc(stored_sample, 16)
                pool.wait_ge(stored_prompt, 16)
                pool.wait_ge(stored_sample, 16)



def stage_in_proj(nc, g):
    with ExitStack() as ctx:
        w_raw = ctx.enter_context(nc.sbuf_tensor("p_w", [P, 2, KT, 256], F32))
        w_hi = ctx.enter_context(nc.sbuf_tensor("p_w_hi", [P, 2, KT, 256], F32R))
        w_lo = ctx.enter_context(nc.sbuf_tensor("p_w_lo", [P, 2, KT, 256], F32R))
        ob = ctx.enter_context(nc.sbuf_tensor("p_ob", [P, 4, TA], F32))
        orow = ctx.enter_context(nc.sbuf_tensor("p_orow", [P, 2, 5, 256], F32))
        ps = ctx.enter_context(nc.psum_tensor("p_ps", [P, 8, 512], F32))
        loaded = [new_sem(nc, g, f"p_w_in{i}") for i in range(4)]
        hi_done = new_sem(nc, g, "p_hi_done")
        lo_done = new_sem(nc, g, "p_lo_done")
        summed = [new_sem(nc, g, f"p_summed{i}") for i in range(4)]
        copied = [new_sem(nc, g, f"p_copied{i}") for i in range(4)]
        stored = [new_sem(nc, g, f"p_stored{i}") for i in range(4)]
        row_summed = [new_sem(nc, g, f"p_row_summed{i}") for i in range(5)]
        row_copied = [new_sem(nc, g, f"p_row_copied{i}") for i in range(5)]
        row_stored = [new_sem(nc, g, f"p_row_stored{i}") for i in range(2)]
        w_view = g.w_in.rearrange("(k p) n -> p k n", p=P)
        CU = KV0 // P
        quads = CU // 4
        chunks = 6
        assert CU == 4 * quads + 2 and KVG == chunks * 256 + 48

        def slot(buf, s, n=P):
            return buf[:, s // 2, :, (s % 2) * P:(s % 2) * P + n]

        def high(act, i, u, n=P):
            s = u % 4
            act.wait_ge(loaded[s], i * 16 + (u // 4 + 1) * 16)
            act.copy(slot(w_hi, s, n), slot(w_raw, s, n)).then_inc(hi_done, 1)

        def low(dve, i, u, n=P):
            s = u % 4
            dve.wait_ge(hi_done, i * 4 + u + 1)
            dve.tensor_tensor(slot(w_lo, s, n), slot(w_raw, s, n), slot(w_hi, s, n).bitcast(F32),
                              ALU.subtract).then_inc(lo_done, 1)

        with nc.Block() as block:
            @block.sync
            def _(sp):
                def load(s, col, n=P):
                    sp.dma_start(slot(w_raw, s, n), w_view[:, :, bass.ds(col, n)]).then_inc(loaded[s], 16)
                for s in range(4):
                    load(s, s * P)
                with sp.Fori(0, quads) as i:
                    for s in range(4):
                        sp.wait_ge(summed[s], i + 1)
                        load(s, i * 512 + (4 + s) * P)
                for s in range(2):
                    sp.wait_ge(summed[s], quads + 1)
                    load(s, (CU + 2 + s) * P)
                for c in range(2, chunks + 1):
                    sp.wait_ge(row_summed[4], c - 1)
                    for s in range(2):
                        if c < chunks:
                            load((CU + 2 * c + s) % 4, (CU + 2 * c + s) * P)
                load((CU + 2 * chunks) % 4, (CU + 2 * chunks) * P, 48)

            @block.tensor
            def _(pe):
                def columns(i, s):
                    b, cols = s // 2, slice((s % 2) * P, (s % 2) * P + P)
                    pe.wait_ge(lo_done, i * 4 + s + 1)
                    pe.wait_ge(copied[s], i * 2)
                    for k in range(KT):
                        last = three_products(pe, [ps[:, 2 * s + h, 0:HALF] for h in range(2)],
                                              w_hi[:, b, k, cols], w_lo[:, b, k, cols],
                                              [g.xh[:, k, h * HALF:(h + 1) * HALF] for h in range(2)],
                                              [g.xl[:, k, h * HALF:(h + 1) * HALF] for h in range(2)],
                                              k == 0, k == KT - 1)
                    last.then_inc(summed[s], 1)

                def rows(chunk, b, units, n):
                    pe.wait_ge(lo_done, units)
                    for t, (r, m) in enumerate(ROW_TILES):
                        pe.wait_ge(row_copied[t], chunk)
                        for k in range(KT):
                            last = three_products(pe, [ps[0:m, t, 0:n]], g.xh[:, k, r:r + m], g.xl[:, k, r:r + m],
                                                  [w_hi[:, b, k, 0:n]], [w_lo[:, b, k, 0:n]], k == 0, k == KT - 1)
                        last.then_inc(row_summed[t], 1)

                with pe.Fori(0, quads) as i:
                    for s in range(4):
                        columns(i, s)
                for s in range(2):
                    columns(quads, s)
                for s in range(4):
                    pe.wait_ge(copied[s], 2 * (quads + (s < 2)))
                with pe.Fori(0, chunks // 2) as i:
                    for b in (1, 0):
                        rows(2 * i + 1 - b, b, i * 4 + CU + 4 - 2 * b, 256)
                rows(chunks, 1, CU + 2 * chunks + 1, 48)

            def copy_columns(eng, i, s, copy):
                eng.wait_ge(summed[s], i + 1)
                eng.wait_ge(stored[s], i * 16)
                for h in range(2):
                    copy(ob[:, s, h * HALF:(h + 1) * HALF], ps[:, 2 * s + h, 0:HALF]).then_inc(copied[s], 1)

            @block.vector
            def _(dve):
                for u in range(2):
                    low(dve, 0, u)
                with dve.Fori(0, quads) as i:
                    for s in range(4):
                        low(dve, i, s + 2)
                        if s % 2 == 0:
                            copy_columns(dve, i, s, dve.tensor_copy)
                low(dve, quads, 2)
                copy_columns(dve, quads, 0, dve.tensor_copy)
                low(dve, quads, 3)

                def row_chunk(i, b, ahead):
                    for u, n in ahead:
                        low(dve, i, u, n)
                    dve.wait_ge(row_stored[b], i * 32)
                    for t, (_r, m) in enumerate(ROW_TILES):
                        dve.wait_ge(row_summed[t], 2 * i + 2 - b)
                        dve.tensor_copy(orow[0:m, b, t, :], ps[0:m, t, 0:256]).then_inc(row_copied[t], 1)

                with dve.Fori(0, chunks // 2 - 1) as i:
                    row_chunk(i, 1, [(CU + 2, P), (CU + 3, P)])
                    row_chunk(i, 0, [(CU + 4, P), (CU + 5, P)])
                row_chunk(chunks // 2 - 1, 1, [(CU + 2, P), (CU + 3, P)])
                row_chunk(chunks // 2 - 1, 0, [(CU + 4, 48)])

            @block.scalar
            def _(act):
                for u in range(2):
                    high(act, 0, u)
                with act.Fori(0, quads) as i:
                    for s in range(4):
                        high(act, i, s + 2)
                        if s % 2 == 1:
                            copy_columns(act, i, s, act.copy)
                for u in range(CU, CU + 2):
                    high(act, 0, u)
                copy_columns(act, quads, 1, act.copy)
                for u in range(CU + 2, CU + 2 * chunks):
                    high(act, 0, u)
                high(act, 0, CU + 2 * chunks, 48)
                act.wait_ge(row_stored[1], chunks // 2 * 32)
                for t, (_r, m) in enumerate(ROW_TILES):
                    act.wait_ge(row_summed[t], chunks + 1)
                    act.activation(orow[0:m, 1, t, 0:48], ps[0:m, t, 0:48], ACT.Sigmoid).then_inc(row_copied[t], 1)

            @block.gpsimd
            def _(pool):
                def store_columns(i, s):
                    pool.wait_ge(copied[s], i * 2 + 2)
                    pool.dma_start(g.proj_t[bass.ds(i * 512 + s * P, P), :], ob[:, s, :]).then_inc(stored[s], 16)

                def store_rows(chunk, b, dst, n):
                    for t in range(5):
                        pool.wait_ge(row_copied[t], chunk + 1)
                    pool.dma_start(dst[0:SEQ].rearrange("(t p) n -> p t n", p=P),
                                   orow[:, b, 0:4, 0:n]).then_inc(row_stored[b], 16)
                    pool.dma_start(dst[SEQ:TC], orow[0:NB, b, 4, 0:n]).then_inc(row_stored[b], 16)

                with pool.Fori(0, quads) as i:
                    for s in range(4):
                        store_columns(i, s)
                for s in range(2):
                    store_columns(quads, s)
                with pool.Fori(0, chunks // 2) as i:
                    for b in (1, 0):
                        store_rows(2 * i + 1 - b, b, g.kv_rows[:, bass.ds(i * 512 + (1 - b) * 256, 256)], 256)
                store_rows(chunks, 1, g.gates, 48)
                for s in range(4):
                    pool.wait_ge(stored[s], 16 * (quads + (s < 2)))
                for b in range(2):
                    pool.wait_ge(row_stored[b], 32 * (chunks // 2 + b))


class Arrays:
    pass


class Chain:

    def __init__(self, eng, sem, base=0):
        self.eng, self.sem, self.base, self.n = eng, sem, base, 0

    def __call__(self, ins):
        ins.then_inc(self.sem, 1)
        self.n += 1
        self.eng.wait_ge(self.sem, self.base + self.n)


def stage_rwkv_prep(nc, g):
    CH = SEQ // C
    HC = TC // 2
    DECAY = -0.6065306597126334
    with ExitStack() as ctx:
        def sb(name, shape):
            return ctx.enter_context(nc.sbuf_tensor("r_" + name, shape, F32))

        def sem(name):
            return new_sem(nc, g, "r_" + name)

        raw = sb("raw", [P, 3, TA + 1])
        diff = sb("diff", [P, 3, TC])
        xr = sb("xr", [P, 3, TC])
        lraw = sb("lraw", [P, 3, TA + 1])
        lora = sb("lora", [P, 3, TC])
        lmu = sb("lmu", [P, 3])
        lw = sb("lw", [P, 3, P])
        vec = sb("vec", [P, 8, NPAIR])
        cv = sb("cv", [P, 8])
        reset = sb("reset", [P, CH, C])
        sw = sb("sw", [P, TC])
        a = sb("a", [P, TC])
        dec = sb("dec", [P, TC])
        kk = sb("kk", [P, TC])
        sq = sb("sq", [P, TC])
        nrm = sb("nrm", [P, TC])
        kf = sb("kf", [P, TC])
        bvec = sb("bvec", [P, TC])
        rkk = sb("rkk", [P, TC])
        cum = sb("cum", [P, 2, SEQ])
        ex = sb("ex", [P, 3, SEQ])
        samp = sb("samp", [P, NPAIR, 6, NB])
        srow = sb("srow", [6 * NB, D_R])
        outb = sb("outb", [P, CH, 5, C])
        ps = ctx.enter_context(nc.psum_tensor("r_ps", [P, 8, 512], F32))
        vec_in, lraw_in, raw_in, lw_in = sem("vec_in"), sem("lraw_in"), sem("raw_in"), sem("lw_in")
        chain, lora_ready, lora_act = sem("chain"), sem("lora_ready"), sem("lora_act")
        z_done, cv_ready, sig_done, g_done = sem("z_done"), sem("cv_ready"), sem("sig_done"), sem("g_done")
        x_ready, sq_ready, ss_done, norm_done = sem("x_ready"), sem("sq_ready"), sem("ss_done"), sem("norm_done")
        rkk_ready, bonus_done, cum_ready, exp_done = sem("rkk_ready"), sem("bonus_done"), sem("cum_ready"), sem("exp_done")
        out_ready, stored, rows_turned, rows_copied, rows_out = (sem("out_ready"), sem("stored"), sem("rows_turned"),
                                                                 sem("rows_copied"), sem("rows_out"))
        zero_ready, bonus_used = sem("zero_ready"), sem("bonus_used")
        lora_rows = [(3 * D_R, LW), (3 * D_R + LW, LA), (3 * D_R + LW + LA, LG)]
        vecs = [g.mu[0:D_R], g.mu[D_R:2 * D_R], g.mu[2 * D_R:3 * D_R], g.w0, g.a0, g.k_k, g.k_a, g.r_k]
        STEPS = 18

        with nc.Block() as block:
            @block.sync
            def _(sp):
                with nc.allow_non_contiguous_dma(reason="one value to a partition"):
                    for j, v in enumerate(vecs):
                        sp.dma_start(vec[:, j, :], v.rearrange("(q p) -> p q", p=P)).then_inc(vec_in, 16)
                    for j, (r, n) in enumerate(lora_rows):
                        sp.dma_start(lmu[0:n, j:j + 1], g.mu[r:r + n].rearrange("(p o) -> p o", o=1)).then_inc(vec_in, 16)
                for j, (r, n) in enumerate(lora_rows):
                    sp.dma_start(lraw[0:n, j, 1:], g.proj_t[r:r + n, :]).then_inc(lraw_in, 16)
                with sp.Fori(0, NPAIR) as i:
                    sp.wait_ge(z_done, i * 3)
                    sp.wait_ge(x_ready, i)
                    for j in range(3):
                        sp.dma_start(raw[:, j, 1:], g.proj_t[bass.ds(i * P + j * D_R, P), :]).then_inc(raw_in, 16)
                    for j, w in enumerate((g.w2, g.a2, g.g2)):
                        n = lora_rows[j][1]
                        sp.dma_start(lw[0:n, j, :], w[:, bass.ds(i * P, P)]).then_inc(lw_in, 16)

            @block.gpsimd
            def _(pool):
                with pool.Fori(0, NPAIR) as i:
                    pool.wait_ge(out_ready, i + 1)
                    pool.dma_start(g.rk_chunks[:, :, bass.ds(i, 1), :].rearrange("c p q n -> p c (q n)"),
                                   outb[:].rearrange("p c f t -> p c (f t)")).then_inc(stored, 16)
                pool.wait_ge(rows_copied, 2)
                pool.dma_start(g.samp_rows, srow[:]).then_inc(rows_out, 16)
                pool.wait_ge(stored, 16 * NPAIR)
                pool.wait_ge(rows_out, 16)

            @block.tensor
            def _(pe):
                pe.wait_ge(lora_act, 3)
                with pe.Fori(0, NPAIR) as i:
                    pe.wait_ge(lw_in, i * 48 + 48)
                    pe.wait_ge(bonus_used, i)
                    pe.wait_ge(sig_done, i * 2)
                    pe.wait_ge(g_done, i)
                    for j in range(3):
                        n = lora_rows[j][1]
                        for h in range(2):
                            last = pe.matmul(ps[:, 2 * j + h, 0:HC], lw[0:n, j, :], lora[0:n, j, h * HC:(h + 1) * HC],
                                             start=True, stop=True)
                        last.then_inc(z_done, 1)
                    pe.wait_ge(sq_ready, i + 1)
                    pe.wait_ge(norm_done, i)
                    for h in range(2):
                        last = pe.matmul(ps[:, 6 + h, 0:HC], g.blk64[:], sq[:, h * HC:(h + 1) * HC], start=True, stop=True)
                    last.then_inc(ss_done, 1)
                    pe.wait_ge(rkk_ready, i + 1)
                    pe.wait_ge(sig_done, i * 2 + 2)
                    for h in range(2):
                        last = pe.matmul(ps[:, h, 0:HC], g.blk64[:], rkk[:, h * HC:(h + 1) * HC], start=True, stop=True)
                    last.then_inc(bonus_done, 1)
                pe.wait_ge(out_ready, NPAIR)
                pe.wait_ge(g_done, NPAIR)
                for q in range(NPAIR):
                    last = pe.transpose(ps[0:6 * NB, 4 + q // 4, (q % 4) * P:(q % 4 + 1) * P],
                                        samp[:, q, :, :].rearrange("p f b -> p (f b)"), g.ident[:])
                last.then_inc(rows_turned, 1)

            @block.scalar
            def _(act):
                act.wait_ge(lora_ready, 3)
                act.activation(lora[0:LW, 0, :], lora[0:LW, 0, :], ACT.Tanh).then_inc(lora_act, 1)
                act.copy(lora[0:LA, 1, :], lora[0:LA, 1, :]).then_inc(lora_act, 1)
                act.activation(lora[0:LG, 2, :], lora[0:LG, 2, :], ACT.Sigmoid).then_inc(lora_act, 1)
                with act.Fori(0, NPAIR) as i:
                    act.wait_ge(cv_ready, i + 1)
                    for j, (dst, sem_) in enumerate(((sw, sig_done), (a, sig_done))):
                        act.wait_ge(z_done, i * 3 + j + 1)
                        act.activation(dst[:, 0:HC], ps[:, 2 * j, 0:HC], ACT.Sigmoid, bias=cv[:, 3 + j:4 + j])
                        act.activation(dst[:, HC:TC], ps[:, 2 * j + 1, 0:HC], ACT.Sigmoid,
                                       bias=cv[:, 3 + j:4 + j]).then_inc(sem_, 1)
                    act.wait_ge(z_done, i * 3 + 3)
                    gt = g.gate_t[:, bass.ds(i, 1), :].rearrange("p a t -> p (a t)")
                    act.copy(gt[:, 0:HC], ps[:, 4, 0:HC])
                    act.copy(gt[:, HC:TC], ps[:, 5, 0:HC]).then_inc(g_done, 1)
                    act.wait_ge(ss_done, i + 1)
                    act.activation(nrm[:, 0:HC], ps[:, 6, 0:HC], ACT.Sqrt)
                    act.activation(nrm[:, HC:TC], ps[:, 7, 0:HC], ACT.Sqrt).then_inc(norm_done, 1)
                    act.wait_ge(cum_ready, i + 1)
                    act.activation(ex[:, 0, :], cum[:, 0, :], ACT.Exp)
                    act.activation(ex[:, 1, :], cum[:, 0, :], ACT.Exp, scale=-1.0)
                    act.activation(ex[:, 2, :], cum[:, 1, :], ACT.Exp)
                    act.activation(samp[:, bass.ds(i, 1), 0, :].rearrange("p a b -> p (a b)"), dec[:, SEQ:TC],
                                   ACT.Exp).then_inc(exp_done, 1)

            @block.vector
            def _(dve):
                step = Chain(dve, chain)
                step(dve.memset(raw[:, :, 0:1], 0.0))
                step(dve.memset(lraw[:, :, 0:1], 0.0))
                step(dve.memset(reset[:], 1.0))
                step(dve.memset(reset[:, :, 0:1], 0.0))
                dve.wait_ge(vec_in, 16 * 11)
                dve.wait_ge(lraw_in, 48)
                for j, (_r, n) in enumerate(lora_rows):
                    x, d, o = lraw[0:n, j, :], diff[0:n, j, :], lora[0:n, j, :]
                    step(dve.tensor_tensor(d[:, 0:SEQ], x[:, 0:SEQ], x[:, 1:SEQ + 1], ALU.subtract))
                    step(dve.tensor_tensor(d[:, SEQ:TC], x[:, TC + 1:TA + 1], x[:, SEQ + 1:TC + 1], ALU.subtract))
                    dve.scalar_tensor_tensor(out=o, in0=d, scalar=lmu[0:n, j:j + 1], in1=x[:, 1:TC + 1], op0=ALU.mult,
                                             op1=ALU.add).then_inc(lora_ready, 1)
                dve.wait_ge(lora_ready, 3)
                before = step.n
                with dve.Fori(0, NPAIR) as i:
                    step = Chain(dve, chain, i * STEPS + before)
                    dve.wait_ge(sig_done, i * 2)
                    dve.tensor_copy(cv[:], vec[:, :, bass.ds(i, 1)].rearrange("p v a -> p (v a)")).then_inc(cv_ready, 1)
                    dve.wait_ge(cv_ready, i + 1)
                    dve.wait_ge(raw_in, i * 48 + 48)
                    step(dve.tensor_tensor(diff[:, :, 0:SEQ], raw[:, :, 0:SEQ], raw[:, :, 1:SEQ + 1], ALU.subtract))
                    step(dve.tensor_tensor(diff[:, :, SEQ:TC], raw[:, :, TC + 1:TA + 1], raw[:, :, SEQ + 1:TC + 1],
                                           ALU.subtract))
                    for j in range(3):
                        ins = dve.scalar_tensor_tensor(out=xr[:, j, :], in0=diff[:, j, :], scalar=cv[:, j:j + 1],
                                                       in1=raw[:, j, 1:TC + 1], op0=ALU.mult, op1=ALU.add)
                    ins.then_inc(x_ready, 1)
                    dve.wait_ge(x_ready, i + 1)
                    r, k, v = xr[:, 0, :], xr[:, 1, :], xr[:, 2, :]
                    step(dve.tensor_scalar(kk[:], k, cv[:, 5:6], None, ALU.mult))
                    dve.tensor_tensor(sq[:], kk[:], kk[:], ALU.mult).then_inc(sq_ready, 1)
                    dve.wait_ge(sig_done, i * 2 + 2)
                    step(dve.tensor_scalar(kf[:], a[:], -1.0, cv[:, 6:7], ALU.add, ALU.mult))
                    step(dve.scalar_tensor_tensor(out=kf[:], in0=kf[:], scalar=1.0, in1=k, op0=ALU.add, op1=ALU.mult))
                    dve.scalar_tensor_tensor(out=rkk[:], in0=r, scalar=cv[:, 7:8], in1=kf[:], op0=ALU.mult,
                                             op1=ALU.mult).then_inc(rkk_ready, 1)
                    step(dve.tensor_scalar(dec[:], sw[:], DECAY, None, ALU.mult))
                    step(dve.tensor_tensor_scan(cum[:, 0, :], reset[:].rearrange("p c t -> p (c t)"), dec[:, 0:SEQ], 0.0,
                                                ALU.mult, ALU.add))
                    dve.tensor_tensor(cum[:, 1, :], cum[:, 0, :], dec[:, 0:SEQ], ALU.subtract).then_inc(cum_ready, 1)
                    dve.wait_ge(norm_done, i + 1)
                    step(dve.tensor_scalar(nrm[:], nrm[:], 1e-12, None, ALU.max))
                    step(dve.reciprocal(nrm[:], nrm[:]))
                    step(dve.tensor_tensor(kk[:], kk[:], nrm[:], ALU.mult))
                    step(dve.tensor_tensor(bvec[:], kk[:], a[:], ALU.mult))
                    dve.wait_ge(bonus_done, i + 1)
                    bt = g.bonus_t[:, bass.ds(i, 1), :].rearrange("p a t -> p (a t)")
                    step(dve.tensor_tensor(bt[:, 0:HC], v[:, 0:HC], ps[:, 0, 0:HC], ALU.mult))
                    dve.tensor_tensor(bt[:, HC:TC], v[:, HC:TC], ps[:, 1, 0:HC], ALU.mult).then_inc(bonus_used, 1)
                    dve.wait_ge(exp_done, i + 1)
                    dve.wait_ge(stored, i * 16)

                    def chunks(x):
                        return x.rearrange("p (c t) -> p c t", t=C)

                    dve.scalar_tensor_tensor(out=outb[:, :, 0, :], in0=chunks(kk[:, 0:SEQ]), scalar=-1.0,
                                             in1=chunks(ex[:, 2, :]), op0=ALU.mult, op1=ALU.mult)
                    dve.tensor_tensor(outb[:, :, 1, :], chunks(r[:, 0:SEQ]), chunks(ex[:, 0, :]), ALU.mult)
                    dve.tensor_copy(outb[:, :, 2, :], chunks(v[:, 0:SEQ]))
                    dve.tensor_tensor(outb[:, :, 3, :], chunks(bvec[:, 0:SEQ]), chunks(ex[:, 1, :]), ALU.mult)
                    dve.tensor_tensor(outb[:, :, 4, :], chunks(kf[:, 0:SEQ]), chunks(ex[:, 1, :]), ALU.mult)
                    step(dve.tensor_copy(g.chunk_decay[:, bass.ds(i, 1), :].rearrange("p a c -> p (a c)"),
                                         chunks(ex[:, 0, :])[:, :, C - 1]))
                    sm = samp[:, bass.ds(i, 1), :, :].rearrange("p a f b -> p (a f) b")
                    step(dve.tensor_scalar(sm[:, 1, :], kk[:, SEQ:TC], -1.0, None, ALU.mult))
                    step(dve.tensor_copy(sm[:, 2, :], bvec[:, SEQ:TC]))
                    step(dve.tensor_copy(sm[:, 3, :], kf[:, SEQ:TC]))
                    step(dve.tensor_copy(sm[:, 4, :], r[:, SEQ:TC]))
                    step(dve.tensor_copy(sm[:, 5, :], v[:, SEQ:TC]))
                    dve.tensor_copy(g.v_samp[:, bass.ds(i, 1), :].rearrange("p a b -> p (a b)"),
                                    v[:, SEQ:TC]).then_inc(out_ready, 1)
                    dve.wait_ge(out_ready, i + 1)
                    assert step.n == STEPS, step.n
                dve.wait_ge(rows_turned, 1)
                for h in range(2):
                    dve.tensor_copy(srow[:, h * 512:(h + 1) * 512], ps[0:6 * NB, 4 + h, :]).then_inc(rows_copied, 1)


def stage_rwkv_chunks(nc, g):
    CH = SEQ // C
    NH = 8
    with ExitStack() as ctx:
        def sb(name, shape):
            return ctx.enter_context(nc.sbuf_tensor("s_" + name, shape, F32))

        def sem(name):
            return new_sem(nc, g, "s_" + name)

        cur = sb("cur", [P, 2, NPAIR, 5, C])
        G = sb("G", [P, 2, NH, P])
        L1, Lo32, Lo64 = sb("L1", [C, 2, NH, C]), sb("Lo32", [C, 2, NH, C]), sb("Lo64", [C, 2, NH, C])
        N1, X = sb("N1", [C, 2, NH, C]), sb("X", [C, 2, NH, C])
        N2, L2, N4, L4, L8 = (sb(n, [C, 2, NH, C]) for n in ("N2", "L2", "N4", "L4", "L8"))
        W, XT, Up = sb("W", [C, 2, NH, C]), sb("XT", [C, 2, NH, C]), sb("Up", [C, 2, NH, C])
        UV = sb("UV", [P, NPAIR, P])
        BK = sb("BK", [P, NPAIR, P])
        S = sb("S", [P, NPAIR, C])
        tmp = sb("tmp", [P, NPAIR, C])
        srow = sb("srow", [C, NPAIR, P])
        ps = ctx.enter_context(nc.psum_tensor("s_ps", [P, 8, 512], F32))
        loaded = [sem("loaded0"), sem("loaded1")]
        pe_done = [sem("pe_done0"), sem("pe_done1")]
        dve_done = [sem("dve_done0"), sem("dve_done1")]
        act_done = [sem("act_done0"), sem("act_done1")]
        zeroed, state_turned, state_copied, state_out = sem("zeroed"), sem("state_turned"), sem("state_copied"), sem("state_out")
        PN, DN, AN = 22, 14, 14

        def bank(gr, n, rows=P):
            return ps[0:rows, 4 * gr + n, :]

        def heads(ap, w=C):
            return ap.rearrange("p (h t) -> p h t", t=w)

        with nc.Block() as block:
            @block.sync
            def _(sp):
                def load(c, b):
                    sp.dma_start(cur[:, b, :, :, :].rearrange("p q f t -> p (q f t)"),
                                 g.rk_chunks[bass.ds(c, 1), :, :, :].rearrange("c p q n -> p (c q n)")
                                 ).then_inc(loaded[b], 16)
                for b in range(2):
                    load(b, b)
                with sp.Fori(0, CH // 2 - 1) as i:
                    for b in range(2):
                        for gr in range(2):
                            sp.wait_ge(pe_done[gr], i * 2 * PN + (b + 1) * PN)
                        load(i * 2 + 2 + b, b)

            @block.tensor
            def _(pe):
                pe.wait_ge(zeroed, 2)
                with pe.Fori(0, CH // 2) as i:
                    for b in range(2):
                        c = i * 2 + b
                        pe.wait_ge(loaded[b], i * 16 + 16)

                        def feat(q, gr, f):
                            return cur[gr * C:(gr + 1) * C, b, q, f, :]

                        def square(out, lhs, rhs, gr):
                            for h in range(NH):
                                last = pe.matmul(out[:, h * C:(h + 1) * C], lhs[:, gr, h, :], rhs[:, gr, h, :],
                                                 start=True, stop=True)
                            return last

                        def need(gr, d, a):
                            pe.wait_ge(dve_done[gr], c * DN + d) if d is not None else None
                            pe.wait_ge(act_done[gr], c * AN + a) if a is not None else None
                            take_wait(g, pe)

                        for gr in range(2):
                            need(gr, 0, 0)
                            for h in range(NH):
                                lo = gr * C
                                last = pe.matmul(bank(gr, h // 4)[:, (h % 4) * P:(h % 4 + 1) * P],
                                                 cur[lo:lo + C, b, h, 3:5, :].rearrange("p f t -> p (f t)"),
                                                 cur[lo:lo + C, b, h, 0:2, :].rearrange("p f t -> p (f t)"),
                                                 start=True, stop=True)
                            last.then_inc(pe_done[gr], 1)
                        for gr in range(2):
                            for h in range(NH):
                                last = pe.matmul(bank(gr, 2, C)[:, h * C:(h + 1) * C], feat(h, gr, 0), feat(h, gr, 3),
                                                 start=True, stop=True)
                            last.then_inc(pe_done[gr], 1)
                        for gr in range(2):
                            for q in range(4):
                                last = pe.transpose(bank(gr, 3)[:, q * P:(q + 1) * P],
                                                    cur[:, b, gr * 4 + q, 1:3, :].rearrange("p f t -> p (f t)"), g.ident[:])
                            last.then_inc(pe_done[gr], 1)
                        for gr in range(2):
                            need(gr, 4, None)
                            for q in range(4):
                                last = pe.transpose(bank(gr, 2)[:, q * P:(q + 1) * P],
                                                    cur[:, b, gr * 4 + q, 3:5, :].rearrange("p f t -> p (f t)"), g.ident[:])
                            last.then_inc(pe_done[gr], 1)
                        for n, lhs, rhs, d, a in ((0, L1, N1, 5, 1), (1, N1, L1, 5, 1),
                                                  (3, L2, N2, 5, 4), (0, N2, L2, 5, 4),
                                                  (2, L2, X, 6, 4),
                                                  (1, N4, L4, 6, 6), (3, L4, X, 7, 6),
                                                  (0, L8, X, 8, 7), (1, Lo32, X, 9, 7)):
                            for gr in range(2):
                                need(gr, d, a)
                                square(bank(gr, n, C), lhs, rhs, gr).then_inc(pe_done[gr], 1)
                        for n, d, a in ((2, 9, 8),):
                            for gr in range(2):
                                need(gr, d, a)
                                for h in range(NH):
                                    last = pe.transpose(bank(gr, n, C)[:, h * C:(h + 1) * C], X[:, gr, h, :],
                                                        g.ident[0:C, 0:C])
                                last.then_inc(pe_done[gr], 1)
                        for n, lhs, rhs, d, a in ((3, XT, W, 9, 9), (0, Lo64, X, 10, 9)):
                            for gr in range(2):
                                need(gr, d, a)
                                square(bank(gr, n, C), lhs, rhs, gr).then_inc(pe_done[gr], 1)
                        for gr in range(2):
                            need(gr, 10, 9)
                            for h in range(NH):
                                last = pe.transpose(bank(gr, 1, C)[:, h * C:(h + 1) * C], X[:, gr, h, :],
                                                    g.ident[0:C, 0:C])
                            last.then_inc(pe_done[gr], 1)
                        for gr in range(2):
                            need(gr, 10, 11)
                            square(bank(gr, 2, C), XT, W, gr).then_inc(pe_done[gr], 1)
                        for gr in range(2):
                            lo = gr * C
                            for q in range(NPAIR):
                                out = bank(gr, 3, C)[:, q * C:(q + 1) * C]
                                pe.matmul(out, feat(q, gr, 0), S[lo:lo + C, q, :], start=True, stop=False)
                                last = pe.matmul(out, G[:, gr, q, 0:C], UV[:, q, lo:lo + C], start=False, stop=True)
                            last.then_inc(pe_done[gr], 1)
                        for gr in range(2):
                            need(gr, 11, 12)
                            square(bank(gr, 0, C), X, Up, gr).then_inc(pe_done[gr], 1)
                        for gr in range(2):
                            need(gr, 11, 13)
                            lo = gr * C
                            for q in range(NPAIR):
                                out = ps[lo:lo + C, 4 * gr + 1, q * C:(q + 1) * C]
                                pe.matmul(out, S[lo:lo + C, q, :], feat(q, gr, 1), start=True, stop=False)
                                last = pe.matmul(out, UV[:, q, lo:lo + C], G[:, gr, q, C:P], start=False, stop=True)
                            last.then_inc(pe_done[gr], 1)
                        for gr in range(2):
                            for q in range(4):
                                last = pe.matmul(bank(gr, 2)[:, q * P:(q + 1) * P], BK[:, 4 * gr + q, :],
                                                 UV[:, 4 * gr + q, :], start=True, stop=True)
                            last.then_inc(pe_done[gr], 1)
                for gr in range(2):
                    pe.wait_ge(dve_done[gr], CH * DN)
                    pe.wait_ge(act_done[gr], CH * AN)
                for q in range(NPAIR):
                    last = pe.transpose(ps[0:C, q // 4, (q % 4) * P:(q % 4 + 1) * P], S[:, q, :], g.ident[:])
                last.then_inc(state_turned, 1)

            @block.scalar
            def _(act):
                with act.Fori(0, CH // 2) as i:
                    for b in range(2):
                        c = i * 2 + b

                        def copy(gr, p, out, in_):
                            act.wait_ge(pe_done[gr], c * PN + p)
                            act.copy(out, in_).then_inc(act_done[gr], 1)

                        for gr in range(2):
                            copy(gr, 3, UV[C:P, 4 * gr:4 * gr + 4, :], heads(ps[C:P, 4 * gr + 3, :], P))
                        for gr in range(2):
                            copy(gr, 4, BK[:, 4 * gr:4 * gr + 4, :], heads(bank(gr, 2), P))
                        for p, n, dst in ((5, 0, N2), (6, 1, L2), (7, 3, N4), (8, 0, L4), (10, 1, L8),
                                          (13, 1, W), (14, 2, XT), (16, 0, W), (17, 1, XT),
                                          (19, 3, Up)):
                            for gr in range(2):
                                copy(gr, p, dst[:, gr, :, :], heads(bank(gr, n, C)))
                        for gr in range(2):
                            copy(gr, 20, UV[0:C, :, gr * C:(gr + 1) * C], heads(bank(gr, 0, C)))
                        for gr in range(2):
                            copy(gr, 21, g.y_t[gr * C:(gr + 1) * C, :, bass.ds(c * C, C)],
                                 heads(ps[gr * C:(gr + 1) * C, 4 * gr + 1, :]))

            @block.vector
            def _(dve):
                dve.memset(UV[0:C, :, :], 0.0).then_inc(zeroed, 1)
                dve.memset(S[:], 0.0).then_inc(zeroed, 1)
                dve.wait_ge(zeroed, 2)
                with dve.Fori(0, CH // 2) as i:
                    for b in range(2):
                        c = i * 2 + b

                        def done(gr, ins):
                            ins.then_inc(dve_done[gr], 1)

                        def mask(m, rows=C, w=C):
                            return m.unsqueeze(1).to_broadcast([rows, NH, w])

                        for gr in range(2):
                            dve.wait_ge(pe_done[gr], c * PN + 1)
                            done(gr, dve.tensor_tensor(
                                G[:, gr, :, :], heads(ps[:, 4 * gr:4 * gr + 2, :].rearrange("p a n -> p (a n)"), P),
                                mask(g.mask_g[:], P, P), ALU.mult))
                        for gr in range(2):
                            dve.wait_ge(pe_done[gr], c * PN + 2)
                            for dst, m in ((L1, g.low16), (Lo32, g.low32), (Lo64, g.low64)):
                                done(gr, dve.tensor_tensor(dst[:, gr, :, :], heads(bank(gr, 2, C)), mask(m[:]), ALU.mult))
                        for gr in range(2):
                            dve.wait_ge(dve_done[gr], c * DN + 1)
                            done(gr, dve.tensor_tensor(N1[:, gr, :, :], G[0:C, gr, :, 0:C], mask(g.up16[:]), ALU.mult))
                        for gr in range(2):
                            dve.wait_ge(dve_done[gr], c * DN + 5)
                            done(gr, dve.tensor_tensor(X[:, gr, :, :], N1[:, gr, :, :], mask(g.ident[0:C, 0:C]), ALU.add))
                        for d, p, n in ((6, 9, 2), (7, 11, 3), (8, 12, 0), (9, 15, 3), (10, 18, 2)):
                            for gr in range(2):
                                dve.wait_ge(pe_done[gr], c * PN + p)
                                dve.wait_ge(dve_done[gr], c * DN + d)
                                done(gr, dve.tensor_tensor(X[:, gr, :, :], X[:, gr, :, :], heads(bank(gr, n, C)), ALU.add))
                        for gr in range(2):
                            dve.wait_ge(pe_done[gr], c * PN + 22)
                            qs = slice(gr * 4, gr * 4 + 4)
                            d = heads(bank(gr, 2), P)
                            dve.tensor_tensor(tmp[0:C, qs, :], S[0:C, qs, :], d[0:C, :, 0:C], ALU.add)
                            done(gr, dve.tensor_tensor(tmp[C:P, qs, :], S[C:P, qs, :], d[C:P, :, C:P], ALU.add))
                        for gr in range(2):
                            qs = slice(gr * 4, gr * 4 + 4)
                            dve.wait_ge(dve_done[gr], c * DN + 12)
                            done(gr, dve.tensor_tensor(
                                S[:, qs, :], tmp[:, qs, :],
                                g.chunk_decay[:, qs, bass.ds(c, 1)].to_broadcast([P, 4, C]), ALU.mult))
                        for gr in range(2):
                            dve.wait_ge(pe_done[1 - gr], c * PN + 22)
                            done(gr, dve.memset(UV[0:C, gr * 4:gr * 4 + 4, :], 0.0))
                dve.wait_ge(state_turned, 1)
                dve.tensor_copy(srow[:].rearrange("p (a q) n -> p a (q n)", a=2), ps[0:C, 0:2, :]).then_inc(state_copied, 1)

            @block.gpsimd
            def _(pool):
                pool.wait_ge(state_copied, 1)
                pool.dma_start(g.new_wkv_prompt.rearrange("h i j -> i h j"),
                               srow[:].rearrange("p q (a j) -> p (q a) j", a=2)).then_inc(state_out, 16)
                pool.wait_ge(state_out, 16)


def stage_rwkv_sample(nc, g):
    with ExitStack() as ctx:
        S = ctx.enter_context(nc.sbuf_tensor("d_S", [P, 2, NPAIR, C], F32))
        vecs = ctx.enter_context(nc.sbuf_tensor("d_vecs", [P, 2, 5, NPAIR, C], F32))
        t = ctx.enter_context(nc.sbuf_tensor("d_t", [P, 2, NPAIR, C], F32))
        sa = ctx.enter_context(nc.sbuf_tensor("d_sa", [P, NPAIR], F32))
        state_in = [new_sem(nc, g, f"d_state_in{i}") for i in range(2)]
        vecs_in = [new_sem(nc, g, f"d_vecs_in{i}") for i in range(2)]
        chain = new_sem(nc, g, "d_chain")
        state_ready = new_sem(nc, g, "d_state_ready")
        y_ready = new_sem(nc, g, "d_y_ready")
        stored = [new_sem(nc, g, f"d_stored{i}") for i in range(2)]
        STEPS = 7
        rows = g.samp_rows.rearrange("(f b) (q a j) -> f b a q j", b=NB, a=2, j=C)
        wkv_in = g.state_wkv.rearrange("b (q a) i j -> b a i q j", a=2)
        wkv_out = g.new_wkv_sample.rearrange("b (q a) i j -> b a i q j", a=2)
        with nc.Block() as block:
            @block.sync
            def _(sp):
                for b in range(NB):
                    s = b % 2
                    if b >= 2:
                        sp.wait_ge(y_ready, b - 1)
                        sp.wait_ge(stored[s], 32 * (b // 2))
                    for a in range(2):
                        sp.dma_start(S[a * C:(a + 1) * C, s, :, :], wkv_in[b, a]).then_inc(state_in[s], 16)

            @block.scalar
            def _(act):
                for b in range(NB):
                    s = b % 2
                    if b >= 2:
                        act.wait_ge(y_ready, b - 1)
                    for a in range(2):
                        for f in range(5):
                            act.dma_start(vecs[a * C:(a + 1) * C, s, f, :, :],
                                          rows[f, b, a].unsqueeze(0).to_broadcast([C, NPAIR, C])).then_inc(vecs_in[s], 16)

            @block.gpsimd
            def _(pool):
                for b in range(NB):
                    s = b % 2
                    pool.wait_ge(state_ready, b + 1)
                    for a in range(2):
                        pool.dma_start(wkv_out[b, a], S[a * C:(a + 1) * C, s, :, :]).then_inc(stored[s], 16)
                for s in range(2):
                    pool.wait_ge(stored[s], 16 * NB)

            @block.vector
            def _(dve):
                step = Chain(dve, chain)
                for b in range(NB):
                    s = b % 2
                    dve.wait_ge(state_in[s], 32 * (b // 2 + 1))
                    dve.wait_ge(vecs_in[s], 160 * (b // 2 + 1))
                    st = S[:, s, :, :]
                    w, nkk, kka, kf, r = (vecs[:, s, f, :, :] for f in range(5))
                    t0, t1 = t[:, 0, :, :], t[:, 1, :, :]
                    step(dve.tensor_tensor(t0, st, nkk, ALU.mult))
                    step(dve.tensor_reduce(sa[:], t0, AX_X, ALU.add))
                    dve.tensor_tensor(st, st, w, ALU.mult)
                    dve.tensor_tensor(t0, kka, sa[:].unsqueeze(2).to_broadcast([P, NPAIR, C]), ALU.mult)
                    step(dve.tensor_tensor(t1, kf, g.v_samp[:, :, b:b + 1].to_broadcast([P, NPAIR, C]), ALU.mult))
                    step(dve.tensor_tensor(t0, t0, t1, ALU.add))
                    dve.tensor_tensor(st, st, t0, ALU.add).then_inc(state_ready, 1)
                    dve.wait_ge(state_ready, b + 1)
                    step(dve.tensor_tensor(t1, st, r, ALU.mult))
                    dve.tensor_reduce(g.y_t[:, :, SEQ + b:SEQ + b + 1].rearrange("p q a -> p (q a)"), t1, AX_X,
                                      ALU.add).then_inc(y_ready, 1)
                    dve.wait_ge(y_ready, b + 1)


def stage_rwkv_post(nc, g):
    HC = TC // 2
    with ExitStack() as ctx:
        yc = ctx.enter_context(nc.sbuf_tensor("e_yc", [P, TC], F32))
        sq = ctx.enter_context(nc.sbuf_tensor("e_sq", [P, TC], F32))
        rs = ctx.enter_context(nc.sbuf_tensor("e_rs", [P, TC], F32))
        ob = ctx.enter_context(nc.sbuf_tensor("e_ob", [P, 2, TC], F32))
        vec = ctx.enter_context(nc.sbuf_tensor("e_vec", [P, 2, NPAIR], F32))
        ps = ctx.enter_context(nc.psum_tensor("e_ps", [P, 4, 512], F32))
        vec_in, mean_done, yc_ready = (new_sem(nc, g, "e_" + n) for n in ("vec_in", "mean_done", "yc_ready"))
        sq_ready, var_done, ve_ready, root_ready = (new_sem(nc, g, "e_" + n) for n in
                                                    ("sq_ready", "var_done", "ve_ready", "root_ready"))
        chain, out_ready = new_sem(nc, g, "e_chain"), new_sem(nc, g, "e_out_ready")
        stored = [new_sem(nc, g, f"e_stored{i}") for i in range(2)]
        with nc.Block() as block:
            @block.sync
            def _(sp):
                with nc.allow_non_contiguous_dma(reason="one value to a partition"):
                    for j, v in enumerate((g.lnx_w, g.lnx_b)):
                        sp.dma_start(vec[:, j, :], v.rearrange("(q p) -> p q", p=P)).then_inc(vec_in, 16)
                for q in range(NPAIR):
                    sp.wait_ge(out_ready, q + 1)
                    sp.dma_start(g.mix_t[q * P:(q + 1) * P, :], ob[:, q % 2, :]).then_inc(stored[q % 2], 16)
                for s in range(2):
                    sp.wait_ge(stored[s], 16 * NPAIR // 2)

            @block.tensor
            def _(pe):
                for q in range(NPAIR):
                    if q:
                        pe.wait_ge(yc_ready, 2 * q)
                    for h in range(2):
                        last = pe.matmul(ps[:, h, 0:HC], g.blk64[:], g.y_t[:, q, h * HC:(h + 1) * HC], start=True, stop=True)
                    last.then_inc(mean_done, 1)
                    pe.wait_ge(sq_ready, q + 1)
                    if q:
                        pe.wait_ge(ve_ready, 2 * q)
                    for h in range(2):
                        last = pe.matmul(ps[:, 2 + h, 0:HC], g.blk64[:], sq[:, h * HC:(h + 1) * HC], start=True, stop=True)
                    last.then_inc(var_done, 1)

            @block.scalar
            def _(act):
                for q in range(NPAIR):
                    act.wait_ge(yc_ready, 2 * q + 2)
                    act.activation(sq[:], yc[:], ACT.Square).then_inc(sq_ready, 1)
                    act.wait_ge(ve_ready, 2 * q + 2)
                    act.activation(rs[:], rs[:], ACT.Sqrt).then_inc(root_ready, 1)

            @block.vector
            def _(dve):
                step = Chain(dve, chain)
                dve.wait_ge(vec_in, 32)
                for q in range(NPAIR):
                    dve.wait_ge(mean_done, q + 1)
                    for h in range(2):
                        w = slice(h * HC, (h + 1) * HC)
                        dve.scalar_tensor_tensor(out=yc[:, w], in0=ps[:, h, 0:HC], scalar=-1.0 / C, in1=g.y_t[:, q, w],
                                                 op0=ALU.mult, op1=ALU.add).then_inc(yc_ready, 1)
                    dve.wait_ge(var_done, q + 1)
                    for h in range(2):
                        dve.tensor_scalar(rs[:, h * HC:(h + 1) * HC], ps[:, 2 + h, 0:HC], 1.0 / C, 64e-5, ALU.mult,
                                          ALU.add).then_inc(ve_ready, 1)
                    dve.wait_ge(root_ready, q + 1)
                    step(dve.reciprocal(rs[:], rs[:]))
                    step(dve.tensor_tensor(yc[:], yc[:], rs[:], ALU.mult))
                    step(dve.tensor_scalar(yc[:], yc[:], vec[:, 0, q:q + 1], vec[:, 1, q:q + 1], ALU.mult, ALU.add))
                    step(dve.tensor_tensor(yc[:], yc[:], g.bonus_t[:, q, :], ALU.add))
                    if q >= 2:
                        dve.wait_ge(stored[q % 2], 16 * (q // 2))
                    dve.tensor_tensor(ob[:, q % 2, :], yc[:], g.gate_t[:, q, :], ALU.mult).then_inc(out_ready, 1)
                    dve.wait_ge(out_ready, q + 1)


def stage_compress(nc, g):
    JP = 8
    with ExitStack() as ctx:
        def sb(name, shape, dt=F32):
            return ctx.enter_context(nc.sbuf_tensor("m_" + name, shape, dt))

        def sem(name):
            return new_sem(nc, g, "m_" + name)

        w1 = sb("w1", [P, 2, JP, P])
        pe_in = sb("pe_in", [P, 2, JP, 2])
        w2 = sb("w2", [C, 2, C])
        pt = sb("pt", [P, NB * 2], I32)
        ptf = sb("ptf", [P, NB * 2])
        row = sb("row", [P, 1], I32)
        rowf = sb("rowf", [P, 1])
        grp = sb("grp", [P, 1], I32)
        grpf = sb("grpf", [P, 1])
        idx = sb("idx", [P, NB * 2], I32)
        idc = sb("idc", [P, 2], I32)
        kv = sb("kv", [P, 2, 16, 512])
        kvr = sb("kvr", [P, 2, 4, 16, C])
        tb = sb("tb", [P, 4, 512])
        part = sb("part", [P, 2, 4, 256])
        pes = sb("pes", [P, 2, 2])
        bias = sb("bias", [C, 2])
        hs = sb("hs", [C, 2, 4, 256])
        ko = sb("ko", [P, 2, 31])
        vo = sb("vo", [31, 256])
        ps = ctx.enter_context(nc.psum_tensor("m_ps", [P, 8, 512], F32))
        w_in, pt_in, chain, idx_ready, idc_ready = (sem(n) for n in ("w_in", "pt_in", "chain", "idx_ready", "idc_ready"))
        loaded = [sem("loaded0"), sem("loaded1")]
        arranged = [sem("arranged_k"), sem("arranged_v")]
        turned, dve_ev, act_ev, mm_done, part_ev = (sem(n) for n in ("turned", "dve_ev", "act_ev", "mm_done", "part_ev"))
        shifted, hid_ready, fin_done, fin_ev = (sem(n) for n in ("shifted", "hid_ready", "fin_done", "fin_ev"))
        pe_summed, pe_copied, bias_summed, bias_ready = (sem(n) for n in ("pe_summed", "pe_copied", "bias_summed", "bias_ready"))
        prompt_in, prompt_ready, prompt_out, iota_ready = (sem(n) for n in ("prompt_in", "prompt_ready", "prompt_out", "iota_ready"))
        cache = g.cache_cmp.rearrange("n (c r) w -> (n c) (r w)", r=16)
        T, EV, PA, F2 = 32, 16, 4, 2

        with nc.Block() as block:
            @block.sync
            def _(sp):
                for e in range(2):
                    for s in range(2):
                        sp.dma_start(w1[:, e, :, s * C:(s + 1) * C],
                                     g.phi_w1[e, s * 1024:(s + 1) * 1024].rearrange("(q p) f -> p q f", p=P)).then_inc(w_in, 16)
                    sp.dma_start(w2[:, e, :], g.phi_w2[e]).then_inc(w_in, 16)
                with nc.allow_non_contiguous_dma(reason="small tables"):
                    for e in range(2):
                        for s in range(2):
                            sp.dma_start(pe_in[:, e, :, s],
                                         g.phi_pe[e, s * 16:(s + 1) * 16].rearrange("(q a) d -> (a d) q", a=2)).then_inc(w_in, 16)
                    by_page = g.page_table.rearrange("b (h n) -> n (b h)", h=2)
                    for n in range(16):
                        sp.dma_start(pt[8 * n:8 * n + 8, :], by_page[n:n + 1, :].to_broadcast([8, 16])).then_inc(pt_in, 16)
                for e in range(2):
                    sp.wait_ge(arranged[e], 2 * NB - 1)
                sp.dma_start(kv[0:32, 0, :, :], g.kv_rows[0:SEQ, 0:512].rearrange("(c j) w -> c j w", j=16)).then_inc(prompt_in, 16)
                sp.wait_ge(prompt_ready, 2)
                sp.dma_start(g.kc_prompt.rearrange("(q p) c -> p q c", p=P), ko[:]).then_inc(prompt_out, 16)
                sp.dma_start(g.vc_prompt, vo[:]).then_inc(prompt_out, 16)
                sp.wait_ge(prompt_out, 32)

            def arrange(eng, i, half, e, w):
                if w == P:
                    eng.wait_ge(loaded[half], i * 16 + 16)
                else:
                    eng.wait_ge(prompt_in, 16)
                eng.wait_ge(turned, i * T + max(0, 8 * (2 * half + e - 1)))
                take_wait(g, eng)
                eng.tensor_copy(kvr[0:w, e], kv[0:w, half, :, e * 256:e * 256 + 256].rearrange(
                    "p j (h d) -> p h j d", h=4)).then_inc(arranged[e], 1)

            def evac_even(dve, i, n, w):
                dve.wait_ge(turned, i * T + n + 1)
                dve.wait_ge(mm_done, i * T + max(0, n - 3))
                dve.tensor_copy(tb[:, n % 4, 0:4 * w], ps[:, n % 4, 0:4 * w]).then_inc(dve_ev, 1)

            @block.gpsimd
            def _(pool):
                pool.iota(row[:], pattern=[[0, 1]], base=0, channel_multiplier=1).then_inc(iota_ready, 1)
                pool.wait_ge(idx_ready, 1)

                def load(col, h, n):
                    pool.tensor_copy(idc[:, h:h + 1], idx[:, bass.ds(col, 1)]).then_inc(idc_ready, 1)
                    pool.wait_ge(idc_ready, n)
                    take_wait(g, pool)
                    pool.indirect_dma_start(
                        out=kv[:, h, :, :].rearrange("p j w -> p (j w)"), out_offset=None, in_=cache,
                        in_offset=bass.IndirectOffsetOnAxis(ap=idc[:, h:h + 1], axis=0)).then_inc(loaded[h], 16)
                for h in range(2):
                    load(h, h, h + 1)
                with pool.Fori(0, NB - 1) as i:
                    for h in range(2):
                        arrange(pool, i, h, 1, P)
                        for e in range(2):
                            pool.wait_ge(arranged[e], i * 2 + h + 1)
                        load(i * 2 + 2 + h, h, i * 2 + 3 + h)
                for h in range(2):
                    arrange(pool, NB - 1, h, 1, P)
                arrange(pool, NB, 0, 1, 32)

            @block.tensor
            def _(pe):
                pe.wait_ge(w_in, 16 * 10)
                for e in range(2):
                    for q in range(JP):
                        last = pe.matmul(ps[:, 4 + e, 0:2], w1[:, e, q, :], pe_in[:, e, q, :], start=(q == 0), stop=(q == JP - 1))
                    last.then_inc(pe_summed, 1)
                pe.wait_ge(pe_copied, 2)
                for e in range(2):
                    for s in range(2):
                        last = pe.matmul(ps[0:C, 6 + e, 0:1], g.ident[:, s * C:(s + 1) * C], pes[:, e, s:s + 1],
                                         start=(s == 0), stop=(s == 1))
                    last.then_inc(bias_summed, 1)
                pe.wait_ge(bias_ready, 2)

                def batch(i, halves, w):
                    units = 2 * halves

                    def turn(n):
                        u, q = n // JP, n % JP
                        half, e = u // 2, u % 2
                        if q == 0:
                            pe.wait_ge(arranged[e], i * 2 + half + 1)
                        if n < 2:
                            pe.wait_ge(fin_ev, i * F2)
                        if n % 2 == 0:
                            pe.wait_ge(dve_ev, i * EV + max(0, n // 2 - 1))
                        else:
                            pe.wait_ge(act_ev, i * EV + max(0, n // 2 - 1))
                        for h in range(4):
                            last = pe.transpose(ps[:, n % 4, h * w:(h + 1) * w],
                                                kvr[0:w, e, h, 2 * q:2 * q + 2, :].rearrange("p j d -> p (j d)"),
                                                g.ident[0:w, 0:w])
                        last.then_inc(turned, 1)

                    def mult(n):
                        u, q = n // JP, n % JP
                        e = u % 2
                        pe.wait_ge(dve_ev if n % 2 == 0 else act_ev, i * EV + n // 2 + 1)
                        if q == 0:
                            pe.wait_ge(part_ev, i * PA + max(0, u - 1))
                        pe.matmul(ps[:, 4 + u % 2, 0:4 * w], w1[:, e, q, :], tb[:, n % 4, 0:4 * w], start=(q == 0),
                                  stop=(q == JP - 1)).then_inc(mm_done, 1)

                    turn(0)
                    for n in range(1, JP * units):
                        turn(n)
                        mult(n - 1)
                    mult(JP * units - 1)
                    pe.wait_ge(part_ev, i * PA + units)
                    nc_ = w * halves - 1
                    for e in range(2):
                        pe.wait_ge(hid_ready, i * F2 + e)
                        take_wait(g, pe)
                        for hh in range(2):
                            for s in range(2):
                                last = pe.matmul(ps[0:C, 6 + hh, 0:2 * nc_], g.ident[:, s * C:(s + 1) * C],
                                                 part[:, e, 2 * hh:2 * hh + 2, s:s + nc_], start=(s == 0), stop=(s == 1))
                        last.then_inc(shifted, 1)
                    pe.wait_ge(hid_ready, i * F2 + 2)
                    take_wait(g, pe)
                    for h in range(4):
                        lo = (h % 2) * C
                        last = pe.matmul(ps[lo:lo + C, 0, (h // 2) * nc_:(h // 2 + 1) * nc_], w2[:, 0, :], hs[:, 0, h, 0:nc_],
                                         start=True, stop=True)
                    last.then_inc(fin_done, 1)
                    for t in range(halves):
                        m = min(w, nc_ - t * w)
                        for h in range(4):
                            last = pe.matmul(ps[0:m, 1, t * 256 + h * C:t * 256 + (h + 1) * C], hs[:, 1, h, t * w:t * w + m],
                                             w2[:, 1, :], start=True, stop=True)
                    last.then_inc(fin_done, 1)

                with pe.Fori(0, NB) as i:
                    batch(i, 2, P)
                batch(NB, 1, 32)

            @block.scalar
            def _(act):
                def batch(i, halves, w):
                    for n in range(1, JP * 2 * halves, 2):
                        act.wait_ge(turned, i * T + n + 1)
                        act.wait_ge(mm_done, i * T + max(0, n - 3))
                        act.copy(tb[:, n % 4, 0:4 * w], ps[:, n % 4, 0:4 * w]).then_inc(act_ev, 1)
                    nc_ = w * halves - 1
                    act.wait_ge(fin_done, i * F2)
                    for e in range(2):
                        act.wait_ge(shifted, i * F2 + e + 1)
                        for hh in range(2):
                            last = act.activation(hs[:, e, 2 * hh:2 * hh + 2, 0:nc_],
                                                  ps[0:C, 6 + hh, 0:2 * nc_].rearrange("p (h c) -> p h c", h=2),
                                                  ACT.Silu, bias=bias[:, e:e + 1])
                        last.then_inc(hid_ready, 1)
                act.wait_ge(bias_ready, 2)
                with act.Fori(0, NB) as i:
                    batch(i, 2, P)
                batch(NB, 1, 32)

            @block.vector
            def _(dve):
                step = Chain(dve, chain)
                dve.wait_ge(pt_in, 16 * 16)
                dve.wait_ge(iota_ready, 1)
                step(dve.tensor_scalar(grp[:], row[:], 7, None, ALU.bitwise_and))
                step(dve.tensor_copy(grpf[:], grp[:]))
                step(dve.tensor_copy(ptf[:], pt[:]))
                step(dve.tensor_scalar(ptf[:], ptf[:], 8.0, grpf[:, 0:1], ALU.mult, ALU.add))
                dve.tensor_copy(idx[:], ptf[:]).then_inc(idx_ready, 1)
                for e in range(2):
                    dve.wait_ge(pe_summed, e + 1)
                    dve.tensor_copy(pes[:, e, :], ps[:, 4 + e, 0:2]).then_inc(pe_copied, 1)
                for e in range(2):
                    dve.wait_ge(bias_summed, e + 1)
                    dve.tensor_copy(bias[:, e:e + 1], ps[0:C, 6 + e, 0:1]).then_inc(bias_ready, 1)

                def batch(i, halves, w, last):
                    dve.wait_ge(shifted, i * F2)
                    for u in range(2 * halves):
                        half, e = u // 2, u % 2
                        if u == 0:
                            arrange(dve, i, 0, 0, w)
                        for n in range(u * JP, (u + 1) * JP, 2):
                            evac_even(dve, i, n, w)
                        dve.wait_ge(mm_done, i * T + (u + 1) * JP)
                        dve.tensor_copy(part[:, e, :, half * P:half * P + w],
                                        ps[:, 4 + u % 2, 0:4 * w].rearrange("p (h c) -> p h c", h=4)).then_inc(part_ev, 1)
                        if u == 0 and halves == 2:
                            arrange(dve, i, 1, 0, w)
                    nc_ = w * halves - 1
                    dve.wait_ge(fin_done, i * F2 + 1)
                    keys = ps[:, 0, 0:2 * nc_].rearrange("p (h c) -> p h c", h=2)
                    if last:
                        dve.tensor_copy(ko[:], keys).then_inc(prompt_ready, 1)
                        dve.wait_ge(fin_done, i * F2 + 2)
                        dve.tensor_copy(vo[:], ps[0:31, 1, 0:256]).then_inc(prompt_ready, 1)
                    else:
                        dve.tensor_copy(g.kc[:, bass.ds(i * 2, 2), :], keys).then_inc(fin_ev, 1)
                        dve.wait_ge(fin_done, i * F2 + 2)
                        v = g.vc[:, bass.ds(i, 1), :].rearrange("p a n -> p (a n)")
                        dve.tensor_copy(v[:, 0:256], ps[:, 1, 0:256])
                        dve.tensor_copy(v[0:P - 1, 256:512], ps[0:P - 1, 1, 256:512]).then_inc(fin_ev, 1)

                with dve.Fori(0, NB) as i:
                    batch(i, 2, P, False)
                batch(NB, 1, 32, True)


def stage_nsa_sample(nc, g):
    PG = 32
    NQD = PG // 4
    NC = 255
    with ExitStack() as ctx:
        def sb(name, shape, dt=F32):
            return ctx.enter_context(nc.sbuf_tensor("b_" + name, shape, dt))

        def sem(name):
            return new_sem(nc, g, "b_" + name)

        qs = sb("qs", [P, 2, 4, NB])
        qz = sb("qz", [P, NB * 272])
        kvn = sb("kvn", [NB, 1536])
        knT = sb("knT", [P, 2, NB])
        gts = sb("gts", [P, 3])
        pages = sb("pages", [P, NB * PG], I32)
        pagef = sb("pagef", [P, NB * PG])
        prow = sb("prow", [P, 1], I32)
        prowf = sb("prowf", [P, 1])
        idx = [sb("idx_k", [P, NB * PG], I32), sb("idx_v", [P, NB * PG], I32)]
        idc = sb("idc", [P, 4, 4], I32)
        bsel = sb("bsel", [P, NB])
        zero = sb("zero", [P, P])
        pc = sb("pc", [P, 256])
        imp = sb("imp", [P, 260])
        score = sb("score", [P, 65])
        best = sb("best", [P, 8])
        off = sb("off", [P, 65])
        kbuf = sb("kbuf", [P, 4, 4, 256])
        kT = sb("kT", [P, 2, 2, 512])
        sl = sb("sl", [P, PG * P + 1])
        sw = sb("sw", [P, 512])
        pTs = sb("pTs", [P, PG, P])
        pTw = sb("pTw", [P, 4, P])
        pTc = sb("pTc", [P, 2, P])
        st = sb("st", [P, 3, 4])
        diag = sb("diag", [P, P])
        pn = sb("pn", [NB, P])
        os_ = sb("os", [P, 2, 4, NB])
        ps = ctx.enter_context(nc.psum_tensor("b_ps", [P, 8, 512], F32))
        in_done, made, chain, idx_ready, idc_ready, qz_ready = (sem(n) for n in (
            "in_done", "made", "chain", "idx_ready", "idc_ready", "qz_ready"))
        cmp_done, nmax_ready, exp_done, pc_ready, imp_done, off_ready = (sem(n) for n in (
            "cmp_done", "nmax_ready", "exp_done", "pc_ready", "imp_done", "off_ready"))
        kloaded = [sem(f"kloaded{s}") for s in range(4)]
        vloaded = [sem(f"vloaded{s}") for s in range(4)]
        kwin = [sem(f"kwin{s}") for s in range(4)]
        vwin = [sem(f"vwin{s}") for s in range(4)]
        kturned, kev_d, kev_a, kmm, score_ev, vmm = (sem(n) for n in ("kturned", "kev_d", "kev_a", "kmm", "score_ev", "vmm"))
        kn_turned, kn_copied, sn_done = sem("kn_turned"), sem("kn_copied"), sem("sn_done")
        p_ready, pt_turned, pt_copied, diag_ready, pn_done, pn_copied = (sem(n) for n in (
            "p_ready", "pt_turned", "pt_copied", "diag_ready", "pn_done", "pn_copied"))
        o_done, os_ready, out_done = sem("o_done"), sem("os_ready"), sem("out_done")
        cache = g.cache_slc.rearrange("n r (k w) -> (n r k) w", k=2)
        heads = g.proj_t[R_COLS:KV0, SEQ:TC].rearrange("(h a g d) b -> a d h g b", h=2, a=2, g=4)
        mix_heads = g.mix_t[D_R:D, SEQ:TC].rearrange("(h a g d) b -> a d h g b", h=2, a=2, g=4)
        NW = NQD * NB

        def window(eng, b, slot, loaded, kv):
            w = slice(kv * 256, kv * 256 + 256)
            eng.dma_start(kbuf[:, slot, 0:3, :], g.cache_win[b, 1:385, w].rearrange("(t p) n -> p t n", p=P)).then_inc(loaded, 16)
            eng.dma_start(kbuf[0:P - 1, slot, 3, :], g.cache_win[b, 385:512, w]).then_inc(loaded, 16)
            eng.dma_start(kbuf[P - 1:P, slot, 3, :], g.kv_rows[SEQ + b:SEQ + b + 1, 1024 + kv * 256:1280 + kv * 256]).then_inc(loaded, 16)

        with nc.Block() as block:
            @block.sync
            def _(sp):
                with nc.allow_non_contiguous_dma(reason="small tables"):
                    for a in range(2):
                        for h in range(2):
                            sp.dma_start(qs[a * C:(a + 1) * C, h, :, :], heads[a, :, h]).then_inc(in_done, 16)
                    for b in range(NB):
                        sp.dma_start(gts[16 * b:16 * b + 16, :], g.gates[SEQ + b].rearrange("(r m) -> m r", r=3)).then_inc(in_done, 16)
                    sp.dma_start(pages[:], g.page_table.rearrange("(o b) n -> o (b n)", o=1).to_broadcast([P, NB * PG])).then_inc(in_done, 16)
                    sp.dma_start(kvn[:], g.kv_rows[SEQ:TC, :]).then_inc(in_done, 16)
                for b in range(NB):
                    sp.wait_ge(kturned, 2 * (NW + b - 3))
                    window(sp, b, b % 4, kwin[b % 4], 0)
                for b in range(NB):
                    sp.wait_ge(vmm, NW + b - 3)
                    window(sp, b, b % 4, vwin[b % 4], 1)
                sp.wait_ge(os_ready, 2)
                for a in range(2):
                    for h in range(2):
                        sp.dma_start(mix_heads[a, :, h], os_[a * C:(a + 1) * C, h, :, :]).then_inc(out_done, 16)
                sp.wait_ge(out_done, 64)

            @block.gpsimd
            def _(pool):
                step = Chain(pool, made)
                step(pool.iota(prow[:], pattern=[[0, 1]], base=0, channel_multiplier=1))
                step(pool.memset(zero[:], 0.0))
                step(pool.memset(qz[:], 0.0))
                step(pool.memset(bsel[:], 1.0))
                step(pool.affine_select(out=bsel[:], in_=bsel[:], compare_op=ALU.is_ge, fill=0.0, base=0,
                                        pattern=[[-16, NB]], channel_multiplier=1))
                step(pool.affine_select(out=bsel[:], in_=bsel[:], compare_op=ALU.is_ge, fill=0.0, base=15,
                                        pattern=[[16, NB]], channel_multiplier=-1))
                step(pool.memset(imp[:], 0.0))
                pool.wait_ge(idx_ready, 2)

                def load(quad, b, kv, loaded):
                    s = b % 4
                    pool.tensor_copy(idc[:, s, :], idx[kv][:, bass.ds(quad * 4 + b * PG, 4)]).then_inc(idc_ready, 1)
                    pool.wait_ge(idc_ready, quad * NB + (kv * NW + b + 1))
                    take_wait(g, pool)
                    for n in range(4):
                        pool.indirect_dma_start(
                            out=kbuf[:, s, n, :], out_offset=None, in_=cache,
                            in_offset=bass.IndirectOffsetOnAxis(ap=idc[:, s, n:n + 1], axis=0)).then_inc(loaded[s], 16)

                def stream(kv, loaded, free, per, base):
                    for b in range(4):
                        load(0, b, kv, loaded)
                    with pool.Fori(0, NQD - 1) as i:
                        for b in range(NB):
                            pool.wait_ge(free, i * (NB * per) + (b + 1) * per)
                            load(i if b < 4 else i + 1, (b + 4) % NB, kv, loaded)
                    for b in range(4, NB):
                        pool.wait_ge(free, ((NQD - 1) * NB + b - 3) * per)
                        load(NQD - 1, b, kv, loaded)
                stream(0, kloaded, kturned, 2, 0)
                pool.wait_ge(kturned, 2 * (NW + NB))
                stream(1, vloaded, vmm, 1, 0)

            @block.tensor
            def _(pe):
                pe.wait_ge(qz_ready, 2)
                for b in range(NB):
                    for h in range(2):
                        last = pe.matmul(ps[:, 5, 0:NC], qz[:, b * 256 + h * P:b * 256 + (h + 1) * P], g.kc[:, 2 * b + h, :],
                                         start=(b + h == 0), stop=(b + h == NB))
                last.then_inc(cmp_done, 1)
                for h in range(2):
                    last = pe.transpose(ps[:, 7, h * NB:(h + 1) * NB], kvn[:, 512 + h * P:512 + (h + 1) * P], g.ident[0:NB, 0:NB])
                last.then_inc(kn_turned, 1)
                pe.wait_ge(kn_copied, 1)
                for b in range(NB):
                    for h in range(2):
                        last = pe.matmul(ps[:, 7, 0:1], qz[:, b * 256 + h * P:b * 256 + (h + 1) * P], knT[:, h, b:b + 1],
                                         start=(b + h == 0), stop=(b + h == NB))
                last.then_inc(sn_done, 1)
                pe.wait_ge(pc_ready, 1)
                pe.matmul(ps[:, 5, 0:NC], g.blk4[:], pc[:, 0:NC], start=True, stop=True).then_inc(imp_done, 1)

                def quad(i, loaded, uses):
                    def turn(b):
                        pe.wait_ge(loaded[b % 4], uses(b))
                        pe.wait_ge(kev_d, i * NB + max(0, b - 1))
                        pe.wait_ge(kev_a, i * NB + max(0, b - 1))
                        for h in range(2):
                            for n in range(4):
                                last = pe.transpose(ps[:, 2 * (b % 2) + h, n * P:(n + 1) * P],
                                                    kbuf[:, b % 4, n, h * P:(h + 1) * P], g.ident[:])
                            last.then_inc(kturned, 1)

                    def mult(b):
                        pe.wait_ge(kev_d, i * NB + b + 1)
                        pe.wait_ge(kev_a, i * NB + b + 1)
                        if b == 0:
                            pe.wait_ge(score_ev, i)
                        for h in range(2):
                            last = pe.matmul(ps[:, 4, :], qz[:, b * 256 + h * P:b * 256 + (h + 1) * P], kT[:, b % 2, h, :],
                                             start=(b + h == 0), stop=(b + h == NB))
                        last.then_inc(kmm, 1)
                    turn(0)
                    for b in range(1, NB):
                        turn(b)
                        mult(b - 1)
                    mult(NB - 1)

                with pe.Fori(0, NQD) as i:
                    quad(i, kloaded, lambda b: i * 128 + 64 * (b // 4 + 1))
                quad(NQD, kwin, lambda b: 48 * (b // 4 + 1))
                pe.wait_ge(score_ev, NQD + 1)
                pe.wait_ge(p_ready, 1)
                pe.transpose(ps[:, 0, 0:P], pc[:, 0:P], g.ident[:])
                pe.transpose(ps[0:P - 1, 0, P:2 * P], pc[:, P:NC], g.ident[:]).then_inc(pt_turned, 1)
                pe.wait_ge(p_ready, 2)
                for n in range(4):
                    last = pe.transpose(ps[:, 1, n * P:(n + 1) * P], sw[:, n * P:(n + 1) * P], g.ident[:])
                last.then_inc(pt_turned, 1)
                pe.wait_ge(p_ready, 3)
                for q in range(NQD):
                    if q >= 2:
                        pe.wait_ge(pt_copied, q + 1)
                    for n in range(4):
                        last = pe.transpose(ps[:, 2 + q % 2, n * P:(n + 1) * P], sl[:, (4 * q + n) * P:(4 * q + n + 1) * P], g.ident[:])
                    last.then_inc(pt_turned, 1)
                pe.wait_ge(diag_ready, 1)
                pe.matmul(ps[0:NB, 5, 0:P], bsel[:], diag[:], start=True, stop=True).then_inc(pn_done, 1)
                out = ps[:, 6, 0:P]
                pe.matmul(out, zero[:], g.ident[:], start=True, stop=False, skip_group_check=True)
                pe.wait_ge(pn_copied, 1)
                for h in range(2):
                    pe.matmul(out.rearrange("p (b h m) -> p b h m", b=NB, h=2)[:, :, h, :], kvn[:, 768 + h * P:768 + (h + 1) * P],
                              pn[:].rearrange("p (b h m) -> p b h m", b=NB, h=2)[:, :, h, :], start=False, stop=False,
                              skip_group_check=True)
                pe.wait_ge(pt_copied, NQD + 2)
                for b in range(NB):
                    for t in range(2):
                        m = P - t
                        for h in range(2):
                            cols = slice(b * 16 + h * 8, b * 16 + h * 8 + 8)
                            pe.matmul(out[:, cols], g.vc[0:m, b, t * 256 + h * P:t * 256 + (h + 1) * P], pTc[0:m, t, cols],
                                      start=False, stop=False, skip_group_check=True)

                def values(loaded, uses, probs):
                    for b in range(NB):
                        pe.wait_ge(loaded[b % 4], uses(b))
                        for n in range(4):
                            for h in range(2):
                                cols = slice(b * 16 + h * 8, b * 16 + h * 8 + 8)
                                last = pe.matmul(out[:, cols], kbuf[:, b % 4, n, h * P:(h + 1) * P], probs(n)[:, cols],
                                                 start=False, stop=False, skip_group_check=True)
                        last.then_inc(vmm, 1)
                    return last

                with pe.Fori(0, NQD) as i:
                    values(vloaded, lambda b: i * 128 + 64 * (b // 4 + 1),
                           lambda n: pTs[:, bass.ds(i * 4 + n, 1), :].rearrange("p a m -> p (a m)"))
                values(vwin, lambda b: 48 * (b // 4 + 1), lambda n: pTw[:, n, :])

            @block.scalar
            def _(act):
                act.wait_ge(nmax_ready, 1)
                act.activation(pc[:, 0:NC], ps[:, 5, 0:NC], ACT.Exp, bias=st[:, 0, 1:2], accum_out=st[:, 0, 2:3]).then_inc(exp_done, 1)
                with act.Fori(0, NQD + 1) as i:
                    for b in range(NB):
                        act.wait_ge(kturned, i * 16 + 2 * b + 2)
                        act.wait_ge(kmm, i * NB + max(0, b - 1))
                        act.copy(kT[:, b % 2, 1, :], ps[:, 2 * (b % 2) + 1, :]).then_inc(kev_a, 1)
                act.wait_ge(nmax_ready, 2)
                act.activation(sw[:], sw[:], ACT.Exp, bias=st[:, 2, 1:2], accum_out=st[:, 2, 2:3]).then_inc(exp_done, 1)
                act.wait_ge(nmax_ready, 3)
                act.activation(sl[:], sl[:], ACT.Exp, bias=st[:, 1, 1:2], accum_out=st[:, 1, 2:3]).then_inc(exp_done, 1)

            @block.vector
            def _(dve):
                step = Chain(dve, chain)
                dve.wait_ge(in_done, 16 * 14)
                dve.wait_ge(made, 7)
                step(dve.tensor_copy(prowf[:], prow[:]))
                step(dve.tensor_scalar(prowf[:], prowf[:], 2.0, None, ALU.mult))
                step(dve.tensor_copy(pagef[:], pages[:]))
                step(dve.tensor_scalar(pagef[:], pagef[:], 256.0, prowf[:, 0:1], ALU.mult, ALU.add))
                dve.tensor_copy(idx[0][:], pagef[:]).then_inc(idx_ready, 1)
                dve.tensor_scalar(idx[1][:], pagef[:], 1.0, None, ALU.add).then_inc(idx_ready, 1)
                for a in range(2):
                    dst = qz[a * C:(a + 1) * C, :].rearrange("p (b h y) -> p b h y", b=NB, h=2)[:, :, :, 4 * a:4 * a + 4]
                    dve.tensor_scalar(dst, qs[a * C:(a + 1) * C].rearrange("p h g b -> p b h g"), 0.125, None,
                                      ALU.mult).then_inc(qz_ready, 1)

                def negmax(br, scores):
                    step(dve.reduce_max(st[:, br, 0:1], scores, AX_X))
                    dve.tensor_scalar(st[:, br, 1:2], st[:, br, 0:1], -1.0, None, ALU.mult).then_inc(nmax_ready, 1)

                def factor(br):
                    step(dve.tensor_scalar(st[:, br, 3:4], st[:, br, 2:3], 1e-30, None, ALU.max))
                    step(dve.reciprocal(st[:, br, 3:4], st[:, br, 3:4]))

                dve.wait_ge(cmp_done, 1)
                negmax(0, ps[:, 5, 0:NC])
                dve.wait_ge(kn_turned, 1)
                dve.tensor_copy(knT[:].rearrange("p h b -> p (h b)"), ps[:, 7, 0:2 * NB]).then_inc(kn_copied, 1)
                dve.wait_ge(exp_done, 1)
                factor(0)
                dve.tensor_scalar(pc[:, 0:NC], pc[:, 0:NC], st[:, 0, 3:4], None, ALU.mult).then_inc(pc_ready, 1)
                dve.wait_ge(imp_done, 1)
                step(dve.tensor_copy(imp[:, 1:NC + 1], ps[:, 5, 0:NC]))
                taps = [imp[:, n:n + 256].rearrange("p (s f) -> p s f", f=4)[:, :, 0] for n in range(5)]
                step(dve.tensor_tensor(score[:, 0:64], taps[0], taps[1], ALU.add))
                for n in range(2, 5):
                    step(dve.tensor_tensor(score[:, 0:64], score[:, 0:64], taps[n], ALU.add))
                step(dve.memset(score[:, 0:1], -NEG))
                step(dve.memset(score[:, 63:65], -NEG))
                for n in range(2):
                    step(dve.max(best[:], score[:]))
                    step(dve.match_replace(score[:], best[:], score[:], -1.0))
                dve.tensor_scalar(off[:], score[:], 0.0, NEG, ALU.is_ge, ALU.mult).then_inc(off_ready, 1)
                dve.tensor_scalar(pc[:, 0:NC], pc[:, 0:NC], gts[:, 0:1], None, ALU.mult).then_inc(p_ready, 1)
                dve.wait_ge(off_ready, 1)
                dve.wait_ge(sn_done, 1)
                step(dve.tensor_copy(sl[:, PG * P:PG * P + 1], ps[:, 7, 0:1]))

                def evac(i):
                    for b in range(NB):
                        dve.wait_ge(kturned, i * 16 + 2 * b + 1)
                        dve.wait_ge(kmm, i * NB + max(0, b - 1))
                        dve.tensor_copy(kT[:, b % 2, 0, :], ps[:, 2 * (b % 2), :]).then_inc(kev_d, 1)
                    dve.wait_ge(kmm, i * NB + NB)
                with dve.Fori(0, NQD) as i:
                    evac(i)
                    dve.tensor_tensor(sl[:, bass.ds(i * 512, 512)].rearrange("p (s r) -> p s r", r=64),
                                      ps[:, 4, :].rearrange("p (s r) -> p s r", r=64),
                                      off[:, bass.ds(i * 8, 8)].unsqueeze(2).to_broadcast([P, 8, 64]),
                                      ALU.add).then_inc(score_ev, 1)
                evac(NQD)
                dve.tensor_copy(sw[:], ps[:, 4, :]).then_inc(score_ev, 1)
                dve.wait_ge(score_ev, NQD + 1)
                negmax(2, sw[:])
                negmax(1, sl[:])
                for n, (br, t) in enumerate(((2, sw), (1, sl))):
                    dve.wait_ge(exp_done, n + 2)
                    factor(br)
                    step(dve.tensor_tensor(st[:, br, 3:4], st[:, br, 3:4], gts[:, br:br + 1], ALU.mult))
                    dve.tensor_scalar(t[:], t[:], st[:, br, 3:4], None, ALU.mult).then_inc(p_ready, 1)
                dve.wait_ge(p_ready, 3)
                dve.tensor_scalar(diag[:], g.ident[:], sl[:, PG * P:PG * P + 1], None, ALU.mult).then_inc(diag_ready, 1)
                dve.wait_ge(pt_turned, 1)
                dve.tensor_copy(pTc[:, 0, :], ps[:, 0, 0:P])
                dve.tensor_copy(pTc[0:P - 1, 1, :], ps[0:P - 1, 0, P:2 * P]).then_inc(pt_copied, 1)
                dve.wait_ge(pt_turned, 2)
                dve.tensor_copy(pTw[:].rearrange("p n m -> p (n m)"), ps[:, 1, :]).then_inc(pt_copied, 1)
                for q in range(NQD):
                    dve.wait_ge(pt_turned, q + 3)
                    dve.tensor_copy(pTs[:, 4 * q:4 * q + 4, :].rearrange("p n m -> p (n m)"), ps[:, 2 + q % 2, :]).then_inc(pt_copied, 1)
                dve.wait_ge(pn_done, 1)
                dve.tensor_copy(pn[:], ps[0:NB, 5, 0:P]).then_inc(pn_copied, 1)
                dve.wait_ge(vmm, NW + NB)
                for a in range(2):
                    src = ps[a * C:(a + 1) * C, 6, 0:P].rearrange("p (b h a g) -> p a h g b", b=NB, h=2, a=2)[:, a]
                    dve.tensor_copy(os_[a * C:(a + 1) * C], src).then_inc(os_ready, 1)


def stage_nsa_prompt(nc, g):
    NQ = SEQ // P
    NC = SEQ // 16 - 1
    units = [(t, br, q) for t in range(NQ) for br in range(3) for q in range(4)]
    NU = len(units)
    SCALE = 0.125
    with ExitStack() as ctx:
        def sb(name, shape):
            return ctx.enter_context(nc.sbuf_tensor("a_" + name, shape, F32))

        def sem(name):
            return new_sem(nc, g, "a_" + name)

        qT = sb("qT", [C, 4, SEQ])
        rows = sb("rows", [P, NQ, 4, C])
        kT = sb("kT", [C, 2, SEQ])
        kcT = sb("kcT", [C, NC])
        vc = sb("vc", [NC, C])
        gates = sb("gates", [P, NQ, 48])
        causal = sb("causal", [P, P])
        cmask = sb("cmask", [P, NQ, NC])
        pr = sb("pr", [P, 3, SEQ])
        pT = sb("pT", [P, 3, SEQ])
        mx = sb("mx", [P, NU])
        nm = sb("nm", [P, NU])
        sums = sb("sums", [P, NU])
        fac = sb("fac", [P, NU])
        acc = sb("acc", [P, NQ, 4, C])
        tmp = sb("tmp", [P, 4, C])
        mo = sb("mo", [P, 2, SEQ])
        ps = ctx.enter_context(nc.psum_tensor("a_ps", [P, 8, 512], F32))
        gates_in, masks_ready, mask_step, head_in, k_turned, k_copied = (sem(n) for n in (
            "gates_in", "masks_ready", "mask_step", "head_in", "k_turned", "k_copied"))
        s_done, max_done, nm_done, e_done, t_done, ptd, pta, o_done = (sem(n) for n in (
            "s_done", "max_done", "nm_done", "e_done", "t_done", "pt_dve", "pt_act", "o_done"))
        chain, comb_done, mix_turned, mix_copied, stored = (sem(n) for n in (
            "chain", "comb_done", "mix_turned", "mix_copied", "stored"))
        fac_done, tmp_done = sem("fac_done"), sem("tmp_done")
        GR = NU // 4
        CH = 2 * GR

        def width(t, br):
            return NC if br == 0 else (t + 1) * P

        def blocks(t, br):
            return [(0, NC)] if br == 0 else [(j * P, P) for j in range(t + 1)]

        with nc.Block() as block:
            @block.sync
            def _(sp):
                sp.dma_start(gates[:], g.gates[0:SEQ].rearrange("(t p) n -> p t n", p=P)).then_inc(gates_in, 16)
                with sp.Fori(0, 4) as i:
                    sp.wait_ge(o_done, i * NU)
                    for q in range(4):
                        sp.dma_start(qT[:, q, :], g.proj_t[bass.ds(i * 256 + R_COLS + q * C, C), 0:SEQ]).then_inc(head_in, 16)
                    for j in range(4):
                        sp.dma_start(rows[:, :, j, :], g.kv_rows[0:SEQ, bass.ds(i * C + 512 + j * 256, C)].rearrange(
                            "(t p) d -> p t d", p=P)).then_inc(head_in, 16)
                    sp.dma_start(kcT[:], g.kc_prompt[bass.ds(i * C, C), :]).then_inc(head_in, 16)
                    sp.dma_start(vc[:], g.vc_prompt[:, bass.ds(i * C, C)]).then_inc(head_in, 16)

            @block.gpsimd
            def _(pool):
                step = Chain(pool, mask_step)
                step(pool.memset(causal[:], 0.0))
                step(pool.memset(cmask[:], 0.0))
                step(pool.affine_select(out=causal[:], in_=causal[:], compare_op=ALU.is_ge, fill=NEG, base=0,
                                        pattern=[[-1, P]], channel_multiplier=1))
                pool.affine_select(out=cmask[:], in_=cmask[:], compare_op=ALU.is_ge, fill=NEG, base=-31,
                                   pattern=[[P, NQ], [-16, NC]], channel_multiplier=1).then_inc(masks_ready, 1)
                with pool.Fori(0, 4) as i:
                    pool.wait_ge(mix_copied, i * 2 + 2)
                    pool.dma_start(g.mix_t[bass.ds(i * 256 + D_R, 256), 0:SEQ].rearrange("(a p) t -> p a t", p=P),
                                   mo[:]).then_inc(stored, 16)
                for c, dst in enumerate((g.new_cmp_prompt, g.new_slc_prompt, g.new_win_prompt)):
                    pool.dma_start(dst, g.kv_rows[0:SEQ, c * 512:(c + 1) * 512]).then_inc(stored, 16)
                for c, dst in enumerate((g.new_cmp_sample, g.new_slc_sample)):
                    pool.dma_start(dst, g.kv_rows[SEQ:TC, c * 512:(c + 1) * 512]).then_inc(stored, 16)
                pool.dma_start(g.new_win_sample[:, SEQ - 1, :], g.kv_rows[SEQ:TC, 1024:1536]).then_inc(stored, 16)
                pool.dma_start(g.new_win_sample[:, 0:SEQ - 1, :], g.cache_win[:, 1:SEQ, :]).then_inc(stored, 16)
                pool.wait_ge(stored, 16 * 11)

            @block.tensor
            def _(pe):
                pe.wait_ge(masks_ready, 1)
                with pe.Fori(0, 4) as i:
                    pe.wait_ge(head_in, i * 160 + 160)
                    pe.wait_ge(mix_copied, i * 2)
                    for j in range(2):
                        pe.wait_ge(k_copied, i * 2 + j)
                        take_wait(g, pe)
                        for t in range(NQ):
                            last = pe.transpose(ps[0:C, 7, t * P:(t + 1) * P], rows[:, t, 2 * j, :], g.ident[:])
                        last.then_inc(k_turned, 1)

                    def scores(u):
                        t, br, q = units[u]
                        if u == 0:
                            pe.wait_ge(k_copied, i * 2 + 2)
                        pe.wait_ge(e_done, i * NU + max(0, u - 2))
                        out = ps[:, u % 3, 0:width(t, br)]
                        query = qT[:, q, t * P:(t + 1) * P]
                        if br == 0:
                            pe.matmul(out, query, kcT[:], start=True, stop=False)
                            last = pe.matmul(out, g.ident[:], cmask[:, t, :], start=False, stop=True)
                        else:
                            own = slice(t * P, (t + 1) * P)
                            if t:
                                pe.matmul(out[:, 0:t * P], query, kT[:, br - 1, 0:t * P], start=True, stop=True)
                            pe.matmul(out[:, own], query, kT[:, br - 1, own], start=True, stop=False)
                            last = pe.matmul(out[:, own], g.ident[:], causal[:], start=False, stop=True)
                        last.then_inc(s_done, 1)

                    def turn(u):
                        t, br, q = units[u]
                        pe.wait_ge(e_done, i * NU + u + 1)
                        pe.wait_ge(ptd if u % 2 == 0 else pta, i * (NU // 2) + max(0, u // 2))
                        for a, w in blocks(t, br):
                            last = pe.transpose(ps[0:w, 3 + u % 2, a:a + P], pr[:, u % 3, a:a + w], g.ident[:])
                        last.then_inc(t_done, 1)

                    def out(u):
                        t, br, q = units[u]
                        gr = u // 4
                        pe.wait_ge(ptd if u % 2 == 0 else pta, i * (NU // 2) + u // 2 + 1)
                        if q == 0:
                            pe.wait_ge(comb_done, i * GR + max(0, gr - 1))
                        bl = blocks(t, br)
                        for n, (a, w) in enumerate(bl):
                            v = vc[:] if br == 0 else rows[:, a // P, 2 * br - 1, :]
                            last = pe.matmul(ps[:, 5 + gr % 2, q * C:(q + 1) * C], pT[0:w, u % 3, a:a + P], v,
                                             start=(n == 0), stop=(n == len(bl) - 1))
                        last.then_inc(o_done, 1)

                    for n in range(NU + 3):
                        if n < NU:
                            scores(n)
                        if 0 <= n - 2 < NU:
                            turn(n - 2)
                        if 0 <= n - 3 < NU:
                            out(n - 3)
                    pe.wait_ge(comb_done, i * GR + GR)
                    for a in range(2):
                        pe.wait_ge(mix_copied, i * 2 + a)
                        for t in range(NQ):
                            last = pe.transpose(ps[:, 7, t * P:(t + 1) * P],
                                                acc[:, t, 2 * a:2 * a + 2, :].rearrange("p q d -> p (q d)"), g.ident[:])
                        last.then_inc(mix_turned, 1)

            @block.scalar
            def _(act):
                with act.Fori(0, 4) as i:
                    for n in range(NU + 2):
                        if n < NU:
                            t, br, q = units[n]
                            w = width(t, br)
                            act.wait_ge(nm_done, i * NU + n + 1)
                            act.wait_ge(t_done, i * NU + max(0, n - 2))
                            if n == 0:
                                act.wait_ge(comb_done, i * GR)
                            act.activation(pr[:, n % 3, 0:w], ps[:, n % 3, 0:w], ACT.Exp, bias=nm[:, n:n + 1], scale=SCALE,
                                           accum_out=sums[:, n:n + 1]).then_inc(e_done, 1)
                        u = n - 2
                        if u >= 0 and u % 2 == 1:
                            t, br, q = units[u]
                            act.wait_ge(t_done, i * NU + u + 1)
                            act.wait_ge(o_done, i * NU + max(0, u - 2))
                            w = NC if br == 0 else P
                            act.copy(pT[0:w, u % 3, 0:(P if br == 0 else width(t, br))],
                                     ps[0:w, 3 + u % 2, 0:(P if br == 0 else width(t, br))]).then_inc(pta, 1)

            @block.vector
            def _(dve):
                dve.wait_ge(gates_in, 16)
                with dve.Fori(0, 4) as i:
                    step = Chain(dve, chain, i * CH)
                    for j in range(2):
                        dve.wait_ge(k_turned, i * 2 + j + 1)
                        dve.tensor_copy(kT[:, j, :], ps[0:C, 7, :]).then_inc(k_copied, 1)
                    for n in range(NU + 4):
                        if n < NU:
                            t, br, q = units[n]
                            dve.wait_ge(s_done, i * NU + n + 1)
                            dve.reduce_max(mx[:, n:n + 1], ps[:, n % 3, 0:width(t, br)], AX_X).then_inc(max_done, 1)
                            dve.wait_ge(max_done, i * NU + n + 1)
                            dve.tensor_scalar(nm[:, n:n + 1], mx[:, n:n + 1], 0.1 * NEG, -SCALE, ALU.max,
                                              ALU.mult).then_inc(nm_done, 1)
                        u = n - 2
                        if 0 <= u < NU and u % 2 == 0:
                            t, br, q = units[u]
                            dve.wait_ge(t_done, i * NU + u + 1)
                            dve.wait_ge(o_done, i * NU + max(0, u - 2))
                            w = NC if br == 0 else P
                            dve.tensor_copy(pT[0:w, u % 3, 0:(P if br == 0 else width(t, br))],
                                            ps[0:w, 3 + u % 2, 0:(P if br == 0 else width(t, br))]).then_inc(ptd, 1)
                        u = n - 4
                        if u >= 0 and u % 4 == 3:
                            t, br, q = units[u]
                            us = slice(u - 3, u + 1)
                            dve.wait_ge(e_done, i * NU + u + 1)
                            step(dve.tensor_scalar(fac[:, us], sums[:, us], 1e-30, None, ALU.max))
                            step(dve.reciprocal(fac[:, us], fac[:, us]))
                            dve.tensor_tensor(fac[:, us], fac[:, us], gates[:, t, bass.ds(i * 4 + br * 16, 4)],
                                              ALU.mult).then_inc(fac_done, 1)
                            dve.wait_ge(fac_done, i * GR + u // 4 + 1)
                            dve.wait_ge(o_done, i * NU + u + 1)
                            if u == 3:
                                dve.wait_ge(mix_turned, i * 2)
                            ob = ps[:, 5 + (u // 4) % 2, 0:4 * C].rearrange("p (q d) -> p q d", q=4)
                            fb = fac[:, us].unsqueeze(2).to_broadcast([P, 4, C])
                            if br == 0:
                                dve.tensor_tensor(acc[:, t, :, :], ob, fb, ALU.mult).then_inc(comb_done, 1)
                            else:
                                dve.tensor_tensor(tmp[:], ob, fb, ALU.mult).then_inc(tmp_done, 1)
                                dve.wait_ge(tmp_done, i * (GR - NQ) + 2 * t + br)
                                dve.tensor_tensor(acc[:, t, :, :], acc[:, t, :, :], tmp[:], ALU.add).then_inc(comb_done, 1)
                            dve.wait_ge(comb_done, i * GR + u // 4 + 1)
                    assert step.n == CH
                    for a in range(2):
                        dve.wait_ge(mix_turned, i * 2 + a + 1)
                        dve.wait_ge(stored, i * 16)
                        dve.tensor_copy(mo[:, a, :], ps[:, 7, :]).then_inc(mix_copied, 1)


def stage_turn_x(nc, g):
    with ExitStack() as ctx:
        rows = ctx.enter_context(nc.sbuf_tensor("t_rows", [P, 2, D], F32))
        ps = ctx.enter_context(nc.psum_tensor("t_ps", [P, 4, 512], F32))
        loaded = [new_sem(nc, g, f"t_loaded{i}") for i in range(2)]
        turned = new_sem(nc, g, "t_turned")
        copied = new_sem(nc, g, "t_copied")
        srcs = [g.x_prompt[r:r + n, :] for r, n in ROW_TILES[:4]] + [g.x_sample]
        with nc.Block() as block:
            @block.sync
            def _(sp):
                for i, (r, n) in enumerate(ROW_TILES):
                    if i >= 2:
                        sp.wait_ge(turned, 4 * (i - 1))
                    sp.dma_start(rows[0:n, i % 2, :], srcs[i]).then_inc(loaded[i % 2], 16)

            @block.tensor
            def _(pe):
                for i, (r, n) in enumerate(ROW_TILES):
                    pe.wait_ge(loaded[i % 2], 16 * (i // 2 + 1))
                    for q in range(4):
                        if i >= 1:
                            pe.wait_ge(copied, 4 * (i - 1) + q + 1)
                        for k in range(4):
                            last = pe.transpose(ps[:, q, k * P:k * P + n],
                                                rows[0:n, i % 2, (4 * q + k) * P:(4 * q + k + 1) * P],
                                                g.ident[0:n, 0:n])
                        last.then_inc(turned, 1)

            @block.vector
            def _(dve):
                for i, (r, n) in enumerate(ROW_TILES):
                    for q in range(4):
                        dve.wait_ge(turned, 4 * i + q + 1)
                        dve.tensor_copy(g.xt[:, 4 * q:4 * q + 4, r:r + n],
                                        ps[:, q, :].rearrange("p (k t) -> p k t", k=4)[:, :, 0:n]).then_inc(copied, 1)


def stage_out_proj(nc, g):
    HC = TC // 2
    with ExitStack() as ctx:
        w_raw = ctx.enter_context(nc.sbuf_tensor("o_w", [P, 3, KT, P], F32))
        w_hi = ctx.enter_context(nc.sbuf_tensor("o_w_hi", [P, 3, KT, P], F32R))
        w_lo = ctx.enter_context(nc.sbuf_tensor("o_w_lo", [P, 3, KT, P], F32R))
        mix_raw = ctx.enter_context(nc.sbuf_tensor("o_mix", [P, 2, 2, TC], F32))
        sq = ctx.enter_context(nc.sbuf_tensor("o_sq", [P, 2, TC], F32))
        rstd = ctx.enter_context(nc.sbuf_tensor("o_rstd", [P, 3, TC], F32))
        gain = ctx.enter_context(nc.sbuf_tensor("o_gain", [P, KT], F32))
        ps = ctx.enter_context(nc.psum_tensor("o_ps", [P, 8, 512], F32))
        loaded = [new_sem(nc, g, f"o_w_in{i}") for i in range(3)]
        mix_in = [new_sem(nc, g, f"o_mix_in{i}") for i in range(2)]
        gain_in = new_sem(nc, g, "o_gain_in")
        mix_hi, mix_lo = new_sem(nc, g, "o_split_hi"), new_sem(nc, g, "o_split_lo")
        hi_done, lo_done = new_sem(nc, g, "o_hi_done"), new_sem(nc, g, "o_lo_done")
        summed = [new_sem(nc, g, f"o_summed{i}") for i in range(3)]
        added = [new_sem(nc, g, f"o_added{i}") for i in range(3)]
        squared = new_sem(nc, g, "o_squared")
        sum_step = new_sem(nc, g, "o_sum_step")
        ms_ready = new_sem(nc, g, "o_ms_ready")
        root_ready = new_sem(nc, g, "o_root_ready")
        rstd_ready = new_sem(nc, g, "o_rstd_ready")
        h_ready, h_hi, h_lo = (new_sem(nc, g, "o_" + n) for n in ("h_ready", "h_hi", "h_lo"))
        w_view = g.w_o.rearrange("(k p) n -> p k n", p=P)
        rounds = KT // 3
        assert KT == 3 * rounds + 1
        last_uses = [rounds + 1, rounds, rounds]
        with nc.Block() as block:
            @block.sync
            def _(sp):
                def load(s, col):
                    sp.dma_start(w_raw[:, s, :, :], w_view[:, :, bass.ds(col, P)]).then_inc(loaded[s], 16)
                for s in range(3):
                    load(s, s * P)
                with sp.Fori(0, rounds - 1) as i:
                    for s in range(3):
                        sp.wait_ge(summed[s], i + 1)
                        load(s, i * (3 * P) + (3 + s) * P)
                sp.wait_ge(summed[0], rounds)
                load(0, 3 * rounds * P)

            @block.gpsimd
            def _(pool):
                for q in range(8):
                    if q >= 2:
                        pool.wait_ge(mix_lo, q - 1)
                    pool.dma_start(mix_raw[:, q % 2], g.mix_t[q * 256:(q + 1) * 256].rearrange(
                        "(k p) t -> p k t", p=P)).then_inc(mix_in[q % 2], 16)
                with nc.allow_non_contiguous_dma(reason="one value to a partition"):
                    pool.dma_start(gain[:], g.g_ffn.rearrange("(k p) -> p k", p=P)).then_inc(gain_in, 16)

            @block.tensor
            def _(pe):
                def unit(i, s, first=False):
                    pe.wait_ge(lo_done, i * 3 + s + 1)
                    pe.wait_ge(added[s], i)
                    for k in range(KT):
                        if first and k % 2 == 0:
                            pe.wait_ge(mix_lo, k // 2 + 1)
                        last = three_products(pe, [ps[:, 2 * s + h, 0:HC] for h in range(2)],
                                              w_hi[:, s, k, :], w_lo[:, s, k, :],
                                              [g.hh[:, k, h * HC:(h + 1) * HC] for h in range(2)],
                                              [g.hl[:, k, h * HC:(h + 1) * HC] for h in range(2)],
                                              k == 0, k == KT - 1)
                    last.then_inc(summed[s], 1)
                for s in range(3):
                    unit(0, s, s == 0)
                with pe.Fori(1, rounds) as i:
                    for s in range(3):
                        unit(i, s)
                unit(rounds, 0)
                for s in range(3):
                    pe.wait_ge(added[s], last_uses[s])
                for k in range(KT):
                    pe.wait_ge(squared, k + 1)
                    for h in range(2):
                        last = pe.matmul(ps[:, h, 0:HC], g.ones[:], sq[:, k % 2, h * HC:(h + 1) * HC],
                                         start=(k == 0), stop=(k == KT - 1))
                    last.then_inc(sum_step, 1)

            @block.scalar
            def _(act):
                def high(i, u):
                    s = u % 3
                    act.wait_ge(loaded[s], i * 16 + (u // 3 + 1) * 16)
                    act.copy(w_hi[:, s, :, :], w_raw[:, s, :, :]).then_inc(hi_done, 1)
                high(0, 0)
                for q in range(8):
                    act.wait_ge(mix_in[q % 2], 16 * (q // 2 + 1))
                    act.copy(g.hh[:, 2 * q:2 * q + 2, :], mix_raw[:, q % 2]).then_inc(mix_hi, 1)
                high(0, 1)
                with act.Fori(0, rounds - 1) as i:
                    for s in range(3):
                        high(i, s + 2)
                for s in range(2, 4):
                    high(rounds - 1, s)
                for s in range(3):
                    act.wait_ge(added[s], last_uses[s])
                for k in range(KT):
                    if k >= 2:
                        act.wait_ge(sum_step, k - 1)
                    act.activation(sq[:, k % 2, :], g.xt[:, k, :], ACT.Square).then_inc(squared, 1)
                act.wait_ge(ms_ready, 2)
                act.activation(rstd[:, 1, :], rstd[:, 0, :], ACT.Sqrt).then_inc(root_ready, 1)
                for k in range(KT):
                    act.wait_ge(h_ready, k + 1)
                    act.copy(g.hh[:, k, :], sq[:, k % 2, :]).then_inc(h_hi, 1)

            @block.vector
            def _(dve):
                def low(i, u):
                    s = u % 3
                    dve.wait_ge(hi_done, i * 3 + u + 1)
                    dve.tensor_tensor(w_lo[:, s, :, :], w_raw[:, s, :, :], w_hi[:, s, :, :].bitcast(F32),
                                      ALU.subtract).then_inc(lo_done, 1)

                def add(i, s):
                    dve.wait_ge(summed[s], i + 1)
                    x = g.xt[:, bass.ds(i * 3 + s, 1), :].rearrange("p a (h t) -> p (a h) t", h=2)
                    dve.tensor_tensor(x, x, ps[:, 2 * s:2 * s + 2, 0:HC], ALU.add).then_inc(added[s], 1)
                low(0, 0)
                for q in range(8):
                    dve.wait_ge(mix_hi, q + 1)
                    dve.tensor_tensor(g.hl[:, 2 * q:2 * q + 2, :], mix_raw[:, q % 2],
                                      g.hh[:, 2 * q:2 * q + 2, :].bitcast(F32), ALU.subtract).then_inc(mix_lo, 1)
                low(0, 1)
                with dve.Fori(0, rounds - 1) as i:
                    for s in range(3):
                        low(i, s + 2)
                        add(i, s)
                for s in range(3):
                    if s < 2:
                        low(rounds - 1, s + 2)
                    add(rounds - 1, s)
                add(rounds, 0)
                dve.wait_ge(sum_step, KT)
                dve.tensor_scalar(rstd[:, 0, 0:HC], ps[:, 0, 0:HC], 1.0 / D, EPS, ALU.mult, ALU.add).then_inc(ms_ready, 1)
                dve.tensor_scalar(rstd[:, 0, HC:TC], ps[:, 1, 0:HC], 1.0 / D, EPS, ALU.mult, ALU.add).then_inc(ms_ready, 1)
                dve.wait_ge(root_ready, 1)
                dve.reciprocal(rstd[:, 2, :], rstd[:, 1, :]).then_inc(rstd_ready, 1)
                dve.wait_ge(rstd_ready, 1)
                dve.wait_ge(gain_in, 16)
                for k in range(KT + 1):
                    if k < KT:
                        if k >= 2:
                            dve.wait_ge(h_lo, k - 1)
                        dve.scalar_tensor_tensor(out=sq[:, k % 2, :], in0=g.xt[:, k, :], scalar=gain[:, k:k + 1],
                                                 in1=rstd[:, 2, :], op0=ALU.mult, op1=ALU.mult).then_inc(h_ready, 1)
                    if k >= 1:
                        dve.wait_ge(h_hi, k)
                        dve.tensor_tensor(g.hl[:, k - 1, :], sq[:, (k - 1) % 2, :], g.hh[:, k - 1, :].bitcast(F32),
                                          ALU.subtract).then_inc(h_lo, 1)


def stage_ffn(nc, g):
    HC = TC // 2
    HT = 4
    PARTS = D_FF // P // HT
    UN = 3 * HT
    SUMS = 16
    GR = 12
    assert PARTS * HT * P == D_FF and D == 2048
    with ExitStack() as ctx:
        w_raw = ctx.enter_context(nc.sbuf_tensor("f_w", [P, 3, 2048], F32))
        w_hi = ctx.enter_context(nc.sbuf_tensor("f_w_hi", [P, 3, 2048], F32R))
        w_lo = ctx.enter_context(nc.sbuf_tensor("f_w_lo", [P, 3, 2048], F32R))
        hid_hi = ctx.enter_context(nc.sbuf_tensor("f_hid_hi", [P, HT, TC], F32R))
        hid_lo = ctx.enter_context(nc.sbuf_tensor("f_hid_lo", [P, HT, TC], F32R))
        sg = ctx.enter_context(nc.sbuf_tensor("f_sg", [P, 2, 2, HC], F32))
        act_up = ctx.enter_context(nc.sbuf_tensor("f_act_up", [P, 2, HC], F32))
        ps = ctx.enter_context(nc.psum_tensor("f_ps", [P, 8, 512], F32))
        loaded = [new_sem(nc, g, f"f_w_in{i}") for i in range(3)]
        hi_done, lo_done, summed, freed = (new_sem(nc, g, "f_" + n) for n in ("hi_done", "lo_done", "summed", "freed"))
        silu_ready, hid_split, hid_ready = (new_sem(nc, g, "f_" + n) for n in ("silu_ready", "hid_split", "hid_ready"))
        gate_v = g.w_gate.rearrange("(k p) n -> p k n", p=P)
        up_v = g.w_up.rearrange("(k p) n -> p k n", p=P)
        down_v = g.w_down.rearrange("(k p) n -> p k n", p=P)

        def through(n):
            return n + 1 if n < 2 * HT else 2 * HT + 2 * (n - 2 * HT) + 2

        def both(t):
            return t.rearrange("p (h t) -> p h t", h=2)

        with nc.Block() as block:
            @block.sync
            def _(sp):
                def load(i, n):
                    i, n = (i, n) if n < UN else (i + 1, n - UN)
                    w = w_raw[:, n % 3, :]
                    if n < 2 * HT:
                        src = (gate_v, up_v)[n % 2][:, :, bass.ds(i * (HT * P) + (n // 2) * P, P)]
                        sp.dma_start(w.rearrange("p (k n) -> p k n", k=KT), src).then_inc(loaded[n % 3], 16)
                    else:
                        v = n - 2 * HT
                        src = down_v[:, bass.ds(i * HT, HT), v * 512:(v + 1) * 512]
                        sp.dma_start(w.rearrange("p (k n) -> p k n", k=HT), src).then_inc(loaded[n % 3], 16)

                def part(i, last):
                    for n in range(UN - 3 if last else UN):
                        sp.wait_ge(summed, i * SUMS + through(n))
                        load(i, n + 3)
                for n in range(3):
                    load(0, n)
                with sp.Fori(0, PARTS - 1) as i:
                    part(i, False)
                part(PARTS - 1, True)

            @block.tensor
            def _(pe):
                def bank(group, j):
                    return ps[:, 4 * (group % 2) + j, 0:HC]

                def halves(x, k):
                    return [x[:, k, h * HC:(h + 1) * HC] for h in range(2)]

                with pe.Fori(0, PARTS) as i:
                    for n in range(2 * HT):
                        j, m, s = n // 2, n % 2, n % 3
                        pe.wait_ge(lo_done, i * UN + n + 1)
                        if m == 0:
                            pe.wait_ge(freed, i * GR + j + 1)
                        for k in range(KT):
                            cols = slice(k * P, (k + 1) * P)
                            last = three_products(pe, [bank(j, 2 * m + h) for h in range(2)], w_hi[:, s, cols], w_lo[:, s, cols],
                                                  halves(g.hh, k), halves(g.hl, k), k == 0, k == KT - 1)
                        last.then_inc(summed, 1)
                    for v in range(HT):
                        s = (2 * HT + v) % 3
                        pe.wait_ge(lo_done, i * UN + 2 * HT + v + 1)
                        for pair in range(2):
                            group = HT + 2 * v + pair
                            pe.wait_ge(freed, i * GR + group + 1)
                            for ks in (range(HT - 1), range(HT - 1, HT)):
                                for m in range(2):
                                    for k in ks:
                                        if v + pair + m == 0:
                                            pe.wait_ge(hid_ready, i * HT + k + 1)
                                        c = k * 512 + (2 * pair + m) * P
                                        last = three_products(pe, [bank(group, 2 * m + h) for h in range(2)],
                                                              w_hi[:, s, c:c + P], w_lo[:, s, c:c + P],
                                                              halves(hid_hi, k), halves(hid_lo, k), k == 0, k == HT - 1)
                            last.then_inc(summed, 1)

            @block.scalar
            def _(act):
                def high(i, n):
                    s = n % 3
                    act.wait_ge(loaded[s], i * (16 * UN // 3) + (n // 3 + 1) * 16)
                    act.copy(w_hi[:, s, :], w_raw[:, s, :]).then_inc(hi_done, 1)

                def part(i, last):
                    for n in range(UN):
                        if not last or n + 2 < UN:
                            high(i, n + 2)
                        if n < 2 * HT and n % 2 == 0:
                            j = n // 2
                            act.wait_ge(summed, i * SUMS + n + 1)
                            act.activation(sg[:, j % 2], ps[:, 4 * (j % 2):4 * (j % 2) + 2, 0:HC],
                                           ACT.Silu).then_inc(silu_ready, 1)
                for n in range(2):
                    high(0, n)
                with act.Fori(0, PARTS - 1) as i:
                    part(i, False)
                part(PARTS - 1, True)

            @block.vector
            def _(dve):
                def low(i, n):
                    s = n % 3
                    dve.wait_ge(hi_done, i * UN + n + 1)
                    dve.tensor_tensor(w_lo[:, s, :], w_raw[:, s, :], w_hi[:, s, :].bitcast(F32),
                                      ALU.subtract).then_inc(lo_done, 1)

                def hidden(i, j):
                    dve.wait_ge(summed, i * SUMS + 2 * j + 2)
                    dve.wait_ge(silu_ready, i * HT + j + 1)
                    b = 4 * (j % 2) + 2
                    dve.tensor_tensor(act_up[:], sg[:, j % 2], ps[:, b:b + 2, 0:HC], ALU.mult).then_inc(freed, 1)
                    dve.wait_ge(freed, i * GR + j + 3)
                    dve.tensor_copy(both(hid_hi[:, j, :]), act_up[:]).then_inc(hid_split, 1)
                    dve.wait_ge(hid_split, i * HT + j + 1)
                    dve.tensor_tensor(both(hid_lo[:, j, :]), act_up[:], both(hid_hi[:, j, :]).bitcast(F32),
                                      ALU.subtract).then_inc(hid_ready, 1)
                    dve.wait_ge(hid_ready, i * HT + j + 1)

                def add(i, pair):
                    dve.wait_ge(summed, i * SUMS + 2 * HT + pair + 1)
                    b = 4 * (pair % 2)
                    x = g.xt[:, 2 * pair:2 * pair + 2, :].rearrange("p m (h t) -> p (m h) t", h=2)
                    dve.tensor_tensor(x, x, ps[:, b:b + 4, 0:HC], ALU.add).then_inc(freed, 1)

                def part(i, last):
                    for n in range(UN):
                        if not last or n + 2 < UN:
                            low(i, n + 2)
                        if n < 2 * HT:
                            if n % 2:
                                hidden(i, n // 2)
                        else:
                            for pair in range(2):
                                add(i, 2 * (n - 2 * HT) + pair)
                for h in range(2):
                    dve.memset(act_up[:, h, :], 0.0).then_inc(freed, 1)
                for n in range(2):
                    low(0, n)
                with dve.Fori(0, PARTS - 1) as i:
                    part(i, False)
                part(PARTS - 1, True)


def stage_final(nc, g):
    with ExitStack() as ctx:
        rows = ctx.enter_context(nc.sbuf_tensor("z_rows", [P, 2, D], F32))
        yrow = ctx.enter_context(nc.sbuf_tensor("z_yrow", [P, 2, D], F32))
        gain = ctx.enter_context(nc.sbuf_tensor("z_gain", [P, D], F32))
        junk = ctx.enter_context(nc.sbuf_tensor("z_junk", [P, D], F32))
        stat = ctx.enter_context(nc.sbuf_tensor("z_stat", [P, 5, 4], F32))
        ps = ctx.enter_context(nc.psum_tensor("z_ps", [P, 4, 512], F32))
        gain_in = new_sem(nc, g, "z_gain_in")
        turned = new_sem(nc, g, "z_turned")
        copied = new_sem(nc, g, "z_copied")
        squares = new_sem(nc, g, "z_squares")
        chain = new_sem(nc, g, "z_chain")
        ms_ready = new_sem(nc, g, "z_ms_ready")
        root_ready = new_sem(nc, g, "z_root_ready")
        y_ready = new_sem(nc, g, "z_y_ready")
        stored = [new_sem(nc, g, f"z_stored{i}") for i in range(2)]
        dsts = [g.y_prompt[r:r + n, :] for r, n in ROW_TILES[:4]] + [g.y_sample]
        with nc.Block() as block:
            @block.sync
            def _(sp):
                sp.dma_start(gain[:], g.g_final[None, :].to_broadcast([P, D])).then_inc(gain_in, 16)
                for i, (r, n) in enumerate(ROW_TILES):
                    sp.wait_ge(y_ready, i + 1)
                    sp.dma_start(dsts[i], yrow[0:n, i % 2, :]).then_inc(stored[i % 2], 16)
                sp.wait_ge(stored[0], 48)
                sp.wait_ge(stored[1], 32)

            @block.tensor
            def _(pe):
                for i, (r, n) in enumerate(ROW_TILES):
                    for q in range(4):
                        if i >= 1:
                            pe.wait_ge(copied, 4 * (i - 1) + q + 1)
                        for k in range(4):
                            last = pe.transpose(ps[0:n, q, k * P:(k + 1) * P], g.xt[:, 4 * q + k, r:r + n], g.ident[:])
                        last.then_inc(turned, 1)

            @block.scalar
            def _(act):
                for i, (r, n) in enumerate(ROW_TILES):
                    act.wait_ge(ms_ready, i + 1)
                    act.activation(stat[0:n, i, 2:3], stat[0:n, i, 1:2], ACT.Sqrt).then_inc(root_ready, 1)

            @block.vector
            def _(dve):
                c = 0
                for i, (r, n) in enumerate(ROW_TILES):
                    for q in range(4):
                        dve.wait_ge(turned, 4 * i + q + 1)
                        dve.tensor_copy(rows[0:n, i % 2, q * 512:(q + 1) * 512], ps[0:n, q, :]).then_inc(copied, 1)
                    dve.wait_ge(copied, 4 * i + 4)
                    x = rows[0:n, i % 2, :]
                    dve.tensor_tensor_reduce(out=junk[0:n, :], in0=x, in1=x, scale=1.0, scalar=0.0, op0=ALU.mult,
                                             op1=ALU.add, accum_out=stat[0:n, i, 0:1]).then_inc(chain, 1)
                    c += 1
                    dve.wait_ge(chain, c)
                    dve.tensor_scalar(stat[0:n, i, 1:2], stat[0:n, i, 0:1], 1.0 / D, EPS, ALU.mult, ALU.add).then_inc(ms_ready, 1)
                    dve.wait_ge(root_ready, i + 1)
                    dve.reciprocal(stat[0:n, i, 3:4], stat[0:n, i, 2:3]).then_inc(chain, 1)
                    c += 1
                    dve.wait_ge(chain, c)
                    if i == 0:
                        dve.wait_ge(gain_in, 16)
                    if i >= 2:
                        dve.wait_ge(stored[i % 2], 16 * (i // 2))
                    dve.scalar_tensor_tensor(out=yrow[0:n, i % 2, :], in0=x, scalar=stat[0:n, i, 3:4],
                                             in1=gain[0:n, :], op0=ALU.mult, op1=ALU.mult).then_inc(y_ready, 1)


def stage_constants(nc, g):
    made = new_sem(nc, g, "c_made")

    with nc.Block() as block:
        @block.gpsimd
        def _(pool):
            step = Chain(pool, made)

            def band(t, rows, cols, pattern, mult, base, op, fill=0.0):
                step(pool.affine_select(out=t, in_=t, compare_op=op, fill=fill, base=base, pattern=pattern,
                                        channel_multiplier=mult))

            step(pool.memset(g.ident[:], 0.0))
            band(g.ident[:], P, P, [[-1, P]], 1, 0, ALU.not_equal, 1.0)
            step(pool.memset(g.ones[:], 1.0))

            def blocks(t, rows, cols, w):
                step(pool.memset(t, 1.0))
                v = t.rearrange("p (n w) -> p n w", w=w)
                band(v, rows, cols, [[-w, cols // w], [0, w]], 1, 0, ALU.is_ge)
                band(v, rows, cols, [[w, cols // w], [0, w]], -1, w - 1, ALU.is_ge)

            blocks(g.blk64[:], P, P, 64)
            blocks(g.blk4[:], P, P, 4)
            step(pool.memset(g.mask_g[:], 1.0))
            for lo in (0, C):
                rows = g.mask_g[lo:lo + C, :]
                band(rows[:, 0:C], C, C, [[1, C]], -1, -1, ALU.is_ge)
                band(rows[:, C:P], C, C, [[1, C]], -1, 0, ALU.is_ge)
            blocks(g.up16[:], C, C, 16)
            band(g.up16[:], C, C, [[1, C]], -1, -1, ALU.is_ge)
            blocks(g.low16[:], C, C, 16)
            band(g.low16[:], C, C, [[-1, C]], 1, -1, ALU.is_ge)
            step(pool.memset(g.low32[:], 0.0))
            step(pool.memset(g.low64[:], 0.0))
            for j in range(2):
                t = g.low32[:, 32 * j:32 * j + 16]
                step(pool.memset(t, 1.0))
                band(t, C, 16, [[0, 16]], 1, -(32 * j + 16), ALU.is_ge)
                band(t, C, 16, [[0, 16]], -1, 32 * j + 31, ALU.is_ge)
            t = g.low64[:, 0:32]
            step(pool.memset(t, 1.0))
            band(t, C, 32, [[0, 32]], 1, -32, ALU.is_ge)


def constants(nc, g, ctx):
    def sb(name, rows, cols):
        return ctx.enter_context(nc.sbuf_tensor(name, [rows, cols], F32))
    g.ident, g.ones, g.blk64, g.blk4, g.mask_g = (sb(n, P, P) for n in ("ident", "ones", "blk64", "blk4", "mask_g"))
    g.up16, g.low16, g.low32, g.low64 = (sb(n, C, C) for n in ("up16", "low16", "low32", "low64"))


def rwkv(nc, g):
    with ExitStack() as ctx:
        def sb(name, shape):
            return ctx.enter_context(nc.sbuf_tensor(name, shape, F32))
        g.gate_t = sb("gate_t", [P, NPAIR, TC])
        g.bonus_t = sb("bonus_t", [P, NPAIR, TC])
        g.y_t = sb("y_t", [P, NPAIR, TC])
        g.chunk_decay = sb("chunk_decay", [P, NPAIR, SEQ // C])
        g.v_samp = sb("v_samp", [P, NPAIR, NB])
        stage_rwkv_prep(nc, g)
        stage_rwkv_chunks(nc, g)
        stage_rwkv_sample(nc, g)
        stage_rwkv_post(nc, g)


def nsa(nc, g):
    with ExitStack() as ctx:
        g.kc = ctx.enter_context(nc.sbuf_tensor("kc", [P, 2 * NB, 255], F32))
        g.vc = ctx.enter_context(nc.sbuf_tensor("vc", [P, NB, 512], F32))
        stage_compress(nc, g)
        stage_nsa_sample(nc, g)
    stage_nsa_prompt(nc, g)


def build(nc, g):
    g.sems, g.waited = [], nc.alloc_semaphore("waited")
    g.proj_t = nc.dram_tensor("proj_t", [KV0, TA], F32, kind="Internal").ap()
    g.kv_rows = nc.dram_tensor("kv_rows", [TC, 1536], F32, kind="Internal").ap()
    g.gates = nc.dram_tensor("gates", [TC, 48], F32, kind="Internal").ap()
    g.rk_chunks = nc.dram_tensor("rk_chunks", [SEQ // C, P, NPAIR, 5 * C], F32, kind="Internal").ap()
    g.samp_rows = nc.dram_tensor("samp_rows", [6 * NB, D_R], F32, kind="Internal").ap()
    g.kc_prompt = nc.dram_tensor("kc_prompt", [256, 31], F32, kind="Internal").ap()
    g.vc_prompt = nc.dram_tensor("vc_prompt", [31, 256], F32, kind="Internal").ap()
    g.mix_t = nc.dram_tensor("mix_t", [D, TC], F32, kind="Internal").ap()
    with ExitStack() as ctx:
        constants(nc, g, ctx)
        stage_constants(nc, g)
        with ExitStack() as c2:
            g.xh = c2.enter_context(nc.sbuf_tensor("xh", [P, KT, TA], F32R))
            g.xl = c2.enter_context(nc.sbuf_tensor("xl", [P, KT, TA], F32R))
            stage_norm(nc, g)
            stage_in_proj(nc, g)
        rwkv(nc, g)
        retire_sems(nc, g)
        nsa(nc, g)
        retire_sems(nc, g)
        with ExitStack() as c2:
            g.xt = c2.enter_context(nc.sbuf_tensor("xt", [P, KT, TC], F32))
            stage_turn_x(nc, g)
            with ExitStack() as c3:
                g.hh = c3.enter_context(nc.sbuf_tensor("hh", [P, KT, TC], F32R))
                g.hl = c3.enter_context(nc.sbuf_tensor("hl", [P, KT, TC], F32R))
                stage_out_proj(nc, g)
                stage_ffn(nc, g)
            stage_final(nc, g)


def views(ins, outs):
    i = ins
    g = Arrays()
    g.x_prompt = i["x_prompt"][0]
    g.x_sample = i["x_sample"][:, 0, :]
    g.shift = i["state_shift"][0]
    g.g_mix = i["g_mix"][0]
    g.w_in = i["w_in"][0]
    g.mu = i["mu"][0]
    g.w0 = i["w0"][0]
    g.w2 = i["w2"][0]
    g.a0 = i["a0"][0]
    g.a2 = i["a2"][0]
    g.g2 = i["g2"][0]
    g.k_k = i["k_k"][0]
    g.k_a = i["k_a"][0]
    g.r_k = i["r_k"][0]
    g.lnx_w = i["lnx_w"][0]
    g.lnx_b = i["lnx_b"][0]
    g.state_wkv = i["state_wkv"][0]
    g.phi_pe = i["phi_pe"][0]
    g.phi_w1 = i["phi_w1"][0]
    g.phi_w2 = i["phi_w2"][0]
    g.page_table = i["page_table"]
    g.cache_cmp = i["cache_cmp_kv"][0].rearrange("n r k h d -> n r (k h d)")
    g.cache_slc = i["cache_slc_kv"][0].rearrange("n r k h d -> n r (k h d)")
    g.cache_win = i["cache_win_kv"][0].rearrange("b r k h d -> b r (k h d)")
    g.new_cmp_prompt = outs[2][0, 0].rearrange("r k h d -> r (k h d)")
    g.new_slc_prompt = outs[3][0, 0].rearrange("r k h d -> r (k h d)")
    g.new_win_prompt = outs[4][0, 0].rearrange("r k h d -> r (k h d)")
    g.new_cmp_sample = outs[7][0, :, 0].rearrange("b k h d -> b (k h d)")
    g.new_slc_sample = outs[8][0, :, 0].rearrange("b k h d -> b (k h d)")
    g.new_win_sample = outs[9][0].rearrange("b r k h d -> b r (k h d)")
    g.new_wkv_prompt = outs[5][0, 0]
    g.new_wkv_sample = outs[10][0]
    g.w_o = i["w_o"][0]
    g.g_ffn = i["g_ffn"][0]
    g.w_gate = i["w_gate"][0]
    g.w_up = i["w_up"][0]
    g.w_down = i["w_down"][0]
    g.g_final = i["g_final"]
    g.y_prompt = outs[0][0]
    g.y_sample = outs[1][:, 0, :]
    g.new_shift_prompt = outs[6][0]
    g.new_shift_sample = outs[11][0]
    g.ins = ins
    g.outs = outs
    return g


_OUTS = [(1, 512, 2048), (8, 1, 2048), (1, 1, 512, 2, 4, 64), (1, 1, 512, 2, 4, 64), (1, 1, 512, 2, 4, 64),
         (1, 1, 16, 64, 64), (1, 1, 2048), (1, 8, 1, 2, 4, 64), (1, 8, 1, 2, 4, 64), (1, 8, 512, 2, 4, 64),
         (1, 8, 16, 64, 64), (1, 8, 2048)]


def kernel(**inputs):
    import numpy as _np
    import concourse.bacc as _bacc
    from concourse import mybir as _mybir
    from concourse.bass_utils import run_bass_kernel_spmd as _run

    nc = _bacc.Bacc("TRN2", target_bir_lowering=False, num_devices=1)
    arrays, ins = {}, {}
    for name, a in inputs.items():
        a = _np.ascontiguousarray(a)
        arrays[f"in_{name}"] = a
        ins[name] = nc.dram_tensor(f"in_{name}", a.shape, _mybir.dt.from_np(a.dtype), kind="ExternalInput").ap()
    outs = [nc.dram_tensor(f"out_{n}", shape, F32, kind="ExternalOutput").ap() for n, shape in enumerate(_OUTS)]
    build(nc, views(ins, outs))
    r = _run(nc, [arrays], core_ids=[0])
    return tuple(r.results[0][f"out_{n}"] for n in range(len(_OUTS)))
```
